# Optimizing a Trainium2 kernel written in Bass

```python
import math
import jax, jax.numpy as jnp
from jax import lax
import numpy as np

D_MODEL = 1024
BATCH = 1
SEQ = 2048
DEPTH = 1

CHUNK = 64
Q_BLOCK = 128
NORM_EPS = 1e-6

DA_HEADS = 8
DA_HEAD_DIM = 64
DA_V_DIM = 2 * DA_HEAD_DIM
ROPE_THETA = 500000.0
ROPE_DIM = DA_HEAD_DIM // 4
QK_WIDTH = DA_HEADS * 2 * DA_HEAD_DIM
V_WIDTH = DA_HEADS * DA_V_DIM

POOL_WINDOWS = (2, 4, 8, 16)
POOL_GROUPS = len(POOL_WINDOWS)
POOL_GROUP_DIM = 128
POOL_WIDTH = POOL_GROUPS * POOL_GROUP_DIM

N_BRANCHES = 2
IN_WIDTH = 2 * QK_WIDTH + V_WIDTH + POOL_WIDTH + N_BRANCHES * D_MODEL

N_EXPERTS = 32
TOP_K = 4
D_FF = D_MODEL
SWIGLU_LIMIT = 7.0
SWIGLU_ALPHA = 1.702

N_MOD = 6

kernel_name = "hybrid_diffattn_pool_moe_block"

def rms_norm(x, g):
    xf = x.astype(jnp.float32)
    y = xf * lax.rsqrt(jnp.mean(xf * xf, axis=-1, keepdims=True) + NORM_EPS)
    return (y * g.astype(jnp.float32)).astype(x.dtype)

def rope_tables(positions, dtype):
    inv_freq = ROPE_THETA ** (-jnp.arange(0, ROPE_DIM, 2, dtype=jnp.float32) / ROPE_DIM)
    ang = positions.astype(jnp.float32)[..., None] * inv_freq
    return jnp.cos(ang)[:, :, None, :].astype(dtype), jnp.sin(ang)[:, :, None, :].astype(dtype)

def apply_partial_rope(t, cos, sin):
    rot, rest = t[..., :ROPE_DIM], t[..., ROPE_DIM:]
    r1, r2 = rot[..., :ROPE_DIM // 2], rot[..., ROPE_DIM // 2:]
    rot = jnp.concatenate([r1 * cos - r2 * sin, r2 * cos + r1 * sin], axis=-1)
    return jnp.concatenate([rot, rest], axis=-1)

def diff_attention(q, k, v, lam, g_sub, lambda_init):
    B, S = q.shape[0], q.shape[1]
    nb = S // Q_BLOCK
    scale = DA_HEAD_DIM ** -0.5
    qb = q.reshape(B, nb, Q_BLOCK, 2 * DA_HEADS, DA_HEAD_DIM).transpose(1, 0, 3, 2, 4)
    kt = k.transpose(0, 2, 1, 3)
    vt = v.transpose(0, 2, 1, 3)
    key_chunk = jnp.arange(S) // CHUNK

    def block(args):
        q_blk, i = args
        s = jnp.einsum('bnqd,bnkd->bnqk', q_blk, kt).astype(jnp.float32) * scale
        q_chunk = (i * Q_BLOCK + jnp.arange(Q_BLOCK)) // CHUNK
        mask = key_chunk[None, :] <= q_chunk[:, None]
        s = jnp.where(mask, s, -jnp.inf)
        p = jax.nn.softmax(s, axis=-1).reshape(B, DA_HEADS, 2, Q_BLOCK, S)
        a = p[:, :, 0] - lam * p[:, :, 1]
        return jnp.einsum('bhqk,bhkd->bhqd', a.astype(vt.dtype), vt)

    o = lax.map(block, (qb, jnp.arange(nb)))
    o = o.transpose(1, 0, 3, 2, 4).reshape(B, S, DA_HEADS, DA_V_DIM)
    o = rms_norm(o, g_sub) * (1.0 - lambda_init)
    return o.reshape(B, S, V_WIDTH)

def multiscale_pool(p, w_group, pool_scale):
    B, S, _ = p.shape
    pf = p.astype(jnp.float32).reshape(B, S, POOL_GROUPS, POOL_GROUP_DIM)
    cs = jnp.concatenate([jnp.zeros((B, 1, POOL_GROUPS, POOL_GROUP_DIM), jnp.float32),
                          jnp.cumsum(pf, axis=1)], axis=1)
    t = jnp.arange(S)
    outs = []
    for g, w in enumerate(POOL_WINDOWS):
        start = jnp.maximum(t + 1 - w, 0)
        cnt = (t + 1 - start).astype(jnp.float32)
        mean = (cs[:, 1:, g] - cs[:, start, g]) / cnt[None, :, None]
        outs.append(mean - pf[:, :, g])
    mixed = jnp.stack(outs, axis=2).astype(p.dtype)
    y = jnp.einsum('bsgc,gcd->bsgd', mixed, w_group)
    return y.reshape(B, S, POOL_WIDTH) * pool_scale

def routed_experts(h, w_router, b_router, w_gate_up, b_gate_up, w_down, b_down):
    B, S, D = h.shape
    xt = h.reshape(-1, D)
    T = xt.shape[0]
    logits = (xt @ w_router).astype(jnp.float32) + b_router.astype(jnp.float32)
    top_v, top_i = lax.top_k(logits, TOP_K)
    probs = jax.nn.softmax(top_v, axis=-1)
    eid = top_i.reshape(-1)
    tok = jnp.repeat(jnp.arange(T), TOP_K)
    order = jnp.argsort(eid)
    eid_s, tok_s = eid[order], tok[order]
    w_s = probs.reshape(-1)[order]
    group_sizes = jnp.bincount(eid, length=N_EXPERTS).astype(jnp.int32)
    xs = xt[tok_s]
    gu = lax.ragged_dot(xs, w_gate_up, group_sizes) + b_gate_up[eid_s]
    gate, up = gu[:, :D_FF], gu[:, D_FF:]
    gate = jnp.minimum(gate, SWIGLU_LIMIT)
    up = jnp.clip(up, -SWIGLU_LIMIT, SWIGLU_LIMIT)
    act = (up + 1.0) * (gate * jax.nn.sigmoid(SWIGLU_ALPHA * gate))
    y = lax.ragged_dot(act, w_down, group_sizes) + b_down[eid_s]
    out = jnp.zeros((T, D), y.dtype).at[tok_s].add(y * w_s[:, None].astype(y.dtype))
    return out.reshape(B, S, D).astype(h.dtype)

def setup_inputs(seed: int = 0) -> dict:
    key = jax.random.key(seed)
    ks = jax.random.split(key, 32)
    f32 = jnp.float32
    nrm = lambda k, shape, s: jax.random.normal(k, shape, f32) * s
    gain = lambda k, shape: 1.0 + 0.05 * jax.random.normal(k, shape, f32)
    L = DEPTH
    offsets = jax.random.randint(ks[2], (BATCH, 1), 0, 64) * CHUNK
    positions = (offsets + jnp.arange(SEQ)[None, :]).astype(jnp.int32)
    return {
        "x": nrm(ks[0], (BATCH, SEQ, D_MODEL), 1.0),
        "c": nrm(ks[1], (BATCH, D_MODEL), 1.0),
        "positions": positions,
        "w_mod": nrm(ks[3], (L, D_MODEL, N_MOD * D_MODEL), D_MODEL ** -0.5),
        "b_mod": nrm(ks[4], (L, N_MOD * D_MODEL), 0.02),
        "g_pre_mix": gain(ks[5], (L, D_MODEL)),
        "w_in": nrm(ks[6], (L, D_MODEL, IN_WIDTH), D_MODEL ** -0.5),
        "lambda_q1": nrm(ks[7], (L, DA_HEAD_DIM), 0.1),
        "lambda_k1": nrm(ks[8], (L, DA_HEAD_DIM), 0.1),
        "lambda_q2": nrm(ks[9], (L, DA_HEAD_DIM), 0.1),
        "lambda_k2": nrm(ks[10], (L, DA_HEAD_DIM), 0.1),
        "g_sub": gain(ks[11], (L, DA_V_DIM)),
        "w_pool_group": nrm(ks[12], (L, POOL_GROUPS, POOL_GROUP_DIM, POOL_GROUP_DIM), POOL_GROUP_DIM ** -0.5),
        "pool_scale": gain(ks[13], (L, POOL_WIDTH)),
        "w_att_branch": nrm(ks[14], (L, V_WIDTH, D_MODEL), V_WIDTH ** -0.5),
        "w_pool_branch": nrm(ks[15], (L, POOL_WIDTH, D_MODEL), POOL_WIDTH ** -0.5),
        "w_out": nrm(ks[16], (L, D_MODEL, D_MODEL), D_MODEL ** -0.5),
        "g_post_mix": gain(ks[17], (L, D_MODEL)),
        "g_pre_ffn": gain(ks[18], (L, D_MODEL)),
        "w_router": nrm(ks[19], (L, D_MODEL, N_EXPERTS), D_MODEL ** -0.5),
        "b_router": nrm(ks[20], (L, N_EXPERTS), 0.01),
        "w_gate_up": nrm(ks[21], (L, N_EXPERTS, D_MODEL, 2 * D_FF), D_MODEL ** -0.5),
        "b_gate_up": nrm(ks[22], (L, N_EXPERTS, 2 * D_FF), 0.01),
        "w_down": nrm(ks[23], (L, N_EXPERTS, D_FF, D_MODEL), D_FF ** -0.5),
        "b_down": nrm(ks[24], (L, N_EXPERTS, D_MODEL), 0.01),
        "g_post_ffn": gain(ks[25], (L, D_MODEL)),
    }

def reference(x, c, positions, w_mod, b_mod, g_pre_mix, w_in, lambda_q1, lambda_k1,
              lambda_q2, lambda_k2, g_sub, w_pool_group, pool_scale, w_att_branch,
              w_pool_branch, w_out, g_post_mix, g_pre_ffn, w_router, b_router,
              w_gate_up, b_gate_up, w_down, b_down, g_post_ffn):
    B, S, D = x.shape
    cos, sin = rope_tables(positions, x.dtype)
    c_act = jax.nn.silu(c)
    splits = np.cumsum([QK_WIDTH, QK_WIDTH, V_WIDTH, POOL_WIDTH, D_MODEL]).tolist()
    for l in range(DEPTH):
        lambda_init = 0.8 - 0.6 * math.exp(-0.3 * l)
        mod = (c_act @ w_mod[l] + b_mod[l])[:, None, :]
        shift_m, scale_m, gate_m, shift_f, scale_f, gate_f = jnp.split(mod, N_MOD, axis=-1)

        u = rms_norm(x, g_pre_mix[l]) * (1.0 + scale_m) + shift_m
        z = u @ w_in[l]
        q, k, v, p, ga, gp = jnp.split(z, splits, axis=-1)
        q = apply_partial_rope(q.reshape(B, S, 2 * DA_HEADS, DA_HEAD_DIM), cos, sin)
        k = apply_partial_rope(k.reshape(B, S, 2 * DA_HEADS, DA_HEAD_DIM), cos, sin)
        v = v.reshape(B, S, DA_HEADS, DA_V_DIM)
        lam = (jnp.exp(jnp.sum(lambda_q1[l].astype(jnp.float32) * lambda_k1[l].astype(jnp.float32)))
               - jnp.exp(jnp.sum(lambda_q2[l].astype(jnp.float32) * lambda_k2[l].astype(jnp.float32)))
               + lambda_init)
        y_att = diff_attention(q, k, v, lam, g_sub[l], lambda_init) @ w_att_branch[l]
        y_pool = multiscale_pool(p, w_pool_group[l], pool_scale[l]) @ w_pool_branch[l]
        merged = jax.nn.sigmoid(ga) * y_att + jax.nn.sigmoid(gp) * y_pool
        mix_out = merged @ w_out[l]
        x = x + gate_m * rms_norm(mix_out, g_post_mix[l])

        u = rms_norm(x, g_pre_ffn[l]) * (1.0 + scale_f) + shift_f
        f = routed_experts(u, w_router[l], b_router[l], w_gate_up[l], b_gate_up[l],
                           w_down[l], b_down[l])
        x = x + gate_f * rms_norm(f, g_post_ffn[l])
    return x


_drawn_inputs = setup_inputs


def setup_inputs(seed=0):
    import zlib

    import numpy as np

    out = dict(_drawn_inputs(seed))
    spreads = {}
    factors = {'lambda_k1': 2.781, 'lambda_q2': 4.964, 'lambda_k2': 8.0, 'b_gate_up': 8.0, 'b_down': 8.0}
    for name, (base, spread) in spreads.items():
        noise = np.random.default_rng([zlib.crc32(name.encode()), seed]).standard_normal(out[name].shape)
        drawn = base * np.exp(spread * noise) if base else spread * noise
        out[name] = __import__('jax').numpy.asarray(drawn.astype(out[name].dtype))
    for name, factor in factors.items():
        out[name] = (out[name] * factor).astype(out[name].dtype)
    return out
```

```python
import math
from contextlib import ExitStack

import concourse.bass as bass
from concourse import mybir
import numpy as np

F32 = mybir.dt.float32
F32R = mybir.dt.float32r
BF16 = mybir.dt.bfloat16
I32 = mybir.dt.int32
U32 = mybir.dt.uint32
ALU = mybir.AluOpType
ACT = mybir.ActivationFunctionType
AX = mybir.AxisListType.X
ds = bass.ds

P = 128
D = 1024
KD = D // P
T = 2048
NT = T // P
BANK = 512
EPS = 1e-6
HEADS = 8
HD = 64
CHUNK = 64
ROPE = HD // 4
HALF = ROPE // 2
THETA = 500000.0
QKW = HEADS * 2 * HD
VW = HEADS * 2 * HD
PG = 4
WINDOWS = (2, 4, 8, 16)
IN_W = 2 * QKW + VW + PG * P + 2 * D
NB_IN = IN_W // BANK
E = 32
TOPK = 4
FF = D
LIMIT = 7.0
ALPHA = 1.702
LAMBDA_INIT = 0.8 - 0.6 * math.exp(-0.3 * 0)
SLOT = 512
JT = SLOT // P
SLOTS = T * TOPK // SLOT + E - 1
MAXB = T // SLOT
NEG = -1e30


class Shared:
    pass


class Inputs:

    def __init__(self, by_name):
        self.x = by_name["x"]
        self.c = by_name["c"]
        self.positions = by_name["positions"]
        self.w_mod = by_name["w_mod"]
        self.b_mod = by_name["b_mod"]
        self.g_pre_mix = by_name["g_pre_mix"]
        self.w_in = by_name["w_in"]
        self.lambda_q1 = by_name["lambda_q1"]
        self.lambda_k1 = by_name["lambda_k1"]
        self.lambda_q2 = by_name["lambda_q2"]
        self.lambda_k2 = by_name["lambda_k2"]
        self.g_sub = by_name["g_sub"]
        self.w_pool_group = by_name["w_pool_group"]
        self.pool_scale = by_name["pool_scale"]
        self.w_att_branch = by_name["w_att_branch"]
        self.w_pool_branch = by_name["w_pool_branch"]
        self.w_out = by_name["w_out"]
        self.g_post_mix = by_name["g_post_mix"]
        self.g_pre_ffn = by_name["g_pre_ffn"]
        self.w_router = by_name["w_router"]
        self.b_router = by_name["b_router"]
        self.w_gate_up = by_name["w_gate_up"]
        self.b_gate_up = by_name["b_gate_up"]
        self.w_down = by_name["w_down"]
        self.b_down = by_name["b_down"]
        self.g_post_ffn = by_name["g_post_ffn"]


class Link:

    def __init__(self, eng, sem, base=0):
        self.eng, self.sem, self.n, self.base = eng, sem, 0, base

    def __call__(self, ins):
        ins.then_inc(self.sem, 1)
        self.n += 1
        self.eng.wait_ge(self.sem, self.base + self.n)


def allocators(nc, ctx):
    def sb(name, shape, dt=F32):
        return ctx.enter_context(nc.sbuf_tensor(name, shape, dt))

    def ps(name, shape, dt=F32):
        return ctx.enter_context(nc.psum_tensor(name, shape, dt))

    sems = []

    def sem(name):
        sems.append(nc.alloc_semaphore(name))
        return sems[-1]

    def clear():
        if sems:
            nc.clear_and_free_semaphores(sems)
            nc.all_engine_barrier()

    ctx.callback(clear)
    return sb, ps, sem


R_BMOD, R_GPRE, R_GPOST, R_GFPRE, R_GFPOST, R_GSUB, R_PSC, R_C = 0, 48, 56, 64, 72, 80, 81, 85


def modulate(nc, a, g):
    with ExitStack() as ctx:
        sb, ps, sem = allocators(nc, ctx)
        RING = 3
        NCH = 6 * D // BANK
        wm = sb("wm", [P, RING, KD, BANK])
        vrow = sb("vrow", [P, P])
        bcol = sb("bcol", [P, BANK])
        brow = sb("brow", [P, 4, P])
        lamv = sb("lamv", [1, 4, HD])
        lprod = sb("lprod", [1, 2, HD])
        lsum = sb("lsum", [1, 4])
        ones1 = sb("ones1", [1, P])
        csil = sb("csil", [P, KD])
        mod = sb("mod", [P, 6 * KD])
        outgain = sb("outgain", [P, 4, D])
        gcol = sb("gcol", [P, 4, KD])
        wide = sb("wide", [P, 2, KD, P])
        posi = sb("posi", [P, NT], I32)
        rot = sb("rot", [P, NT, 2, P])
        sinv = sb("sinv", [P, NT, HALF])
        cosv = sb("cosv", [P, NT, HALF])
        posf = sb("posf", [P, NT])
        ang = sb("ang", [P, NT, HALF])
        kk = sb("kk", [P, 2, NT, HALF])
        tmp = sb("tmp", [P, NT, HALF])
        rsin = sb("rsin", [P, NT, HALF])
        rcos = sb("rcos", [P, NT, HALF])
        psv = ps("psv", [P, BANK])
        psm = ps("psm", [P, BANK])
        psb = ps("psb", [P, BANK])
        psl = ps("psl", [P, BANK])
        psr = ps("psr", [P, 2, BANK])
        psw = ps("psw", [P, 2, BANK])
        zeroed, loaded, wloaded = sem("m_zeroed"), sem("m_loaded"), [sem(f"m_w{i}") for i in range(RING)]
        wused, consts, vcols, vready = sem("m_wused"), sem("m_consts"), sem("m_vcols"), sem("m_vready")
        sig, csil_ready, mod_ready = sem("m_sig"), sem("m_csil"), sem("m_mod")
        dlink, plink = sem("m_dlink"), sem("m_plink")
        lam_sum, lam_exp, lam_one, lam_ps = sem("m_ls"), sem("m_le"), sem("m_lone"), sem("m_lps")
        bps, wide_ready, wide_ps, trig, sines = sem("m_bps"), sem("m_wr"), sem("m_wps"), sem("m_trig"), sem("m_sines")
        bias_done = sem('m_bd')
        wide_copied, kept = sem('m_wc'), sem('m_kept')
        rot_set, rot_ready, rot_ps, rot_copied = sem("m_rset"), sem("m_rr"), sem("m_rps"), sem("m_rc")
        block = ctx.enter_context(nc.Block())
        w_mod = a.w_mod[0].rearrange("(k p) n -> p k n", p=P)

        @block.sync
        def _(sp):
            sp.wait_ge(zeroed, 1)
            for row, src in ((R_BMOD, a.b_mod.rearrange("a (r c) -> (a r) c", c=P)),
                             (R_GPRE, a.g_pre_mix.rearrange("a (r c) -> (a r) c", c=P)),
                             (R_GPOST, a.g_post_mix.rearrange("a (r c) -> (a r) c", c=P)),
                             (R_GFPRE, a.g_pre_ffn.rearrange("a (r c) -> (a r) c", c=P)),
                             (R_GFPOST, a.g_post_ffn.rearrange("a (r c) -> (a r) c", c=P)),
                             (R_GSUB, a.g_sub),
                             (R_PSC, a.pool_scale.rearrange("a (r c) -> (a r) c", c=P)),
                             (R_C, a.c.rearrange("a (r c) -> (a r) c", c=P))):
                sp.dma_start(vrow[row:row + src.shape[0], :], src).then_inc(loaded, 16)
            for i, v in enumerate((a.lambda_q1, a.lambda_q2, a.lambda_k1, a.lambda_k2)):
                sp.dma_start(lamv[0:1, i, :], v).then_inc(loaded, 16)
            with nc.allow_non_contiguous_dma(reason="positions to columns"):
                sp.dma_start(posi[:, :], a.positions.rearrange("a (t p) -> p (a t)", p=P)).then_inc(loaded, 16)
            sp.dma_start(brow[:, :, :], a.b_gate_up[0].rearrange("e (f c) -> (e f) c", c=P)
                         .rearrange("(g r) c -> r g c", r=P)).then_inc(loaded, 16)
            for j in range(NCH):
                if j >= RING:
                    sp.wait_ge(wused, j - RING + 1)
                sp.dma_start(wm[:, j % RING], w_mod[:, :, j * BANK:(j + 1) * BANK]).then_inc(wloaded[j % RING], 16)
            sp.wait_ge(wide_copied, 4)
            sp.dma_start(g.outgain_d, outgain[:, :, :].rearrange("p n d -> p (n d)")).then_inc(kept, 16)
            sp.wait_ge(bias_done, 1)
            sp.dma_start(g.bcol_d, bcol[:, :]).then_inc(kept, 16)
            sp.wait_ge(kept, 32)

        @block.gpsimd
        def _(pool):
            link = Link(pool, plink)
            nc.gpsimd.memset(vrow[:, :], 0.0).then_inc(zeroed, 1)
            link(nc.gpsimd.memset(g.ident[:, :], 0.0))
            link(nc.gpsimd.affine_select(out=g.ident[:, :], in_=g.ident[:, :], compare_op=ALU.not_equal, fill=1.0,
                                         base=0, pattern=[[-1, P]], channel_multiplier=1))
            nc.gpsimd.memset(ones1[:, :], 1.0).then_inc(consts, 1)
            nc.gpsimd.memset(rot[:, :, 0, :], 1.0)
            nc.gpsimd.memset(rot[:, :, 1, :], 0.0).then_inc(rot_set, 1)

        @block.tensor
        def _(pe):
            pe.wait_ge(consts, 1)
            pe.wait_ge(loaded, 16 * 14)
            nc.tensor.transpose(psv[:, 0:P], vrow[:, :], g.ident[:, :]).then_inc(vcols, 1)
            for q in range(4):
                last = nc.tensor.transpose(psb[:, q * P:(q + 1) * P], brow[:, q, :], g.ident[:, :])
            last.then_inc(bps, 1)
            pe.wait_ge(csil_ready, 1)
            for j in range(NCH):
                pe.wait_ge(wloaded[j % RING], 16 * (j // RING + 1))
                for m in range(4):
                    col = j * 4 + m
                    for k in range(KD):
                        last = nc.tensor.matmul(psm[:, col:col + 1], wm[:, j % RING, k, m * P:(m + 1) * P],
                                                csil[:, k:k + 1], start=(k == 0), stop=(k == KD - 1))
                last.then_inc(wused, 1)
            pe.wait_ge(lam_one, 1)
            nc.tensor.matmul(psl[:, 0:1], ones1[0:1, :], lsum[0:1, 3:4], start=True, stop=True).then_inc(lam_ps, 1)
            for v in range(4):
                pe.wait_ge(wide_ready, v + 1)
                if v:
                    pe.wait_ge(wide_copied, v)
                for k in range(KD):
                    last = nc.tensor.transpose(psw[:, k // 4, (k % 4) * P:(k % 4 + 1) * P],
                                               wide[:, v % 2, k, :], g.ident[:, :])
                last.then_inc(wide_ps, 1)
            pe.wait_ge(rot_ready, 1)
            for t in range(NT):
                if t >= 2:
                    pe.wait_ge(rot_copied, t - 1)
                for v in range(2):
                    last = nc.tensor.transpose(psr[:, t % 2, v * P:(v + 1) * P], rot[:, t, v, :], g.ident[:, :])
                last.then_inc(rot_ps, 1)

        @block.scalar
        def _(act):
            act.wait_ge(vready, 1)
            nc.scalar.activation(csil[:, :], g.vcol[:, R_C:R_C + KD], ACT.Sigmoid).then_inc(sig, 1)
            act.wait_ge(lam_sum, 1)
            nc.scalar.activation(lsum[0:1, 0:2], lsum[0:1, 0:2], ACT.Exp).then_inc(lam_exp, 1)
            act.wait_ge(trig, 1)
            nc.scalar.activation(sinv[:, :, :], rsin[:, :, :], ACT.Sin).then_inc(sines, 1)
            nc.scalar.activation(cosv[:, :, :], rcos[:, :, :], ACT.Sin).then_inc(sines, 1)

        @block.vector
        def _(dve):
            link = Link(dve, dlink)
            dve.wait_ge(vcols, 1)
            nc.vector.tensor_copy(g.vcol[:, :], psv[:, 0:P]).then_inc(vready, 1)
            dve.wait_ge(vready, 1)
            dve.wait_ge(sig, 1)
            nc.vector.tensor_tensor(csil[:, :], csil[:, :], g.vcol[:, R_C:R_C + KD], ALU.mult).then_inc(csil_ready, 1)
            dve.wait_ge(bps, 1)
            link(nc.vector.tensor_copy(bcol[:, :], psb[:, :]))
            ups = bcol[:, :].rearrange("p (e h f) -> p e h f", h=2, f=KD)[:, :, 1, :]
            nc.vector.tensor_scalar(ups, ups, 1.0, None, ALU.add).then_inc(bias_done, 1)
            dve.wait_ge(loaded, 16 * 14)
            link(nc.vector.tensor_tensor(lprod[:, :, :], lamv[:, 0:2, :], lamv[:, 2:4, :], ALU.mult))
            nc.vector.tensor_reduce(lsum[0:1, 0:2], lprod[:, :, :], AX, ALU.add).then_inc(lam_sum, 1)
            dve.wait_ge(lam_exp, 1)
            link(nc.vector.tensor_tensor(lsum[0:1, 2:3], lsum[0:1, 1:2], lsum[0:1, 0:1], ALU.subtract))
            nc.vector.tensor_scalar(lsum[0:1, 3:4], lsum[0:1, 2:3], -LAMBDA_INIT, None, ALU.add).then_inc(lam_one, 1)
            link(nc.vector.tensor_copy(posf[:, :], posi[:, :]))
            inv = np.float32(THETA) ** (-np.arange(0, ROPE, 2, dtype=np.float32) / np.float32(ROPE))
            for i in range(HALF):
                link(nc.vector.tensor_scalar(ang[:, :, i], posf[:, :], float(inv[i]), None, ALU.mult))
            near, far = 1.5 * 2.0 ** 23, 1.5 * 2.0 ** 35
            link(nc.vector.tensor_scalar(tmp[:, :, :], ang[:, :, :], 1.0 / (2 * math.pi), None, ALU.mult))
            link(nc.vector.tensor_scalar(kk[:, 0], tmp[:, :, :], near, None, ALU.add))
            link(nc.vector.tensor_scalar(kk[:, 0], kk[:, 0], near, None, ALU.subtract))
            link(nc.vector.tensor_scalar(kk[:, 1], kk[:, 0], far, None, ALU.add))
            link(nc.vector.tensor_scalar(kk[:, 1], kk[:, 1], far, None, ALU.subtract))
            link(nc.vector.tensor_tensor(kk[:, 0], kk[:, 0], kk[:, 1], ALU.subtract))
            c1 = math.floor(2 * math.pi * 2 ** 8) / 2 ** 8
            c2 = math.floor((2 * math.pi - c1) * 2 ** 19) / 2 ** 19
            for part in (c1, c2, 2 * math.pi - c1 - c2):
                for q in (1, 0):
                    link(nc.vector.scalar_tensor_tensor(out=ang[:, :, :], in0=kk[:, q], scalar=-part, in1=ang[:, :, :],
                                                        op0=ALU.mult, op1=ALU.add))
            lim = 3.1415925
            link(nc.vector.tensor_scalar(rsin[:, :, :], ang[:, :, :], lim, -lim, ALU.min, ALU.max))
            link(nc.vector.tensor_scalar(tmp[:, :, :], rsin[:, :, :], -1.0, None, ALU.mult))
            link(nc.vector.tensor_tensor(tmp[:, :, :], tmp[:, :, :], rsin[:, :, :], ALU.min))
            nc.vector.tensor_scalar(rcos[:, :, :], tmp[:, :, :], math.pi / 2, None, ALU.add).then_inc(trig, 1)
            dve.wait_ge(lam_ps, 1)
            nc.vector.tensor_copy(g.neglam[:, :], psl[:, 0:1])
            link(nc.vector.tensor_tensor(mod[:, :], psm[:, 0:6 * KD], g.vcol[:, R_BMOD:R_BMOD + 6 * KD], ALU.add))
            for n, (r_pre, r_post) in enumerate(((R_GPRE, R_GPOST), (R_GFPRE, R_GFPOST))):
                m = 3 * KD * n
                link(nc.vector.tensor_copy(g.shift[:, n, :], mod[:, m:m + KD]))
                link(nc.vector.scalar_tensor_tensor(out=g.gain[:, n, :], in0=mod[:, m + KD:m + 2 * KD], scalar=1.0,
                                                    in1=g.vcol[:, r_pre:r_pre + KD], op0=ALU.add, op1=ALU.mult))
                link(nc.vector.tensor_tensor(gcol[:, n, :], mod[:, m + 2 * KD:m + 3 * KD],
                                             g.vcol[:, r_post:r_post + KD], ALU.mult))
            link(nc.vector.tensor_copy(gcol[:, 2, :], g.gain[:, 1, :]))
            link(nc.vector.tensor_copy(gcol[:, 3, :], g.shift[:, 1, :]))
            for n in range(4):
                for k in range(KD):
                    ins = nc.vector.tensor_copy(wide[:, n % 2, k, :], gcol[:, n, k:k + 1].to_broadcast([P, P]))
                ins.then_inc(wide_ready, 1)
                dve.wait_ge(wide_ps, n + 1)
                nc.vector.tensor_copy(outgain[:, n], psw[:, :, :].rearrange("p b c -> p (b c)")).then_inc(wide_copied, 1)
            dve.wait_ge(sines, 2)
            dve.wait_ge(rot_set, 1)
            tab = rot[:, :, :, :].rearrange("p t v (h c) -> p t v h c", c=HD)
            for h in range(2):
                link(nc.vector.tensor_copy(tab[:, :, 0, h, 0:HALF], cosv[:, :, :]))
                link(nc.vector.tensor_copy(tab[:, :, 0, h, HALF:ROPE], cosv[:, :, :]))
                link(nc.vector.tensor_scalar(tab[:, :, 1, h, 0:HALF], sinv[:, :, :], -1.0, None, ALU.mult))
                link(nc.vector.tensor_copy(tab[:, :, 1, h, HALF:ROPE], sinv[:, :, :]))
            nc.vector.memset(tmp[:, :, :], 0.0).then_inc(rot_ready, 1)
            for t in range(NT):
                dve.wait_ge(rot_ps, t + 1)
                nc.vector.tensor_copy(g.rot[:, :, t * P:(t + 1) * P], psr[:, t % 2, 0:2 * P].rearrange("p (v c) -> p v c", v=2)).then_inc(rot_copied, 1)


def normalise(nc, a, g):
    with ExitStack() as ctx:
        sb, ps, sem = allocators(nc, ctx)
        G = 4
        x = sb("n_x", [P, 2, G, D])
        junk = sb("n_junk", [P, D])
        rms = sb("n_rms", [P, NT])
        inv = sb("n_inv", [P, NT])
        u = sb("n_u", [P, KD, P])
        pst = ps("n_pst", [P, 2, KD, P])
        loaded = [sem(f"n_l{i}") for i in range(2)]
        squared, rooted, dlink = sem("n_sq"), sem("n_root"), sem("n_dlink")
        mean_ready, scaled, turned, hi_done, lo_done = sem("n_mean"), sem("n_sc"), sem("n_tu"), sem("n_hi"), sem("n_lo")
        block = ctx.enter_context(nc.Block())
        xd = a.x[0].rearrange("(t p) d -> p t d", p=P)

        @block.sync
        def _(sp):
            for q in range(NT // G):
                if q >= 2:
                    sp.wait_ge(turned, G * (q - 1))
                sp.dma_start(x[:, q % 2], xd[:, G * q:G * q + G, :]).then_inc(loaded[q % 2], 16)

        @block.scalar
        def _(act):
            def squares(q):
                act.wait_ge(loaded[q % 2], 16 * (q // 2 + 1))
                for t in range(G * q, G * q + G):
                    if t:
                        act.wait_ge(squared, t)
                    nc.scalar.activation(junk[:, :], x[:, q % 2, t % G, :], ACT.Square,
                                         accum_out=rms[:, t:t + 1]).then_inc(squared, 1)
                act.wait_ge(mean_ready, q + 1)
                nc.scalar.activation(inv[:, G * q:G * q + G], inv[:, G * q:G * q + G], ACT.Sqrt).then_inc(rooted, 1)

            squares(0)
            for t in range(NT):
                if t % G == 0 and t + G < NT:
                    squares(t // G + 1)
                act.wait_ge(turned, t + 1)
                for k in range(KD):
                    ins = nc.scalar.activation(g.uth[:, k, t * P:(t + 1) * P], pst[:, t % 2, k, :], ACT.Identity,
                                               scale=g.gain[:, 0, k:k + 1], bias=g.shift[:, 0, k:k + 1])
                ins.then_inc(hi_done, 1)

        @block.vector
        def _(dve):
            link = Link(dve, dlink)

            def means(q):
                dve.wait_ge(squared, G * q + G)
                nc.vector.tensor_scalar(inv[:, G * q:G * q + G], rms[:, G * q:G * q + G], 1.0 / D, EPS,
                                        ALU.mult, ALU.add).then_inc(mean_ready, 1)
                dve.wait_ge(rooted, q + 1)
                link(nc.vector.reciprocal(inv[:, G * q:G * q + G], inv[:, G * q:G * q + G]))

            def scale(t):
                xt = x[:, t // G % 2, t % G, :]
                nc.vector.tensor_scalar(xt, xt, inv[:, t:t + 1], None, ALU.mult).then_inc(scaled, 1)

            means(0)
            scale(0)
            scale(1)
            for t in range(NT):
                if t % G == 0 and t + G < NT:
                    means(t // G + 1)
                dve.wait_ge(hi_done, t + 1)
                if t >= 1:
                    dve.wait_ge(lo_done, t)
                for k in range(KD):
                    ins = nc.vector.tensor_scalar(u[:, k, :], pst[:, t % 2, k, :], g.gain[:, 0, k:k + 1],
                                                  g.shift[:, 0, k:k + 1], ALU.mult, ALU.add)
                link(ins)
                ut = g.uth[:, :, t * P:(t + 1) * P].bitcast(F32)
                nc.vector.tensor_tensor(g.utl[:, :, t * P:(t + 1) * P], u[:, :, :], ut, ALU.subtract).then_inc(lo_done, 1)
                if t + 2 < NT:
                    scale(t + 2)

        @block.tensor
        def _(pe):
            for t in range(NT):
                pe.wait_ge(scaled, t + 1)
                if t >= 2:
                    pe.wait_ge(lo_done, t - 1)
                for k in range(KD):
                    ins = nc.tensor.transpose(pst[:, t % 2, k, :], x[:, t // G % 2, t % G, k * P:(k + 1) * P],
                                              g.ident[:, :])
                ins.then_inc(turned, 1)


COLS = 2 * P
BLOCKS = IN_W // COLS
TB = T // BANK
SEGMENTS = (("q", 0, QKW // COLS), ("k", QKW // COLS, QKW // COLS), ("v", 2 * QKW // COLS, VW // COLS),
            ("p", (2 * QKW + VW) // COLS, PG * P // COLS),
            ("g", (2 * QKW + VW + PG * P) // COLS, 2 * D // COLS))


SWAP = [HALF + i for i in range(HALF)] + list(range(HALF)) + list(range(ROPE, 32))


def units_of(kind):
    return [(m, t) for m in range(2) for t in range(TB)] if kind != "v" else [(0, t) for t in range(NT)]


def project(nc, a, g):
    with ExitStack() as ctx:
        sb, ps, sem = allocators(nc, ctx)
        RING = 4
        raw = sb("j_raw", [P, KD, COLS])
        wh = [sb(f"j_wh{i}", [P, KD, COLS], F32R) for i in range(2)]
        wl = [sb(f"j_wl{i}", [P, KD, COLS], F32R) for i in range(2)]
        z = sb("j_z", [P, RING, BANK])
        swap = sb("j_swap", [P, 2, BANK])
        psz = ps("j_psz", [P, RING, BANK])
        wloaded, hi_done, lo_done = sem("j_w"), sem("j_hi"), sem("j_lo")
        made, copied, roped, dlink = sem("j_made"), sem("j_copied"), sem("j_roped"), sem("j_dlink")
        stored = [sem(f"j_st{i}") for i in range(RING)]
        block = ctx.enter_context(nc.Block())
        w = a.w_in[0].rearrange("(k p) n -> p k n", p=P)

        def blocks(eng, body, peel_last=False):
            unit = 0
            for kind, first, count in SEGMENTS:
                per = len(units_of(kind))
                turns = count // 2 - (peel_last and kind == "g")
                with eng.Fori(0, turns) as i:
                    for slot in range(2):
                        body(kind, i * 2 + (first + slot), slot, i * (2 * per) + (unit + slot * per), False)
                if turns < count // 2:
                    for slot in range(2):
                        body(kind, first + 2 * turns + slot, slot, unit + (2 * turns + slot) * per, slot == 1)
                unit += count * per

        @block.gpsimd
        def _(pool):
            nc.gpsimd.dma_start(raw[:, :, :], w[:, :, 0:COLS]).then_inc(wloaded, 16)
            with pool.Fori(1, BLOCKS) as b:
                pool.wait_ge(lo_done, b)
                nc.gpsimd.dma_start(raw[:, :, :], w[:, :, ds(b * COLS, COLS)]).then_inc(wloaded, 16)

        @block.scalar
        def _(act):
            for r in range(RING):
                act.sem_inc(stored[r], 16)
            act.sem_inc(copied, RING)
            act.wait_ge(wloaded, 16)
            nc.scalar.copy(wh[0][:, :, :], raw[:, :, :]).then_inc(hi_done, 1)

            def body(kind, b, slot, unit, last):
                for n in range(len(units_of(kind))):
                    r = n % RING
                    act.wait_ge(made, unit + (n + 1))
                    act.wait_ge(stored[r], unit * (16 // RING) + 16 * (n // RING + 1))
                    wide = psz[:, r, :] if kind != "v" else psz[:, r, 0:COLS]
                    out = z[:, r, :] if kind != "v" else z[:, r, 0:COLS]
                    if kind == "g":
                        ins = nc.scalar.activation(out, wide, ACT.Sigmoid)
                    elif kind == "q":
                        ins = nc.scalar.activation(out, wide, ACT.Copy, scale=HD ** -0.5)
                    else:
                        ins = nc.scalar.copy(out, wide)
                    ins.then_inc(copied, 1)
                    if n == 1 and not last:
                        act.wait_ge(wloaded, b * 16 + 32)
                        nc.scalar.copy(wh[1 - slot][:, :, :], raw[:, :, :]).then_inc(hi_done, 1)

            blocks(act, body, peel_last=True)

        @block.vector
        def _(dve):
            def split_lo(after, slot):
                dve.wait_ge(hi_done, after)
                nc.vector.tensor_tensor(wl[slot][:, :, :], raw[:, :, :], wh[slot][:, :, :].bitcast(F32),
                                        ALU.subtract).then_inc(lo_done, 1)

            split_lo(1, 0)

            def body(kind, b, slot, unit, last):
                for n, (m, t) in enumerate(units_of(kind)):
                    r = n % RING
                    if kind in "qk":
                        dve.wait_ge(copied, unit + (n + 1 + RING))
                        zz = z[:, r, :]
                        nc.vector.tensor_tensor(swap[:, 1, :], zz, g.rot[:, 0, t * BANK:(t + 1) * BANK],
                                                ALU.mult).then_inc(dlink, 1)
                        nc.vector.stream_shuffle(swap[:, 0, :], zz, SWAP).then_inc(dlink, 1)
                        dve.wait_ge(dlink, unit * 3 + (3 * n + 2))
                        nc.vector.tensor_tensor(swap[:, 0, :], swap[:, 0, :], g.rot[:, 1, t * BANK:(t + 1) * BANK],
                                                ALU.mult).then_inc(dlink, 1)
                        dve.wait_ge(dlink, unit * 3 + (3 * n + 3))
                        nc.vector.tensor_tensor(zz, swap[:, 0, :], swap[:, 1, :], ALU.add).then_inc(roped, 1)
                        dve.wait_ge(roped, unit + (n + 1))
                    if n == 1 and not last:
                        split_lo(b + 2, 1 - slot)

            blocks(dve, body, peel_last=True)

        @block.tensor
        def _(pe):
            def body(kind, b, slot, unit, last):
                pe.wait_ge(lo_done, b + 1)
                for n, (m, t) in enumerate(units_of(kind)):
                    r = n % RING
                    pe.wait_ge(copied, unit + (n + 1))
                    for k in range(KD):
                        if kind != "v":
                            tok = slice(t * BANK, (t + 1) * BANK)
                            col = slice(m * P, (m + 1) * P)
                            terms = ((wh[slot][:, k, col], g.uth[:, k, tok]), (wh[slot][:, k, col], g.utl[:, k, tok]),
                                     (wl[slot][:, k, col], g.uth[:, k, tok]))
                            out = psz[:, r, :]
                        else:
                            tok = slice(t * P, (t + 1) * P)
                            terms = ((g.uth[:, k, tok], wh[slot][:, k, :]), (g.uth[:, k, tok], wl[slot][:, k, :]),
                                     (g.utl[:, k, tok], wh[slot][:, k, :]))
                            out = psz[:, r, 0:COLS]
                        for j, (still, moving) in enumerate(terms):
                            ins = nc.tensor.matmul(out, still, moving, start=(k == 0 and j == 0),
                                                   stop=(k == KD - 1 and j == 2))
                    ins.then_inc(made, 1)

            blocks(pe, body)

        @block.sync
        def _(sp):
            def body(kind, b, slot, unit, last):
                for n, (m, t) in enumerate(units_of(kind)):
                    r = n % RING
                    if kind in "qk":
                        sp.wait_ge(roped, unit + (n + 1))
                    else:
                        sp.wait_ge(copied, unit + (n + 1 + RING))
                    if kind == "v":
                        out = g.v_d[t * P:(t + 1) * P, ds(b * COLS - 2 * QKW, COLS)]
                        src = z[:, r, 0:COLS]
                    else:
                        out = g.zt_d[ds(b * COLS + m * P, P), t * BANK:(t + 1) * BANK]
                        src = z[:, r, :]
                    nc.sync.dma_start(out, src).then_inc(stored[r], 16)

            blocks(sp, body)
            total = sum(count * len(units_of(kind)) for kind, _, count in SEGMENTS)
            for r in range(RING):
                sp.wait_ge(stored[r], 16 * (total // RING + 1))


def pool_mix(nc, a, g):
    with ExitStack() as ctx:
        sb, ps, sem = allocators(nc, ctx)
        PAD = max(WINDOWS)
        p = sb("w_p", [P, 2, PAD + T])
        lev = sb("w_lev", [P, 2, PAD + T])
        cnt = sb("w_cnt", [P, PG, PAD])
        head = sb("w_head", [P, PAD])
        mh = sb("w_mh", [P, T], F32R)
        ml = sb("w_ml", [P, T], F32R)
        wraw = sb("w_raw", [P, PG, P])
        wh = sb("w_wh", [P, PG, P], F32R)
        wl = sb("w_wl", [P, PG, P], F32R)
        y = sb("w_y", [P, 2, T])
        psy = ps("w_ps", [P, 4, BANK])
        ploaded, wloaded = [sem("w_pl0"), sem("w_pl1")], sem("w_wl")
        cleared, wsplit, dlink, mixed = sem("w_clr"), sem("w_ws"), sem("w_dl"), sem("w_mix")
        hi_done, lo_done, made, left = sem("w_hi"), sem("w_lo"), sem("w_made"), sem("w_left")
        wlow, stored, table = sem("w_wlow"), [sem("w_st0"), sem("w_st1")], sem("w_tab")
        block = ctx.enter_context(nc.Block())
        p_row = 2 * QKW + VW

        @block.sync
        def _(sp):
            sp.dma_start(wraw[:, :, :], a.w_pool_group[0].rearrange("g c d -> c g d")).then_inc(wloaded, 16)
            for q in range(PG):
                if q >= 2:
                    sp.wait_ge(lo_done, q - 1)
                sp.dma_start(p[:, q % 2, PAD:], g.zt_d[p_row + q * P:p_row + (q + 1) * P, :]).then_inc(ploaded[q % 2], 16)
                if q >= 1:
                    sp.wait_ge(left, 4 * q)
                    sp.dma_start(g.yt_d[(q - 1) * P:q * P, :], y[:, (q - 1) % 2, :]).then_inc(stored[(q - 1) % 2], 16)
            sp.wait_ge(left, 4 * PG)
            sp.dma_start(g.yt_d[(PG - 1) * P:PG * P, :], y[:, (PG - 1) % 2, :]).then_inc(stored[(PG - 1) % 2], 16)
            sp.wait_ge(stored[0], 32)
            sp.wait_ge(stored[1], 32)

        @block.gpsimd
        def _(pool):
            nc.gpsimd.memset(lev[:, :, 0:PAD], 0.0)
            nc.gpsimd.memset(p[:, :, 0:PAD], 0.0).then_inc(cleared, 1)
            for q, w in enumerate(WINDOWS):
                for t in range(PAD):
                    ins = nc.gpsimd.memset(cnt[:, q, t:t + 1], 1.0 / min(t + 1, w))
            ins.then_inc(table, 1)

        @block.scalar
        def _(act):
            act.wait_ge(wloaded, 16)
            nc.scalar.copy(wh[:, :, :], wraw[:, :, :]).then_inc(wsplit, 1)
            for q in range(PG):
                act.wait_ge(mixed, q + 1)
                if q:
                    act.wait_ge(made, 4 * q)
                nc.scalar.copy(mh[:, :], p[:, q % 2, PAD:]).then_inc(hi_done, 1)
                for t in range(TB):
                    act.wait_ge(made, 4 * q + t + 1)
                    if t == 0 and q >= 2:
                        act.wait_ge(stored[q % 2], 16)
                    nc.scalar.activation(y[:, q % 2, t * BANK:(t + 1) * BANK], psy[:, t, :], ACT.Copy,
                                         scale=g.vcol[:, R_PSC + q:R_PSC + q + 1]).then_inc(left, 1)

        @block.vector
        def _(dve):
            link = Link(dve, dlink)
            dve.wait_ge(wsplit, 1)
            nc.vector.tensor_tensor(wl[:, :, :], wraw[:, :, :], wh[:, :, :].bitcast(F32), ALU.subtract).then_inc(wlow, 1)
            dve.wait_ge(cleared, 1)
            dve.wait_ge(table, 1)
            for q, w in enumerate(WINDOWS):
                dve.wait_ge(ploaded[q % 2], 16 * (q // 2 + 1))
                src, step, n = p[:, q % 2], 1, 0
                while step < w:
                    dst = lev[:, n % 2]
                    link(nc.vector.tensor_tensor(dst[:, PAD:], src[:, PAD:], src[:, PAD - step:PAD + T - step], ALU.add))
                    src, step, n = dst, step * 2, n + 1
                pq = p[:, q % 2]
                link(nc.vector.tensor_tensor(head[:, :], src[:, PAD:2 * PAD], cnt[:, q], ALU.mult))
                link(nc.vector.tensor_tensor(head[:, :], head[:, :], pq[:, PAD:2 * PAD], ALU.subtract))
                link(nc.vector.scalar_tensor_tensor(out=pq[:, PAD:], in0=src[:, PAD:], scalar=1.0 / w, in1=pq[:, PAD:],
                                                    op0=ALU.mult, op1=ALU.subtract))
                nc.vector.tensor_copy(pq[:, PAD:2 * PAD], head[:, :]).then_inc(mixed, 1)
                dve.wait_ge(hi_done, q + 1)
                nc.vector.tensor_tensor(ml[:, :], pq[:, PAD:], mh[:, :].bitcast(F32), ALU.subtract).then_inc(lo_done, 1)

        @block.tensor
        def _(pe):
            pe.wait_ge(wlow, 1)
            for q in range(PG):
                pe.wait_ge(lo_done, q + 1)
                for t in range(TB):
                    if q:
                        pe.wait_ge(left, 4 * (q - 1) + t + 1)
                    c = slice(t * BANK, (t + 1) * BANK)
                    nc.tensor.matmul(psy[:, t, :], wh[:, q, :], mh[:, c], start=True, stop=False)
                    nc.tensor.matmul(psy[:, t, :], wh[:, q, :], ml[:, c], start=False, stop=False)
                    nc.tensor.matmul(psy[:, t, :], wl[:, q, :], mh[:, c], start=False, stop=True).then_inc(made, 1)


def attend(nc, a, g):
    with ExitStack() as ctx:
        sb, ps, sem = allocators(nc, ctx)
        SR, TR = 5, 2
        PC = T // 2
        kh = [sb(f"t_kh{i}", [P, 2, T], F32R) for i in range(2)]
        kl = [sb(f"t_kl{i}", [P, 2, T], F32R) for i in range(2)]
        rq = sb("t_rq", [P, 2, T])
        qs = [sb(f"t_qs{i}", [P, 2, T], F32R) for i in range(2)]
        v2 = [sb(f"t_v2{i}", [P, NT, 2, P], F32R) for i in range(2)]
        pr = sb("t_pr", [P, 2, 2, T])
        ath = sb("t_ath", [P, NT, P], F32R)
        atl = sb("t_atl", [P, NT, P], F32R)
        ost = sb("t_ost", [P, NT, P])
        o1 = sb("t_o1", [P, P])
        mx = sb("t_mx", [P, 2, 4])
        mm = sb("t_mm", [P, 2])
        negm = sb("t_negm", [P, 2, 2])
        part = sb("t_part", [P, 2, 2, 4])
        tot = sb("t_tot", [P, 2, 2])
        rec = sb("t_rec", [P, 2, 2])
        mix = sb("t_mix", [P, 2])
        mrow = sb("t_mrow", [1, P], BF16)
        mcol = sb("t_mcol", [1, CHUNK], BF16)
        pss = ps("t_pss", [P, SR, BANK])
        pst = ps("t_pst", [P, TR, BANK])
        pso = ps("t_pso", [P, BANK])
        raw_in, raw_ready, hi_done, split = sem("t_raw"), sem("t_rawr"), sem("t_hi"), sem("t_split")
        freed = sem("t_freed")
        s_ready, exp_done, negm_ready, a_ready = sem("t_s"), sem("t_exp"), sem("t_negm"), sem("t_a")
        t_ready, th_done, tl_done, av_done = sem("t_t"), sem("t_th"), sem("t_tl"), sem("t_av")
        o1_done, o_done, ostored, masks, dl = sem("t_o1"), sem("t_o"), sem("t_ost"), sem("t_masks"), sem("t_dl")
        block = ctx.enter_context(nc.Block())

        nb = [-(-(i + 1) * P // BANK) for i in range(NT)]
        width = lambda i, b: min(BANK, (i + 1) * P - b * BANK)
        seq, n = {}, 0
        for i in range(NT):
            for s in range(2):
                for b in range(nb[i]):
                    seq[i, s, b] = n
                    n += 1
        SB = n
        gbase = [sum(nb[:i]) for i in range(NT + 1)]
        GB = gbase[NT]
        assert SB % SR == 0 and GB % TR == 0
        PIECES = 10

        def steps(start, behind, both, finish):
            for j in range(NT + 2):
                tile = lambda i: i if 0 <= i < NT else None
                start(tile(j))
                behind(tile(j - 1), tile(j - 2))
                both(tile(j - 1), tile(j))
                finish(tile(j - 2), tile(j))

        def heads(eng, body):
            with eng.Fori(0, HEADS // 2) as hh:
                for par in range(2):
                    body(hh * 2 + par, par, hh)

        def hi_piece(par, n):
            if n < 4:
                c = slice(n % 2 * PC, (n % 2 + 1) * PC)
                return kh[par][:, n // 2, c], kl[par][:, n // 2, c].bitcast(F32)
            if n < 8:
                c = slice(n % 2 * PC, (n % 2 + 1) * PC)
                return qs[par][:, n // 2 - 2, c], rq[:, n // 2 - 2, c]
            t = slice((n - 8) * NT // 2, (n - 7) * NT // 2)
            return v2[par][:, t, 0, :], v2[par][:, t, 1, :].bitcast(F32)

        def lo_piece(par, n):
            hi, raw = hi_piece(par, n)
            if 4 <= n < 8:
                return hi[HD:P], raw[HD:P], hi[HD:P].bitcast(F32)
            if n < 4:
                return kl[par][:, n // 2, n % 2 * PC:(n % 2 + 1) * PC], raw, hi.bitcast(F32)
            return v2[par][:, (n - 8) * NT // 2:(n - 7) * NT // 2, 1, :], raw, hi.bitcast(F32)

        @block.gpsimd
        def _(pool):
            nc.gpsimd.memset(mrow[:, :], 0.0).then_inc(masks, 1)
            pool.wait_ge(masks, 1)
            nc.gpsimd.memset(mrow[:, 0:CHUNK], 1.0).then_inc(masks, 1)
            nc.gpsimd.memset(mcol[:, :], NEG).then_inc(masks, 1)
            q_v = g.zt_d[0:QKW, :]
            k_v = g.zt_d[QKW:2 * QKW, :]
            v_v = g.v_d.rearrange("(t p) d -> p t d", p=P)

            def load(h, par):
                row = h * P
                for half in range(2):
                    rows = slice(half * HD, (half + 1) * HD)
                    nc.gpsimd.dma_start(kl[par][rows].bitcast(F32),
                                        k_v[ds(row, P), :].rearrange("(s d) t -> d s t", s=2)).then_inc(raw_in, 16)
                    nc.gpsimd.dma_start(rq[rows], q_v[ds(row, P), :].rearrange("(s d) t -> d s t", s=2)).then_inc(raw_in, 16)
                nc.gpsimd.dma_start(v2[par][:, :, 1, :].bitcast(F32), v_v[:, :, ds(row, P)]).then_inc(raw_in, 16)
                pool.wait_ge(raw_in, h * 80 + 80)

            load(0, 0)
            pool.sem_inc(raw_ready, 1)
            pool.wait_ge(split, PIECES)

            def body(h, par, hh):
                pool.wait_ge(av_done, h * NT + 1)
                pool.sem_inc(freed, 1)
                if par:
                    with pool.If(hh < HEADS // 2 - 1):
                        load(nc.s_assert_within(h + 1, 0, HEADS - 1, skip_runtime_bounds_check_because="the branch bounds it"),
                             1 - par)
                else:
                    load(h + 1, 1 - par)
                pool.sem_inc(raw_ready, 1)
                for n in range(PIECES):
                    pool.wait_ge(hi_done, h * PIECES + (PIECES + n + 1))
                    out, raw, hi = lo_piece(1 - par, n)
                    nc.gpsimd.tensor_tensor(out, raw, hi, ALU.subtract).then_inc(split, 1)
                    pool.wait_ge(split, h * PIECES + (PIECES + n + 1))

            heads(pool, body)

        @block.sync
        def _(sp):
            sp.sem_inc(ostored, 16)
            with sp.Fori(0, HEADS) as h:
                sp.wait_ge(o_done, h * NT + (NT + 1))
                sp.dma_start(g.o_d.rearrange("(t p) d -> p t d", p=P)[:, :, ds(h * P, P)], ost[:, :, :]).then_inc(ostored, 16)
            sp.wait_ge(ostored, 16 * (HEADS + 1))

        @block.scalar
        def _(act):
            act.sem_inc(s_ready, 1)
            act.sem_inc(av_done, 1)
            act.sem_inc(o_done, 1)
            act.sem_inc(exp_done, SR)
            act.sem_inc(tl_done, TR)
            act.wait_ge(raw_ready, 1)
            for n in range(PIECES):
                out, raw = hi_piece(0, n)
                nc.scalar.copy(out, raw).then_inc(hi_done, 1)

            def body(h, par, hh):
                def exps(i, s):
                    act.wait_ge(negm_ready, h * (2 * NT) + (2 * i + s + 1))
                    for b in range(nb[i]):
                        w = width(i, b)
                        nc.scalar.activation(pr[:, i % 2, s, b * BANK:b * BANK + w], pss[:, seq[i, s, b] % SR, 0:w],
                                             ACT.Exp, bias=negm[:, i % 2, s:s + 1],
                                             accum_out=part[:, i % 2, s, b:b + 1]).then_inc(exp_done, 1)

                def start(i):
                    if i is not None:
                        exps(i, 0)

                def behind(i, before):
                    n = (i or 0) - 5
                    if 0 <= n < PIECES:
                        if n == 0:
                            act.wait_ge(raw_ready, h + 2)
                        out, raw = hi_piece(1 - par, n)
                        nc.scalar.copy(out, raw).then_inc(hi_done, 1)

                def both(i, after):
                    for q in range(nb[i] if i is not None else 0):
                        act.wait_ge(t_ready, h * GB + (gbase[i] + q + 1))
                        c = min(4, i + 1 - 4 * q) * P
                        nc.scalar.copy(ath[:, 4 * q:4 * q + c // P, :].rearrange("p t c -> p (t c)"),
                                       pst[:, (gbase[i] + q) % TR, 0:c]).then_inc(th_done, 1)

                def finish(before, i):
                    if before is not None:
                        act.wait_ge(av_done, h * NT + (before + 2))
                        act.wait_ge(o_done, h * NT + (before + 1))
                        nc.scalar.activation(o1[:, :], pso[:, 0:P], ACT.Copy,
                                             scale=rec[:, before % 2, 0:1]).then_inc(o1_done, 1)
                    if i is not None:
                        exps(i, 1)

                steps(start, behind, both, finish)

            heads(act, body)

        @block.vector
        def _(dve):
            for n in range(PIECES):
                dve.wait_ge(hi_done, n + 1)
                out, raw, hi = lo_piece(0, n)
                nc.vector.tensor_tensor(out, raw, hi, ALU.subtract).then_inc(split, 1)

            def body(h, par, hh):
                chain = [0]
                LINKS = sum((2 * (n + (n > 1))) + (n > 1) + 2 for n in nb)

                def link(ins):
                    chain[0] += 1
                    ins.then_inc(dl, 1)
                    dve.wait_ge(dl, h * LINKS + chain[0])

                def maximum(i, s, b):
                    dve.wait_ge(s_ready, h * SB + (seq[i, s, b] + 2))
                    ins = nc.vector.tensor_reduce(mx[:, s, b:b + 1], pss[:, seq[i, s, b] % SR, 0:width(i, b)], AX, ALU.max)
                    if b + 1 < nb[i]:
                        chain[0] += 1
                        ins.then_inc(dl, 1)
                        return
                    link(ins)
                    top = mx[:, s, 0:1]
                    if nb[i] > 1:
                        link(nc.vector.tensor_reduce(mm[:, s:s + 1], mx[:, s, 0:nb[i]], AX, ALU.max))
                        top = mm[:, s:s + 1]
                    nc.vector.tensor_scalar(negm[:, i % 2, s:s + 1], top, -1.0, None, ALU.mult).then_inc(negm_ready, 1)

                def start(i):
                    for b in range(nb[i] if i is not None else 0):
                        maximum(i, 0, b)

                def behind(i, before):
                    if i is None:
                        return
                    dve.wait_ge(exp_done, h * SB + (seq[i, 1, nb[i] - 1] + 1 + SR))
                    sums = part[:, i % 2, :, 0]
                    if nb[i] > 1:
                        link(nc.vector.tensor_reduce(tot[:, i % 2], part[:, i % 2, :, 0:nb[i]], AX, ALU.add))
                        sums = tot[:, i % 2]
                    link(nc.vector.reciprocal(rec[:, i % 2], sums))
                    link(nc.vector.scalar_tensor_tensor(out=mix[:, i % 2:i % 2 + 1], in0=sums[:, 0:1],
                                                        scalar=g.neglam[:, 0:1], in1=rec[:, i % 2, 1:2],
                                                        op0=ALU.mult, op1=ALU.mult))
                    w = (i + 1) * P
                    nc.vector.scalar_tensor_tensor(out=pr[:, i % 2, 0, 0:w], in0=pr[:, i % 2, 1, 0:w],
                                                   scalar=mix[:, i % 2:i % 2 + 1], in1=pr[:, i % 2, 0, 0:w],
                                                   op0=ALU.mult, op1=ALU.add).then_inc(a_ready, 1)

                def both(i, after):
                    for q in range(4):
                        if after is not None and q < nb[after]:
                            maximum(after, 1, q)
                        if i is not None and q < nb[i]:
                            dve.wait_ge(th_done, h * GB + (gbase[i] + q + 1))
                            c = min(4, i + 1 - 4 * q) * P
                            flat = slice(4 * q, 4 * q + c // P)
                            nc.vector.tensor_tensor(atl[:, flat, :].rearrange("p t c -> p (t c)"),
                                                    pst[:, (gbase[i] + q) % TR, 0:c],
                                                    ath[:, flat, :].rearrange("p t c -> p (t c)").bitcast(F32),
                                                    ALU.subtract).then_inc(tl_done, 1)

                def finish(before, i):
                    if before is None:
                        return
                    if before == 0:
                        dve.wait_ge(ostored, h * 16 + 16)
                    dve.wait_ge(o1_done, h * NT + (before + 1))
                    nc.vector.scalar_tensor_tensor(out=ost[:, before, :], in0=pso[:, P:2 * P],
                                                   scalar=rec[:, before % 2, 0:1], in1=o1[:, :],
                                                   op0=ALU.mult, op1=ALU.add).then_inc(o_done, 1)

                steps(start, behind, both, finish)
                assert chain[0] == LINKS, (chain[0], LINKS)

            heads(dve, body)

        @block.tensor
        def _(pe):
            pe.wait_ge(masks, 3)

            def body(h, par, hh):
                pe.wait_ge(split, h * PIECES + PIECES)

                def scores(i, s, b):
                    still = qs[par][:, s, i * P:(i + 1) * P]
                    n, w = seq[i, s, b], width(i, b)
                    last = b == nb[i] - 1
                    pe.wait_ge(exp_done, h * SB + (n + 1))
                    c = slice(b * BANK, b * BANK + w)
                    nc.tensor.matmul(pss[:, n % SR, 0:w], still, kh[par][:, s, c], start=True, stop=False)
                    ins = nc.tensor.matmul(pss[:, n % SR, 0:w], still, kl[par][:, s, c], start=False, stop=not last)
                    if last:
                        ins = nc.tensor.matmul(pss[:, n % SR, w - CHUNK:w], mrow[:, :], mcol[:, :], start=False, stop=True)
                    ins.then_inc(s_ready, 1)

                def start(i):
                    for b in range(nb[i] if i is not None else 0):
                        scores(i, 0, b)

                def behind(i, before):
                    if before is None:
                        return
                    pe.wait_ge(o_done, h * NT + (before + 1))
                    pe.wait_ge(tl_done, h * GB + (gbase[before + 1] + TR))
                    for t in range(before + 1):
                        both_v = v2[par][:, t].rearrange("p s c -> p (s c)")
                        nc.tensor.matmul(pso[:, 0:2 * P], ath[:, t, :], both_v, start=(t == 0), stop=False)
                        ins = nc.tensor.matmul(pso[:, 0:2 * P], atl[:, t, :], both_v, start=False, stop=(t == before))
                    ins.then_inc(av_done, 1)

                def both(i, after):
                    for q in range(4):
                        if after is not None and q < nb[after]:
                            scores(after, 1, q)
                        if i is not None and q < nb[i]:
                            if q == 0:
                                pe.wait_ge(a_ready, h * NT + (i + 1))
                            pe.wait_ge(tl_done, h * GB + (gbase[i] + q + 1))
                            for t in range(4 * q, min(4 * q + 4, i + 1)):
                                ins = nc.tensor.transpose(pst[:, (gbase[i] + q) % TR, (t % 4) * P:(t % 4 + 1) * P],
                                                          pr[:, i % 2, 0, t * P:(t + 1) * P], g.ident[:, :])
                            ins.then_inc(t_ready, 1)

                steps(start, behind, both, lambda before, i: None)

            heads(pe, body)


def pipeline(eng, stages, count):
    deepest = max(lag for _, lag in stages)
    first = deepest + 2 + deepest % 2

    def step(at, base):
        for fn, lag in stages:
            if base is None:
                if 0 <= at - lag < count:
                    fn(at - lag, (at - lag) % 2)
            else:
                fn(base + (at - lag), (at - lag) % 2)

    for n in range(first):
        step(n, None)
    with eng.Fori(0, (count - first) // 2) as i:
        step(first, i * 2)
        step(first + 1, i * 2)
    for n in range(count, count + deepest):
        step(n, None)


def early(t, n):
    return isinstance(t, int) and t < n


def branches(nc, a, g):
    with ExitStack() as ctx:
        sb, ps, sem = allocators(nc, ctx)
        KP = PG
        KW = KD + KP
        raw = sb("b_raw", [P, 2, D])
        wh = sb("b_wh", [P, KW, D], F32R)
        wl = sb("b_wl", [P, KW, D], F32R)
        o = sb("b_o", [P, TB, HEADS, P])
        sq = sb("b_sq", [P, HEADS, P])
        rs = sb("b_rs", [P, TB, HEADS])
        gs = sb("b_gs", [P, 1])
        xh = sb("b_xh", [P, KW, BANK], F32R)
        xl = sb("b_xl", [P, KW, BANK], F32R)
        gate = sb("b_gate", [P, 2, 2, BANK])
        ma = sb("b_ma", [P, BANK])
        mg = sb("b_mg", [P, 2, BANK])
        yraw = gate[:, :, :, :].rearrange("p a b c -> p (a b) c")
        psa = ps("b_psa", [P, 2, 2, BANK])
        pst = ps("b_pst", [P, 2, BANK])
        wloaded, whi, wlo = [sem("b_w0"), sem("b_w1")], sem("b_whi"), sem("b_wlo")
        oin, yin, gin = sem("b_oin"), sem("b_yin"), [sem("b_g0"), sem("b_g1")]
        dl, mean, rooted, normed = sem("b_dl"), sem("b_mean"), sem("b_root"), sem("b_norm")
        turned, xhi, xlo, yhi, ylo = sem("b_turn"), sem("b_xhi"), sem("b_xlo"), sem("b_yhi"), sem("b_ylo")
        made, merged, stored = sem("b_made"), sem("b_merged"), [sem("b_s0"), sem("b_s1")]
        block = ctx.enter_context(nc.Block())
        watt = a.w_att_branch[0].rearrange("(k p) n -> k p n", p=P)
        wpool = a.w_pool_branch[0].rearrange("(k p) n -> k p n", p=P)
        ov = g.o_d.rearrange("(b t p) (h c) -> b p t h c", t=TB, p=P, h=HEADS)
        GA = 2 * QKW + VW + PG * P

        @block.gpsimd
        def _(pool):
            for k in range(KW):
                if k >= 2:
                    pool.wait_ge(wlo, k - 1)
                src = watt[k] if k < KD else wpool[k - KD]
                nc.gpsimd.dma_start(raw[:, k % 2], src).then_inc(wloaded[k % 2], 16)
            for b in range(TB):
                if b:
                    pool.wait_ge(turned, KD * b)
                nc.gpsimd.dma_start(o[:, :, :, :].rearrange("p t h c -> p t (h c)"),
                                    ov[b].rearrange("p t h c -> p t (h c)")).then_inc(oin, 16)

        @block.sync
        def _(sp):
            for b in range(TB):
                cols = slice(b * BANK, (b + 1) * BANK)
                if b:
                    sp.wait_ge(merged, KD * b)
                sp.dma_start(yraw, g.yt_d.rearrange("(k p) t -> p k t", p=P)[:, :, cols]).then_inc(yin, 16)
                sp.wait_ge(ylo, b + 1)
                for m in range(KD):
                    if m >= 2:
                        sp.wait_ge(merged, KD * b + m - 1)
                    for v in range(2):
                        row = GA + v * D + m * P
                        sp.dma_start(gate[:, m % 2, v], g.zt_d[row:row + P, cols]).then_inc(gin[m % 2], 16)
                    if m >= 1:
                        sp.wait_ge(merged, KD * b + m)
                        sp.dma_start(g.mt_d[(m - 1) * P:m * P, cols], mg[:, (m - 1) % 2]).then_inc(stored[(m - 1) % 2], 16)
                sp.wait_ge(merged, KD * b + KD)
                sp.dma_start(g.mt_d[(KD - 1) * P:KD * P, cols], mg[:, (KD - 1) % 2]).then_inc(stored[(KD - 1) % 2], 16)
            for r in range(2):
                sp.wait_ge(stored[r], 16 * TB * KD // 2)

        @block.scalar
        def _(act):
            for k in range(KW):
                act.wait_ge(wloaded[k % 2], 16 * (k // 2 + 1))
                nc.scalar.copy(wh[:, k, :], raw[:, k % 2]).then_inc(whi, 1)
            for b in range(TB):
                act.wait_ge(mean, b + 1)
                nc.scalar.activation(rs[:, :, :], rs[:, :, :], ACT.Sqrt).then_inc(rooted, 1)
                act.wait_ge(yin, 16 * (b + 1))
                if b:
                    act.wait_ge(made, KD * b)
                nc.scalar.copy(xh[:, KD:, :], yraw).then_inc(yhi, 1)
                for h in range(HEADS):
                    act.wait_ge(turned, KD * b + h + 1)
                    nc.scalar.activation(xh[:, h, :], pst[:, h % 2, :], ACT.Copy, scale=gs[:, 0:1]).then_inc(xhi, 1)

        @block.vector
        def _(dve):
            link = Link(dve, dl)
            link(nc.vector.tensor_scalar(gs[:, :], g.vcol[:, R_GSUB:R_GSUB + 1], 1.0 - LAMBDA_INIT, None, ALU.mult))
            for k in range(KW):
                dve.wait_ge(whi, k + 1)
                nc.vector.tensor_tensor(wl[:, k, :], raw[:, k % 2], wh[:, k, :].bitcast(F32), ALU.subtract).then_inc(wlo, 1)
            for b in range(TB):
                dve.wait_ge(oin, 16 * (b + 1))
                for t in range(TB):
                    link(nc.vector.tensor_tensor(sq[:, :, :], o[:, t], o[:, t], ALU.mult))
                    link(nc.vector.tensor_reduce(rs[:, t, :], sq[:, :, :], AX, ALU.add))
                nc.vector.tensor_scalar(rs[:, :, :], rs[:, :, :], 1.0 / P, EPS, ALU.mult, ALU.add).then_inc(mean, 1)
                dve.wait_ge(rooted, b + 1)
                link(nc.vector.reciprocal(rs[:, :, :], rs[:, :, :]))
                for t in range(TB):
                    ins = nc.vector.tensor_tensor(o[:, t], o[:, t], rs[:, t, :].to_broadcast([P, HEADS, P]), ALU.mult)
                ins.then_inc(normed, 1)
                dve.wait_ge(yhi, b + 1)
                nc.vector.tensor_tensor(xl[:, KD:, :], yraw, xh[:, KD:, :].bitcast(F32), ALU.subtract).then_inc(ylo, 1)
                for h in range(HEADS):
                    dve.wait_ge(xhi, KD * b + h + 1)
                    nc.vector.scalar_tensor_tensor(out=xl[:, h, :], in0=pst[:, h % 2, :], scalar=gs[:, 0:1],
                                                   in1=xh[:, h, :].bitcast(F32), op0=ALU.mult,
                                                   op1=ALU.subtract).then_inc(xlo, 1)
                for m in range(KD):
                    n = KD * b + m
                    dve.wait_ge(made, n + 1)
                    dve.wait_ge(gin[m % 2], 32 * (n // 2 + 1))
                    if n:
                        dve.wait_ge(merged, n)
                    link(nc.vector.tensor_tensor(ma[:, :], psa[:, m % 2, 0, :], gate[:, m % 2, 0], ALU.mult))
                    if n >= 2:
                        dve.wait_ge(stored[m % 2], 16 * (n // 2))
                    link(nc.vector.tensor_tensor(mg[:, m % 2], psa[:, m % 2, 1, :], gate[:, m % 2, 1], ALU.mult))
                    nc.vector.tensor_tensor(mg[:, m % 2], mg[:, m % 2], ma[:, :], ALU.add).then_inc(merged, 1)

        @block.tensor
        def _(pe):
            for b in range(TB):
                pe.wait_ge(normed, b + 1)
                for h in range(HEADS):
                    if KD * b + h >= 2:
                        pe.wait_ge(xlo, KD * b + h - 1)
                    for t in range(TB):
                        ins = nc.tensor.transpose(pst[:, h % 2, t * P:(t + 1) * P], o[:, t, h, :], g.ident[:, :])
                    ins.then_inc(turned, 1)
                pe.wait_ge(xlo, KD * b + KD)
                pe.wait_ge(ylo, b + 1)
                pe.wait_ge(wlo, KW)
                for m in range(KD):
                    n = KD * b + m
                    if n >= 2:
                        pe.wait_ge(merged, n - 1)
                    c = slice(m * P, (m + 1) * P)
                    for v, ks in enumerate((range(KD), range(KD, KW))):
                        for k in ks:
                            out = psa[:, m % 2, v, :]
                            nc.tensor.matmul(out, wh[:, k, c], xh[:, k, :], start=(k == ks[0]), stop=False)
                            nc.tensor.matmul(out, wh[:, k, c], xl[:, k, :], start=False, stop=False)
                            ins = nc.tensor.matmul(out, wl[:, k, c], xh[:, k, :], start=False, stop=(k == ks[-1]))
                    ins.then_inc(made, 1)


def merge(nc, a, g):
    with ExitStack() as ctx:
        sb, ps, sem = allocators(nc, ctx)
        raw = sb("e_raw", [P, 2, D])
        wh = sb("e_wh", [P, KD, D], F32R)
        wl = sb("e_wl", [P, KD, D], F32R)
        wr = sb("e_wr", [P, KD, E])
        br = sb("e_br", [P, E])
        rows = sb("e_rows", [P, 4, D])
        mraw = sb("e_mraw", [P, 2, KD, P])
        mh = sb("e_mh", [P, 2, KD, P], F32R)
        ml = sb("e_ml", [P, 2, KD, P], F32R)
        x = sb("e_x", [P, 2, D])
        u2 = sb("e_u2", [P, 2, D])
        u2t = sb("e_u2t", [P, 2, KD, P])
        junk = sb("e_junk", [P, D])
        rt = sb("e_rt", [P, 2, 2])
        psm = ps("e_psm", [P, 2, 2, BANK])
        pst = ps("e_pst", [P, 2, BANK])
        psr = ps("e_psr", [P, 2, BANK])
        wloaded, whi, wlo, small = [sem("e_w0"), sem("e_w1")], sem("e_whi"), sem("e_wlo"), sem("e_small")
        min_, xin, mhi, mlo = [sem("e_m0"), sem("e_m1")], [sem("e_x0"), sem("e_x1")], sem("e_mhi"), sem("e_mlo")
        made, sq1, mean1, root1, x1_ready = sem("e_made"), sem("e_sq1"), sem("e_mean1"), sem("e_root1"), sem("e_x1r")
        sq2, mean2, root2, u2_ready = sem("e_sq2"), sem("e_mean2"), sem("e_root2"), sem("e_u2r")
        x1st, u2st, turned, u2t_ready = [sem("e_a0"), sem("e_a1")], [sem("e_b0"), sem("e_b1")], sem("e_turn"), sem("e_u2t")
        routed, logit, dl = sem("e_routed"), sem("e_logit"), sem("e_dl")
        block = ctx.enter_context(nc.Block())
        w_out = a.w_out[0].rearrange("(k p) n -> k p n", p=P)
        mt = g.mt_d.rearrange("(k p) t -> p k t", p=P)

        @block.gpsimd
        def _(pool):
            nc.gpsimd.dma_start(wr[:, :, :], a.w_router[0].rearrange("(k p) e -> p k e", p=P)).then_inc(small, 16)
            nc.gpsimd.dma_start(br[:, :], a.b_router.to_broadcast([P, E])).then_inc(small, 16)
            nc.gpsimd.dma_start(rows[:, :, :].rearrange("p n d -> p (n d)"), g.outgain_d).then_inc(small, 16)

            def load(t, r):
                if not early(t, 2):
                    pool.wait_ge(mlo, t - 1)
                    pool.wait_ge(u2_ready, t - 1)
                    pool.wait_ge(x1st[r], (t - r) * 8)
                nc.gpsimd.dma_start(mraw[:, r], mt[:, :, ds(t * P, P)]).then_inc(min_[r], 16)
                nc.gpsimd.dma_start(x[:, r], a.x[0][ds(t * P, P), :]).then_inc(xin[r], 16)

            pipeline(pool, [(load, 0)], NT)

        @block.sync
        def _(sp):
            for k in range(KD):
                if k >= 2:
                    sp.wait_ge(wlo, k - 1)
                sp.dma_start(raw[:, k % 2], w_out[k]).then_inc(wloaded[k % 2], 16)

            def store(t, r):
                sp.wait_ge(x1_ready, t + 1)
                sp.dma_start(g.x1_d[ds(t * P, P), :], x[:, r]).then_inc(x1st[r], 16)
                sp.wait_ge(u2_ready, t + 1)
                sp.dma_start(g.u2_d[ds(t * P, P), :], u2[:, r]).then_inc(u2st[r], 16)

            pipeline(sp, [(store, 0)], NT)
            for r in range(2):
                sp.wait_ge(x1st[r], 8 * NT)
                sp.wait_ge(u2st[r], 8 * NT)

        @block.scalar
        def _(act):
            for k in range(KD):
                act.wait_ge(wloaded[k % 2], 16 * (k // 2 + 1))
                nc.scalar.copy(wh[:, k, :], raw[:, k % 2]).then_inc(whi, 1)

            def high(t, r):
                act.wait_ge(min_[r], (t - r) * 8 + 16)
                if not early(t, 2):
                    act.wait_ge(made, t - 1)
                nc.scalar.copy(mh[:, r], mraw[:, r]).then_inc(mhi, 1)

            def norms(t, r):
                act.wait_ge(made, t + 1)
                if not early(t, 1):
                    act.wait_ge(sq2, t)
                nc.scalar.activation(junk[:, :], psm[:, r].rearrange("p b c -> p (b c)"), ACT.Square,
                                     accum_out=rt[:, r, 0:1]).then_inc(sq1, 1)
                act.wait_ge(mean1, t + 1)
                nc.scalar.activation(rt[:, r, 0:1], rt[:, r, 0:1], ACT.Sqrt).then_inc(root1, 1)
                act.wait_ge(x1_ready, t + 1)
                nc.scalar.activation(junk[:, :], x[:, r], ACT.Square, accum_out=rt[:, r, 1:2]).then_inc(sq2, 1)
                act.wait_ge(mean2, t + 1)
                nc.scalar.activation(rt[:, r, 1:2], rt[:, r, 1:2], ACT.Sqrt).then_inc(root2, 1)

            def columns(t, r):
                for half in range(2):
                    act.wait_ge(turned, t * 2 + (half + 1))
                    if not early(t, 2) and half == 0:
                        act.wait_ge(routed, t - 1)
                    nc.scalar.copy(u2t[:, r, 4 * half:4 * half + 4].rearrange("p k c -> p (k c)"),
                                   pst[:, half, :]).then_inc(u2t_ready, 1)

            pipeline(act, [(high, 0), (columns, 2), (norms, 1)], NT)

        @block.vector
        def _(dve):
            for k in range(KD):
                dve.wait_ge(whi, k + 1)
                nc.vector.tensor_tensor(wl[:, k, :], raw[:, k % 2], wh[:, k, :].bitcast(F32), ALU.subtract).then_inc(wlo, 1)
            dve.wait_ge(small, 48)

            def low(t, r):
                dve.wait_ge(mhi, t + 1)
                nc.vector.tensor_tensor(ml[:, r], mraw[:, r], mh[:, r].bitcast(F32), ALU.subtract).then_inc(mlo, 1)

            def norms(t, r):
                n = [0]

                def link(ins):
                    n[0] += 1
                    ins.then_inc(dl, 1)
                    dve.wait_ge(dl, t * 4 + n[0])

                dve.wait_ge(sq1, t + 1)
                nc.vector.tensor_scalar(rt[:, r, 0:1], rt[:, r, 0:1], 1.0 / D, EPS, ALU.mult, ALU.add).then_inc(mean1, 1)
                dve.wait_ge(root1, t + 1)
                link(nc.vector.reciprocal(rt[:, r, 0:1], rt[:, r, 0:1]))
                if not early(t, 2):
                    dve.wait_ge(u2st[r], (t - r) * 8)
                    dve.wait_ge(turned, t * 2 - 2)
                link(nc.vector.scalar_tensor_tensor(out=u2[:, r], in0=psm[:, r].rearrange("p b c -> p (b c)"),
                                                    scalar=rt[:, r, 0:1], in1=rows[:, 0], op0=ALU.mult, op1=ALU.mult))
                dve.wait_ge(xin[r], (t - r) * 8 + 16)
                nc.vector.tensor_tensor(x[:, r], x[:, r], u2[:, r], ALU.add).then_inc(x1_ready, 1)
                dve.wait_ge(sq2, t + 1)
                nc.vector.tensor_scalar(rt[:, r, 1:2], rt[:, r, 1:2], 1.0 / D, EPS, ALU.mult, ALU.add).then_inc(mean2, 1)
                dve.wait_ge(root2, t + 1)
                link(nc.vector.reciprocal(rt[:, r, 1:2], rt[:, r, 1:2]))
                link(nc.vector.scalar_tensor_tensor(out=u2[:, r], in0=x[:, r], scalar=rt[:, r, 1:2], in1=rows[:, 2],
                                                    op0=ALU.mult, op1=ALU.mult))
                nc.vector.tensor_tensor(u2[:, r], u2[:, r], rows[:, 3], ALU.add).then_inc(u2_ready, 1)

            def logits(t, r):
                dve.wait_ge(routed, t + 1)
                nc.vector.tensor_tensor(g.logits[:, ds(t * E, E)], psr[:, r, 0:E], br[:, :], ALU.add).then_inc(logit, 1)

            pipeline(dve, [(logits, 3), (low, 0), (norms, 1)], NT)

        @block.tensor
        def _(pe):
            pe.wait_ge(wlo, KD)

            def product(t, r):
                pe.wait_ge(mlo, t + 1)
                if not early(t, 2):
                    pe.wait_ge(x1_ready, t - 1)
                for half in range(2):
                    c = slice(half * BANK, (half + 1) * BANK)
                    out = psm[:, r, half, :]
                    for k in range(KD):
                        nc.tensor.matmul(out, mh[:, r, k, :], wh[:, k, c], start=(k == 0), stop=False)
                        nc.tensor.matmul(out, mh[:, r, k, :], wl[:, k, c], start=False, stop=False)
                        ins = nc.tensor.matmul(out, ml[:, r, k, :], wh[:, k, c], start=False, stop=(k == KD - 1))
                ins.then_inc(made, 1)

            def turn(t, r):
                pe.wait_ge(u2_ready, t + 1)
                if not early(t, 1):
                    pe.wait_ge(u2t_ready, t * 2)
                for half in range(2):
                    for k in range(4 * half, 4 * half + 4):
                        ins = nc.tensor.transpose(pst[:, half, (k % 4) * P:(k % 4 + 1) * P],
                                                  u2[:, r, k * P:(k + 1) * P], g.ident[:, :])
                    ins.then_inc(turned, 1)

            def route(t, r):
                pe.wait_ge(u2t_ready, t * 2 + 2)
                if not early(t, 2):
                    pe.wait_ge(logit, t - 1)
                for k in range(KD):
                    ins = nc.tensor.matmul(psr[:, r, 0:E], u2t[:, r, k, :], wr[:, k, :], start=(k == 0), stop=(k == KD - 1))
                ins.then_inc(routed, 1)

            pipeline(pe, [(route, 2), (product, 0), (turn, 1)], NT)


def dispatch(nc, a, g):
    with ExitStack() as ctx:
        sb, ps, sem = allocators(nc, ctx)
        S1 = SLOTS + 1
        C = NT * TOPK
        iota_e = sb("d_iota_e", [P, C, E])
        iota_s = sb("d_iota_s", [P, E, S1])
        before = sb("d_before", [P, P])
        ones = sb("d_ones", [P, P])
        tokid = sb("d_tokid", [P, NT], I32)
        zeros = sb("d_zeros", [P, (SLOTS + 1) * SLOT // P], I32)
        top = sb("d_top", [P, NT, 8])
        index = sb("d_index", [P, NT, 8], U32)
        idx = sb("d_idx", [P, C])
        hot = sb("d_hot", [P, C, E])
        mask = sb("d_mask", [P, NT, E])
        tot = sb("d_tot", [P, NT, E])
        count = sb("d_count", [P, E])
        nblk = sb("d_nblk", [P, E])
        cum = sb("d_cum", [P, 2, E + 16])
        start = sb("d_start", [P, E])
        run = sb("d_run", [P, NT, E])
        prod = sb("d_prod", [P, NT, E])
        posf = sb("d_posf", [P, NT, TOPK])
        ended = sb("d_ended", [P, E, S1])
        begun = sb("d_begun", [P, E, S1])
        slotf = sb("d_slotf", [P, 2, S1])
        cnt = sb("d_cnt", [P, S1])
        tmp4 = sb("d_tmp4", [P, NT, TOPK])
        psum1 = sb("d_psum1", [P, NT])
        psr = ps("d_psr", [P, BANK])
        psn = ps("d_psn", [P, BANK])
        consts, cleared, zeroed, dl, pl = sem("d_consts"), sem("d_clr"), sem("d_zero"), sem("d_dl"), sem("d_pl")
        masked, ranked, powers, diffs = sem("d_masked"), sem("d_ranked"), sem("d_pow"), sem("d_diff")
        placed, scattered = sem("d_placed"), sem("d_scat")
        block = ctx.enter_context(nc.Block())

        @block.sync
        def _(sp):
            sp.wait_ge(cleared, 1)
            sp.dma_start(g.tok_d.rearrange("(p c) o -> p (c o)", p=P), zeros[:, :]).then_inc(zeroed, 16)
            sp.wait_ge(zeroed, 16)

        @block.gpsimd
        def _(pool):
            link = Link(pool, pl)
            nc.gpsimd.memset(zeros[:, :], 0).then_inc(cleared, 1)
            link(nc.gpsimd.iota(iota_e[:, :, :], [[0, C], [1, E]], base=0, channel_multiplier=0,
                                allow_small_or_imprecise_dtypes=True))
            link(nc.gpsimd.iota(iota_s[:, :, :], [[0, E], [1, S1]], base=0, channel_multiplier=0,
                                allow_small_or_imprecise_dtypes=True))
            link(nc.gpsimd.iota(tokid[:, :], [[P, NT]], base=0, channel_multiplier=1))
            link(nc.gpsimd.memset(ones[:, :], 1.0))
            link(nc.gpsimd.affine_select(out=before[:, :], in_=ones[:, :], compare_op=ALU.is_gt, fill=0.0, base=0,
                                         pattern=[[1, P]], channel_multiplier=-1))
            nc.gpsimd.memset(cum[:, :, :], 0.0).then_inc(consts, 1)
            pool.wait_ge(placed, 1)
            pool.wait_ge(zeroed, 16)
            for t in range(NT):
                for k in range(TOPK):
                    c = t * TOPK + k
                    nc.gpsimd.indirect_dma_start(g.tok_d, bass.IndirectOffsetOnAxis(ap=g.pos[:, c:c + 1], axis=0),
                                                 tokid[:, t:t + 1], None).then_inc(scattered, 16)
            pool.wait_ge(scattered, 16 * C)

        @block.tensor
        def _(pe):
            pe.wait_ge(consts, 1)
            pe.wait_ge(masked, 1)
            flat = mask[:, :, :].rearrange("p t e -> p (t e)")
            nc.tensor.matmul(psr[:, :], before[:, :], flat, start=True, stop=True).then_inc(ranked, 1)
            nc.tensor.matmul(psn[:, :], ones[:, :], flat, start=True, stop=True).then_inc(ranked, 1)

        @block.scalar
        def _(act):
            act.wait_ge(diffs, 1)
            nc.scalar.activation(g.prob[:, :, :], g.prob[:, :, :], ACT.Exp).then_inc(powers, 1)

        @block.vector
        def _(dve):
            link = Link(dve, dl)
            logits = g.logits[:, :].rearrange("p (t e) -> p t e", e=E)
            for t in range(NT):
                link(nc.vector.max(top[:, t, :], logits[:, t, :]))
                link(nc.vector.max_index(index[:, t, :], top[:, t, :], logits[:, t, :]))
            nc.vector.tensor_tensor(g.prob[:, :, :], top[:, :, 0:TOPK], top[:, :, 0].to_broadcast([P, NT, TOPK]),
                                    ALU.subtract).then_inc(diffs, 1)
            link(nc.vector.tensor_copy(idx[:, :].rearrange("p (t k) -> p t k", k=TOPK), index[:, :, 0:TOPK]))
            dve.wait_ge(consts, 1)
            link(nc.vector.tensor_tensor(hot[:, :, :], iota_e[:, :, :], idx[:, :].to_broadcast([P, C, E]), ALU.is_equal))
            h4 = hot[:, :, :].rearrange("p (t k) e -> p t k e", k=TOPK)
            link(nc.vector.tensor_tensor(mask[:, :, :], h4[:, :, 0, :], h4[:, :, 1, :], ALU.add))
            link(nc.vector.tensor_tensor(mask[:, :, :], mask[:, :, :], h4[:, :, 2, :], ALU.add))
            nc.vector.tensor_tensor(mask[:, :, :], mask[:, :, :], h4[:, :, 3, :], ALU.add).then_inc(masked, 1)
            dve.wait_ge(powers, 1)
            link(nc.vector.tensor_reduce(psum1[:, :], g.prob[:, :, :], AX, ALU.add))
            link(nc.vector.reciprocal(psum1[:, :], psum1[:, :]))
            link(nc.vector.tensor_tensor(g.prob[:, :, :], g.prob[:, :, :], psum1[:, :].to_broadcast([P, NT, TOPK]), ALU.mult))
            dve.wait_ge(ranked, 2)
            link(nc.vector.tensor_copy(tot[:, :, :].rearrange("p t e -> p (t e)"), psn[:, :]))
            link(nc.vector.tensor_reduce(count[:, :], tot[:, :, :].rearrange("p t e -> p e t"), AX, ALU.add))
            link(nc.vector.tensor_scalar(nblk[:, :], count[:, :], 0.0, None, ALU.is_gt))
            for j in range(1, MAXB):
                link(nc.vector.scalar_tensor_tensor(out=nblk[:, :], in0=count[:, :], scalar=float(j * SLOT), in1=nblk[:, :],
                                                    op0=ALU.is_gt, op1=ALU.add))
            link(nc.vector.tensor_copy(cum[:, 0, 16:], nblk[:, :]))
            n = 0
            for step in (1, 2, 4, 8, 16):
                link(nc.vector.tensor_tensor(cum[:, 1 - n, 16:], cum[:, n, 16:], cum[:, n, 16 - step:16 - step + E], ALU.add))
                n = 1 - n
            cm = cum[:, n, 16:]
            link(nc.vector.tensor_tensor(start[:, :], cm, nblk[:, :], ALU.subtract))
            link(nc.vector.tensor_scalar(run[:, 0, :], start[:, :], float(SLOT), None, ALU.mult))
            for t in range(NT - 1):
                link(nc.vector.tensor_tensor(run[:, t + 1, :], run[:, t, :], tot[:, t, :], ALU.add))
            link(nc.vector.tensor_tensor(run[:, :, :].rearrange("p t e -> p (t e)"), psr[:, :],
                                         run[:, :, :].rearrange("p t e -> p (t e)"), ALU.add))
            for k in range(TOPK):
                link(nc.vector.tensor_tensor(prod[:, :, :], h4[:, :, k, :], run[:, :, :], ALU.mult))
                link(nc.vector.tensor_reduce(posf[:, :, k], prod[:, :, :], AX, ALU.add))
            nc.vector.tensor_copy(g.pos[:, :], posf[:, :, :].rearrange("p t k -> p (t k)")).then_inc(placed, 1)
            link(nc.vector.tensor_tensor(ended[:, :, :], iota_s[:, :, :], cm.to_broadcast([P, E, S1]), ALU.is_ge))
            link(nc.vector.tensor_tensor(begun[:, :, :], iota_s[:, :, :], start[:, :].to_broadcast([P, E, S1]), ALU.is_ge))
            link(nc.vector.tensor_tensor(begun[:, :, :], begun[:, :, :], ended[:, :, :], ALU.subtract))
            link(nc.vector.tensor_reduce(slotf[:, 0, :], ended[:, :, :].rearrange("p e s -> p s e"), AX, ALU.add))
            link(nc.vector.tensor_scalar(slotf[:, 0, :], slotf[:, 0, :], float(E - 1), None, ALU.min))
            link(nc.vector.scalar_tensor_tensor(out=count[:, :], in0=start[:, :], scalar=float(SLOT), in1=count[:, :],
                                                op0=ALU.mult, op1=ALU.add))
            link(nc.vector.tensor_tensor(begun[:, :, :], begun[:, :, :], count[:, :].to_broadcast([P, E, S1]), ALU.mult))
            link(nc.vector.tensor_reduce(cnt[:, :], begun[:, :, :].rearrange("p e s -> p s e"), AX, ALU.add))
            link(nc.vector.scalar_tensor_tensor(out=cnt[:, :], in0=iota_s[:, 0, :], scalar=-float(SLOT), in1=cnt[:, :],
                                                op0=ALU.mult, op1=ALU.add))
            link(nc.vector.tensor_scalar(slotf[:, 1, :], cnt[:, :], 0.0, None, ALU.is_gt))
            for j in range(1, JT):
                link(nc.vector.scalar_tensor_tensor(out=slotf[:, 1, :], in0=cnt[:, :], scalar=float(j * P),
                                                    in1=slotf[:, 1, :], op0=ALU.is_gt, op1=ALU.add))
            link(nc.vector.tensor_copy(g.table[:, :], slotf[:, :, :].rearrange("p n s -> p (n s)")))


def experts(nc, a, g):
    with ExitStack() as ctx:
        sb, ps, sem = allocators(nc, ctx)
        CH = 6
        PIECES = 2 * CH
        RAW = 2
        raw = sb("x_raw", [P, RAW, KD, BANK])
        wh = [sb(f"x_wh{i}", [P, KD, BANK], F32R) for i in range(2)]
        wl = [sb(f"x_wl{i}", [P, KD, BANK], F32R) for i in range(2)]
        xg = sb("x_xg", [P, JT, D])
        xh = sb("x_xh", [P, KD, SLOT], F32R)
        xl = sb("x_xl", [P, KD, SLOT], F32R)
        ah = sb("x_ah", [P, KD, SLOT], F32R)
        al = sb("x_al", [P, KD, SLOT], F32R)
        gt = sb("x_gt", [P, SLOT])
        ut = sb("x_ut", [P, SLOT])
        sg = sb("x_sg", [P, SLOT])
        y = sb("x_y", [P, JT, D])
        bd = sb("x_bd", [P, D])
        ball = sb("x_ball", [P, BANK])
        bias = sb("x_bias", [P, 2 * KD])
        tok = sb("x_tok", [P, JT], I32)
        psg = ps("x_psg", [P, 4, BANK])
        pst = ps("x_pst", [P, 4, BANK])
        wloaded = [sem(f"x_w{i}") for i in range(RAW)]
        whi, wlo, bin_, bdin, tokin = sem("x_whi"), sem("x_wlo"), sem("x_bin"), sem("x_bdin"), sem("x_tokin")
        tokseen, filled = sem("x_tokseen"), sem("x_filled")
        xin, turned, xhi, xlo = sem("x_in"), sem("x_turn"), sem("x_xhi"), sem("x_xlo")
        made, gated, sig, acted, ahi, alo = sem("x_made"), sem("x_gated"), sem("x_sig"), sem("x_acted"), sem("x_ahi"), sem("x_alo")
        down, yout, stored, yfree, dl = sem("x_down"), sem("x_yout"), sem("x_stored"), sem("x_yfree"), sem("x_dl")
        block = ctx.enter_context(nc.Block())
        wgu = a.w_gate_up[0].rearrange("e (k p) n -> e p k n", p=P)
        wdn = a.w_down[0].rearrange("e (k p) n -> e p k n", p=P)
        tokv = g.tok_d.rearrange("(s j p) o -> s p (j o)", j=JT, p=P)
        yv = g.y_d.rearrange("(s j p) d -> s p j d", j=JT, p=P)
        H = D // 2
        LEAST = T * TOPK // SLOT

        def tiles(eng, s):
            return eng.value_load(g.table[0:1, ds(s + (SLOTS + 1), 1)], min_val=0, max_val=JT)

        def slots(eng, body, first=0):
            with eng.Fori(first, SLOTS) as s:
                n = tiles(eng, s)
                with eng.If(n > 0):
                    body(s, n, None if eng == nc.sync else tiles(eng, s + 1))

        def loaded_piece(i):
            chunk = raw[:, i // 2 % RAW]
            if i < KD:
                return chunk.rearrange("p k (v h c) -> p k v h c", v=2, h=2)[:, :, :, i % 2, :]
            return chunk[:, :, i % 2 * COLS:(i % 2 + 1) * COLS]

        def split_piece(part, i):
            place = part[i // 2 % 2][:, :, i % 2 * COLS:(i % 2 + 1) * COLS]
            return place.rearrange("p k (v c) -> p k v c", v=2) if i < KD else place

        def by_tiles(eng, n, body):
            for v in range(1, JT + 1):
                with eng.If(n == v):
                    body(v)

        def bank(v, half, j):
            return 3 if half and j == v - 1 else j

        @block.sync
        def _(sp):
            sp.dma_start(ball[:, :], g.bcol_d).then_inc(bin_, 16)

            def body(s, n, after):
                e = sp.value_load(g.table[0:1, ds(s, 1)], min_val=0, max_val=E - 1)
                for c in range(CH):
                    sp.wait_ge(wlo, s * PIECES + (2 * c + 2))
                    r = c % RAW
                    if c < 4:
                        for v in range(2):
                            lo = v * FF + c * COLS
                            sp.dma_start(raw[:, r, :, v * COLS:(v + 1) * COLS],
                                         wgu[ds(e, 1), :, :, lo:lo + COLS].rearrange("e p k n -> p (e k) n")).then_inc(wloaded[r], 16)
                    else:
                        for v in range(2):
                            k0 = v * KD // 2
                            sp.dma_start(raw[:, r, k0:k0 + KD // 2, :],
                                         wdn[ds(e, 1), :, k0:k0 + KD // 2, (c - 4) * BANK:(c - 3) * BANK]
                                         .rearrange("e p k n -> p (e k) n")).then_inc(wloaded[r], 16)
                    if c == 3:
                        sp.wait_ge(yout, s * 8 + 5)
                        sp.dma_start(bd[:, :], a.b_down[0][ds(e, 1), :].to_broadcast([P, D])).then_inc(bdin, 16)

            def fill(s):
                for q in range(2):
                    far = s * 2 + (LEAST + q)
                    with sp.If(tiles(sp, far) > 0):
                        sp.sem_inc(filled, 16)
                    with sp.Else():
                        sp.dma_start(g.y_d[ds(far * SLOT, SLOT), :], g.u2_d[0:SLOT, :]).then_inc(filled, 16)

            with sp.Fori(0, LEAST) as s:
                body(s, None, None)
                fill(s)
            slots(sp, body, LEAST)
            sp.wait_ge(filled, 16 * 2 * LEAST)

        @block.gpsimd
        def _(pool):
            def gather(s):
                with nc.allow_non_contiguous_dma(reason="a slot's token numbers, one to a partition"):
                    nc.gpsimd.dma_start(tok[:, :], tokv[ds(s, 1)].rearrange("s p j -> p (s j)")).then_inc(tokin, 16)
                pool.wait_ge(tokin, s * 16 + 16)
                pool.sem_inc(tokseen, 1)
                for j in range(JT):
                    nc.gpsimd.indirect_dma_start(xg[:, j, :], None, g.u2_d,
                                                 bass.IndirectOffsetOnAxis(ap=tok[:, j:j + 1], axis=0)).then_inc(xin, 16)
                pool.wait_ge(xin, s * 64 + 64)

            gather(0)

            def body(s, n, after):
                with pool.If(after > 0):
                    pool.wait_ge(turned, s * KD + KD)
                    gather(s + 1)
                for half in range(2):
                    pool.wait_ge(yout, s * 8 + (4 * half + 9))
                    nc.gpsimd.dma_start(yv[ds(s, 1), :, :, half * H:(half + 1) * H].rearrange("s p j d -> p (s j) d"),
                                        y[:, :, half * H:(half + 1) * H]).then_inc(stored, 16)
                    pool.wait_ge(stored, s * 32 + (16 * half + 16))
                    pool.sem_inc(yfree, 1)

            slots(pool, body)

        @block.scalar
        def _(act):
            def split(s, i):
                c = i // 2
                act.wait_ge(wloaded[c % RAW], s * (32 * CH // RAW) + (32 * (c // RAW) + 32))
                nc.scalar.copy(split_piece(wh, i), loaded_piece(i)).then_inc(whi, 1)

            def rows(s, part, v):
                for k in range(4 * part, 4 * part + 4):
                    act.wait_ge(turned, s * KD + (k + 1))
                    nc.scalar.copy(xh[:, k, 0:v * P], pst[:, k % 4, 0:v * P]).then_inc(xhi, 1)

            act.sem_inc(xlo, 4)
            act.sem_inc(yout, 5)
            act.sem_inc(yfree, 2)
            for i in range(4):
                split(0, i)
            rows(0, 0, JT)
            rows(0, 1, JT)

            def body(s, n, after):
                def version(v):
                    w = v * P
                    for f in range(KD):
                        act.wait_ge(gated, s * 16 + (2 * f + 1))
                        nc.scalar.activation(sg[:, 0:w], gt[:, 0:w], ACT.Sigmoid, scale=ALPHA).then_inc(sig, 1)
                        if f < KD - 1:
                            split(s, f + 4)
                        act.wait_ge(acted, s * KD + (f + 1))
                        nc.scalar.copy(ah[:, f, 0:w], ut[:, 0:w]).then_inc(ahi, 1)
                    split(s, PIECES - 1)

                by_tiles(act, n, version)

                def following(v):
                    rows(s + 1, 0, v)
                    rows(s + 1, 1, v)
                    for half in range(2):
                        act.wait_ge(down, s * 8 + (4 * half + 4))
                        split(s + 1, 2 * half)
                        split(s + 1, 2 * half + 1)

                by_tiles(act, after, following)

            slots(act, body)

        @block.vector
        def _(dve):
            def split(s, i):
                dve.wait_ge(whi, s * PIECES + (i + 1))
                nc.vector.tensor_tensor(split_piece(wl, i), loaded_piece(i), split_piece(wh, i).bitcast(F32),
                                        ALU.subtract).then_inc(wlo, 1)

            def rows(s, part, v):
                w = v * P
                for k in range(4 * part, 4 * part + 4):
                    dve.wait_ge(xhi, s * KD + (k + 1))
                    nc.vector.tensor_tensor(xl[:, k, 0:w], pst[:, k % 4, 0:w], xh[:, k, 0:w].bitcast(F32),
                                            ALU.subtract).then_inc(xlo, 1)

            nc.vector.memset(y[:, :, :], 0.0).then_inc(dl, 1)
            dve.sem_inc(wlo, 4)
            dve.wait_ge(bin_, 16)
            for i in range(3):
                split(0, i)
            rows(0, 0, JT)
            rows(0, 1, JT)

            def body(s, n, after):
                e = dve.value_load(g.table[0:1, ds(s, 1)], min_val=0, max_val=E - 1)
                DL = KD + 1
                dve.wait_ge(alo, s * KD + 1)
                nc.vector.tensor_copy(bias[:, :], ball[:, ds(e * (2 * KD), 2 * KD)]).then_inc(dl, 1)

                def version(v):
                    w = v * P
                    dve.wait_ge(dl, s * DL + 2)
                    for f in range(KD):
                        dve.wait_ge(made, s * KD + (f + 1))
                        dve.wait_ge(alo, s * KD + (f + 1))
                        pair = 2 * (f % 2)
                        nc.vector.tensor_scalar(gt[:, 0:w], psg[:, pair, 0:w], bias[:, f:f + 1], LIMIT,
                                                ALU.add, ALU.min).then_inc(gated, 1)
                        nc.vector.tensor_scalar(ut[:, 0:w], psg[:, pair + 1, 0:w], bias[:, KD + f:KD + f + 1], LIMIT + 1,
                                                ALU.add, ALU.min).then_inc(gated, 1)
                        if f < KD - 1:
                            split(s, f + 3)
                        dve.wait_ge(sig, s * KD + (f + 1))
                        dve.wait_ge(gated, s * 16 + (2 * f + 2))
                        nc.vector.tensor_tensor(gt[:, 0:w], gt[:, 0:w], sg[:, 0:w], ALU.mult).then_inc(dl, 1)
                        dve.wait_ge(dl, s * DL + (f + 3))
                        nc.vector.scalar_tensor_tensor(out=ut[:, 0:w], in0=ut[:, 0:w], scalar=1.0 - LIMIT, in1=gt[:, 0:w],
                                                       op0=ALU.max, op1=ALU.mult).then_inc(acted, 1)
                        dve.wait_ge(ahi, s * KD + (f + 1))
                        nc.vector.tensor_tensor(al[:, f, 0:w], ut[:, 0:w], ah[:, f, 0:w].bitcast(F32),
                                                ALU.subtract).then_inc(alo, 1)

                by_tiles(dve, n, version)
                split(s, PIECES - 2)
                by_tiles(dve, after, lambda v: rows(s + 1, 0, v))
                split(s, PIECES - 1)
                for half in range(2):
                    def outputs(v):
                        dve.wait_ge(bdin, s * 16 + 16)
                        dve.wait_ge(yfree, s * 2 + (half + 1))
                        for j in range(v):
                            dve.wait_ge(down, s * 8 + (4 * half + j + 1))
                            nc.vector.tensor_tensor(y[:, j, half * H:(half + 1) * H], psg[:, bank(v, half, j), :], bd[:, half * H:(half + 1) * H],
                                                    ALU.add).then_inc(yout, 1 if j < v - 1 else JT + 1 - v)

                    by_tiles(dve, n, outputs)
                    if half == 0:
                        by_tiles(dve, after, lambda v: rows(s + 1, 1, v))
                    with dve.If(after > 0):
                        split(s + 1, half)
                        if half:
                            split(s + 1, 2)

            dve.sem_inc(alo, 1)
            slots(dve, body)

        @block.tensor
        def _(pe):
            def turn(s, part, v):
                pe.wait_ge(xin, s * 64 + 64)
                for k in range(4 * part, 4 * part + 4):
                    pe.wait_ge(xlo, s * KD + (k + 1))
                    for j in range(v):
                        ins = nc.tensor.transpose(pst[:, k % 4, j * P:(j + 1) * P], xg[:, j, k * P:(k + 1) * P], g.ident[:, :])
                    ins.then_inc(turned, 1)

            turn(0, 0, JT)
            turn(0, 1, JT)

            def body(s, n, after):
                pe.wait_ge(xlo, s * KD + (KD + 4))
                pe.wait_ge(yout, s * 8 + 5)

                def version(v):
                    w = max(v, 2) * P
                    for f in range(KD):
                        c = f // 2
                        pe.wait_ge(wlo, s * PIECES + (f + 5))
                        if f >= 2:
                            pe.wait_ge(gated, s * 16 + (2 * f - 2))
                        for u in range(2):
                            col = slice((f % 2) * COLS + u * P, (f % 2) * COLS + (u + 1) * P)
                            out = psg[:, 2 * (f % 2) + u, 0:w]
                            for k in range(KD):
                                nc.tensor.matmul(out, wh[c % 2][:, k, col], xh[:, k, 0:w], start=(k == 0), stop=False)
                                nc.tensor.matmul(out, wh[c % 2][:, k, col], xl[:, k, 0:w], start=False, stop=False)
                                ins = nc.tensor.matmul(out, wl[c % 2][:, k, col], xh[:, k, 0:w], start=False,
                                                       stop=(k == KD - 1))
                        ins.then_inc(made, 1)

                by_tiles(pe, n, version)
                for half in range(2):
                    by_tiles(pe, after, lambda v: turn(s + 1, half, v))

                    def outputs(v):
                        pe.wait_ge(wlo, s * PIECES + (KD + 2 * half + 6))
                        for j in range(v):
                            if half:
                                pe.wait_ge(yout, s * 8 + (min(bank(v, half, j), v - 1) + 6))
                            out = psg[:, bank(v, half, j), :]
                            t = slice(j * P, (j + 1) * P)
                            for k in range(KD):
                                if half == 0 and j == 0:
                                    pe.wait_ge(alo, s * KD + (k + 2))
                                nc.tensor.matmul(out, ah[:, k, t], wh[half][:, k, :], start=(k == 0), stop=False)
                                nc.tensor.matmul(out, ah[:, k, t], wl[half][:, k, :], start=False, stop=False)
                                ins = nc.tensor.matmul(out, al[:, k, t], wh[half][:, k, :], start=False,
                                                       stop=(k == KD - 1))
                            ins.then_inc(down, 1 if j < v - 1 else JT + 1 - v)

                    by_tiles(pe, n, outputs)

            slots(pe, body)


def combine(nc, a, g, out):
    with ExitStack() as ctx:
        sb, ps, sem = allocators(nc, ctx)
        yg = sb("c_y", [P, 2, TOPK, D])
        x1 = sb("c_x1", [P, 2, D])
        row = sb("c_row", [P, D])
        f = sb("c_f", [P, D])
        junk = sb("c_junk", [P, D])
        res = sb("c_res", [P, 2, D])
        rt = sb("c_rt", [P, 2, 1])
        small, yin, xin, dl = sem("c_small"), [sem("c_y0"), sem("c_y1")], [sem("c_x0"), sem("c_x1")], sem("c_dl")
        summed, sq, mean, root, done = sem("c_sum"), sem("c_sq"), sem("c_mean"), sem("c_root"), sem("c_done")
        stored = [sem("c_s0"), sem("c_s1")]
        block = ctx.enter_context(nc.Block())
        od = out[0]

        @block.gpsimd
        def _(pool):
            for t in range(NT):
                r = t % 2
                if t >= 2:
                    pool.wait_ge(done, t - 1)
                for k in range(TOPK):
                    nc.gpsimd.indirect_dma_start(yg[:, r, k, :], None, g.y_d,
                                                 bass.IndirectOffsetOnAxis(ap=g.pos[:, t * TOPK + k:t * TOPK + k + 1], axis=0)
                                                 ).then_inc(yin[r], 16)

        @block.sync
        def _(sp):
            sp.dma_start(row[:, :], g.outgain_d[:, D:2 * D]).then_inc(small, 16)

            def load(t, r):
                if not early(t, 2):
                    sp.wait_ge(done, t - 1)
                sp.dma_start(x1[:, r], g.x1_d[ds(t * P, P), :]).then_inc(xin[r], 16)

            def store(t, r):
                sp.wait_ge(done, t + 1)
                sp.dma_start(od[ds(t * P, P), :], res[:, r]).then_inc(stored[r], 16)

            pipeline(sp, [(load, 0), (store, 1)], NT)
            for r in range(2):
                sp.wait_ge(stored[r], 8 * NT)

        @block.scalar
        def _(act):
            def body(t, r):
                act.wait_ge(summed, t + 1)
                nc.scalar.activation(junk[:, :], f[:, :], ACT.Square, accum_out=rt[:, r, :]).then_inc(sq, 1)
                act.wait_ge(mean, t + 1)
                nc.scalar.activation(rt[:, r, :], rt[:, r, :], ACT.Sqrt).then_inc(root, 1)

            pipeline(act, [(body, 0)], NT)

        @block.vector
        def _(dve):
            dve.wait_ge(small, 16)

            def body(t, r):
                L = TOPK + 1
                n = [0]

                def link(ins):
                    n[0] += 1
                    ins.then_inc(dl, 1)
                    dve.wait_ge(dl, t * L + n[0])

                dve.wait_ge(yin[r], (t - r) * 32 + 64)
                link(nc.vector.tensor_scalar(f[:, :], yg[:, r, 0, :], g.prob[:, ds(t, 1), 0:1].rearrange("p a b -> p (a b)"),
                                             None, ALU.mult))
                for k in range(1, TOPK):
                    ins = nc.vector.scalar_tensor_tensor(out=f[:, :], in0=yg[:, r, k, :],
                                                         scalar=g.prob[:, ds(t, 1), k:k + 1].rearrange("p a b -> p (a b)"),
                                                         in1=f[:, :], op0=ALU.mult, op1=ALU.add)
                    if k < TOPK - 1:
                        link(ins)
                ins.then_inc(summed, 1)
                dve.wait_ge(sq, t + 1)
                nc.vector.tensor_scalar(rt[:, r, :], rt[:, r, :], 1.0 / D, EPS, ALU.mult, ALU.add).then_inc(mean, 1)
                dve.wait_ge(root, t + 1)
                link(nc.vector.reciprocal(rt[:, r, :], rt[:, r, :]))
                link(nc.vector.scalar_tensor_tensor(out=f[:, :], in0=f[:, :], scalar=rt[:, r, :], in1=row[:, :],
                                                    op0=ALU.mult, op1=ALU.mult))
                dve.wait_ge(xin[r], (t - r) * 8 + 16)
                if not early(t, 2):
                    dve.wait_ge(stored[r], (t - r) * 8)
                nc.vector.tensor_tensor(res[:, r], x1[:, r], f[:, :], ALU.add).then_inc(done, 1)
                dve.wait_ge(done, t + 1)

            pipeline(dve, [(body, 0)], NT)


def build(nc, a, out):
    with ExitStack() as ctx:
        g = Shared()
        sb, ps, sem = allocators(nc, ctx)

        def dram(name, shape, dt=F32):
            return nc.dram_tensor(name, shape, dt).ap()

        g.outgain_d = dram("outgain_d", [P, 4 * D])
        g.bcol_d = dram("bcol_d", [P, BANK])
        g.zt_d = dram("zt_d", [IN_W, T])
        g.yt_d = dram("yt_d", [PG * P, T])
        g.o_d = dram("o_d", [T, VW])
        g.mt_d = dram("mt_d", [D, T])
        g.x1_d = dram("x1_d", [T, D])
        g.u2_d = dram("u2_d", [T, D])
        g.tok_d = dram("tok_d", [(SLOTS + 1) * SLOT, 1], I32)
        g.y_d = dram("y_d", [(SLOTS + 1) * SLOT, D])
        g.v_d = dram("v_d", [T, VW])
        g.ident = sb("ident", [P, P])
        g.vcol = sb("vcol", [P, P])
        g.neglam = sb("neglam", [P, 1])
        g.shift = sb("shift", [P, 2, KD])
        g.gain = sb("gain", [P, 2, KD])
        with ExitStack() as mixing:
            esb = allocators(nc, mixing)[0]
            g.rot = esb("rot_t", [P, 2, T])
            modulate(nc, a, g)
            g.uth = esb("uth", [P, KD, T], F32R)
            g.utl = esb("utl", [P, KD, T], F32R)
            normalise(nc, a, g)
            project(nc, a, g)
        pool_mix(nc, a, g)
        attend(nc, a, g)
        branches(nc, a, g)
        g.prob = sb("prob", [P, NT, TOPK])
        g.pos = sb("pos", [P, NT * TOPK], I32)
        g.table = sb("table", [P, 2 * (SLOTS + 1)], I32)
        with ExitStack() as routing:
            g.logits = allocators(nc, routing)[0]("logits", [P, NT * E])
            merge(nc, a, g)
            dispatch(nc, a, g)
        experts(nc, a, g)
        combine(nc, a, g, out)


_INS = ["x", "c", "positions", "w_mod", "b_mod", "g_pre_mix", "w_in", "lambda_q1", "lambda_k1", "lambda_q2",
        "lambda_k2", "g_sub", "w_pool_group", "pool_scale", "w_att_branch", "w_pool_branch", "w_out", "g_post_mix",
        "g_pre_ffn", "w_router", "b_router", "w_gate_up", "b_gate_up", "w_down", "b_down", "g_post_ffn"]


def kernel(**inputs):
    import numpy as _np
    import concourse.bacc as _bacc
    from concourse import mybir as _mybir
    from concourse.bass_utils import run_bass_kernel_spmd as _run

    nc = _bacc.Bacc("TRN2", target_bir_lowering=False, num_devices=1)
    arrays, aps = {}, {}
    for name in _INS:
        arr = _np.ascontiguousarray(inputs[name])
        arrays[f"in_{name}"] = arr
        aps[name] = nc.dram_tensor(f"in_{name}", arr.shape, _mybir.dt.from_np(arr.dtype), kind="ExternalInput").ap()
    out = nc.dram_tensor("out_dram", (1, T, D), _mybir.dt.float32, kind="ExternalOutput").ap()
    build(nc, Inputs(aps), out)
    r = _run(nc, [arrays], core_ids=[0])
    return r.results[0]["out_dram"]
```

```python
import math
from contextlib import ExitStack

import concourse.bass as bass
from concourse import mybir
import numpy as np

F32 = mybir.dt.float32
F32R = mybir.dt.float32r
BF16 = mybir.dt.bfloat16
I32 = mybir.dt.int32
U32 = mybir.dt.uint32
ALU = mybir.AluOpType
ACT = mybir.ActivationFunctionType
AX = mybir.AxisListType.X
ds = bass.ds

P = 128
D = 1024
KD = D // P
T = 2048
NT = T // P
BANK = 512
EPS = 1e-6
HEADS = 8
HD = 64
CHUNK = 64
ROPE = HD // 4
HALF = ROPE // 2
THETA = 500000.0
QKW = HEADS * 2 * HD
VW = HEADS * 2 * HD
PG = 4
WINDOWS = (2, 4, 8, 16)
IN_W = 2 * QKW + VW + PG * P + 2 * D
NB_IN = IN_W // BANK
E = 32
TOPK = 4
FF = D
LIMIT = 7.0
ALPHA = 1.702
LAMBDA_INIT = 0.8 - 0.6 * math.exp(-0.3 * 0)
SLOT = 512
JT = SLOT // P
SLOTS = T * TOPK // SLOT + E - 1
MAXB = T // SLOT
NEG = -1e30


class Shared:
    pass


class Inputs:

    def __init__(self, by_name):
        self.x = by_name["x"]
        self.c = by_name["c"]
        self.positions = by_name["positions"]
        self.w_mod = by_name["w_mod"]
        self.b_mod = by_name["b_mod"]
        self.g_pre_mix = by_name["g_pre_mix"]
        self.w_in = by_name["w_in"]
        self.lambda_q1 = by_name["lambda_q1"]
        self.lambda_k1 = by_name["lambda_k1"]
        self.lambda_q2 = by_name["lambda_q2"]
        self.lambda_k2 = by_name["lambda_k2"]
        self.g_sub = by_name["g_sub"]
        self.w_pool_group = by_name["w_pool_group"]
        self.pool_scale = by_name["pool_scale"]
        self.w_att_branch = by_name["w_att_branch"]
        self.w_pool_branch = by_name["w_pool_branch"]
        self.w_out = by_name["w_out"]
        self.g_post_mix = by_name["g_post_mix"]
        self.g_pre_ffn = by_name["g_pre_ffn"]
        self.w_router = by_name["w_router"]
        self.b_router = by_name["b_router"]
        self.w_gate_up = by_name["w_gate_up"]
        self.b_gate_up = by_name["b_gate_up"]
        self.w_down = by_name["w_down"]
        self.b_down = by_name["b_down"]
        self.g_post_ffn = by_name["g_post_ffn"]


class Link:

    def __init__(self, eng, sem, base=0):
        self.eng, self.sem, self.n, self.base = eng, sem, 0, base

    def __call__(self, ins):
        ins.then_inc(self.sem, 1)
        self.n += 1
        self.eng.wait_ge(self.sem, self.base + self.n)


def allocators(nc, ctx):
    def sb(name, shape, dt=F32):
        return ctx.enter_context(nc.sbuf_tensor(name, shape, dt))

    def ps(name, shape, dt=F32):
        return ctx.enter_context(nc.psum_tensor(name, shape, dt))

    sems = []

    def sem(name):
        sems.append(nc.alloc_semaphore(name))
        return sems[-1]

    def clear():
        if sems:
            nc.clear_and_free_semaphores(sems)
            nc.all_engine_barrier()

    ctx.callback(clear)
    return sb, ps, sem


R_BMOD, R_GPRE, R_GPOST, R_GFPRE, R_GFPOST, R_GSUB, R_PSC, R_C = 0, 48, 56, 64, 72, 80, 81, 85


def modulate(nc, a, g):
    with ExitStack() as ctx:
        sb, ps, sem = allocators(nc, ctx)
        RING = 3
        NCH = 6 * D // BANK
        wm = sb("wm", [P, RING, KD, BANK])
        vrow = sb("vrow", [P, P])
        bcol = sb("bcol", [P, BANK])
        brow = sb("brow", [P, 4, P])
        lamv = sb("lamv", [1, 4, HD])
        lprod = sb("lprod", [1, 2, HD])
        lsum = sb("lsum", [1, 4])
        ones1 = sb("ones1", [1, P])
        csil = sb("csil", [P, KD])
        mod = sb("mod", [P, 6 * KD])
        modrow = sb("modrow", [1, 6 * D])
        outgain = sb("outgain", [1, 4, D])
        gcol = sb("gcol", [P, 4, KD])
        posi = sb("posi", [P, NT], I32)
        rot = sb("rot", [P, NT, 2, P])
        sinv = sb("sinv", [P, NT, HALF])
        cosv = sb("cosv", [P, NT, HALF])
        posf = sb("posf", [P, NT])
        ang = sb("ang", [P, NT, HALF])
        kk = sb("kk", [P, 2, NT, HALF])
        tmp = sb("tmp", [P, NT, HALF])
        rsin = sb("rsin", [P, NT, HALF])
        rcos = sb("rcos", [P, NT, HALF])
        psv = ps("psv", [P, BANK])
        psm = ps("psm", [P, BANK])
        psb = ps("psb", [P, BANK])
        psl = ps("psl", [P, BANK])
        psr = ps("psr", [P, 2, BANK])
        psw = ps("psw", [P, 2, BANK])
        zeroed, loaded, wloaded = sem("m_zeroed"), sem("m_loaded"), [sem(f"m_w{i}") for i in range(RING)]
        wused, consts, vcols, vready = sem("m_wused"), sem("m_consts"), sem("m_vcols"), sem("m_vready")
        sig, csil_ready, mod_ready = sem("m_sig"), sem("m_csil"), sem("m_mod")
        dlink, plink = sem("m_dlink"), sem("m_plink")
        lam_sum, lam_exp, lam_one, lam_ps = sem("m_ls"), sem("m_le"), sem("m_lone"), sem("m_lps")
        bps, gains_ready, gain_ps, trig, sines = sem("m_bps"), sem("m_gr"), sem("m_gps"), sem("m_trig"), sem("m_sines")
        bias_done, row_out, cols_ready = sem("m_bd"), sem("m_rowout"), sem("m_cols")
        gain_out, kept = sem("m_go"), sem("m_kept")
        rot_set, rot_ready, rot_ps, rot_copied = sem("m_rset"), sem("m_rr"), sem("m_rps"), sem("m_rc")
        block = ctx.enter_context(nc.Block())
        w_mod = a.w_mod[0].rearrange("(k p) n -> p k n", p=P)

        @block.sync
        def _(sp):
            sp.wait_ge(zeroed, 1)
            for row, src in ((R_BMOD, a.b_mod.rearrange("a (r c) -> (a r) c", c=P)),
                             (R_GPRE, a.g_pre_mix.rearrange("a (r c) -> (a r) c", c=P)),
                             (R_GPOST, a.g_post_mix.rearrange("a (r c) -> (a r) c", c=P)),
                             (R_GFPRE, a.g_pre_ffn.rearrange("a (r c) -> (a r) c", c=P)),
                             (R_GFPOST, a.g_post_ffn.rearrange("a (r c) -> (a r) c", c=P)),
                             (R_GSUB, a.g_sub),
                             (R_PSC, a.pool_scale.rearrange("a (r c) -> (a r) c", c=P)),
                             (R_C, a.c.rearrange("a (r c) -> (a r) c", c=P))):
                sp.dma_start(vrow[row:row + src.shape[0], :], src).then_inc(loaded, 16)
            for i, v in enumerate((a.lambda_q1, a.lambda_q2, a.lambda_k1, a.lambda_k2)):
                sp.dma_start(lamv[0:1, i, :], v).then_inc(loaded, 16)
            with nc.allow_non_contiguous_dma(reason="positions to columns"):
                sp.dma_start(posi[:, :], a.positions.rearrange("a (t p) -> p (a t)", p=P)).then_inc(loaded, 16)
            sp.dma_start(brow[:, :, :], a.b_gate_up[0].rearrange("e (f c) -> (e f) c", c=P)
                         .rearrange("(g r) c -> r g c", r=P)).then_inc(loaded, 16)
            for j in range(NCH):
                if j >= RING:
                    sp.wait_ge(wused, j - RING + 1)
                sp.dma_start(wm[:, j % RING], w_mod[:, :, j * BANK:(j + 1) * BANK]).then_inc(wloaded[j % RING], 16)
            sp.wait_ge(gain_out, 4)
            sp.dma_start(g.outgain_d, outgain[0:1, :, :].rearrange("p n d -> p (n d)")).then_inc(kept, 16)
            sp.wait_ge(bias_done, 1)
            sp.dma_start(g.bcol_d, bcol[:, :]).then_inc(kept, 16)
            sp.wait_ge(kept, 32)

        @block.gpsimd
        def _(pool):
            link = Link(pool, plink)
            nc.gpsimd.memset(vrow[:, :], 0.0).then_inc(zeroed, 1)
            link(nc.gpsimd.memset(g.ident[:, :], 0.0))
            link(nc.gpsimd.affine_select(out=g.ident[:, :], in_=g.ident[:, :], compare_op=ALU.not_equal, fill=1.0,
                                         base=0, pattern=[[-1, P]], channel_multiplier=1))
            nc.gpsimd.memset(ones1[:, :], 1.0).then_inc(consts, 1)
            nc.gpsimd.memset(rot[:, :, 0, :], 1.0)
            nc.gpsimd.memset(rot[:, :, 1, :], 0.0).then_inc(rot_set, 1)

        @block.tensor
        def _(pe):
            pe.wait_ge(consts, 1)
            pe.wait_ge(loaded, 16 * 14)
            nc.tensor.transpose(psv[:, 0:P], vrow[:, :], g.ident[:, :]).then_inc(vcols, 1)
            for q in range(4):
                last = nc.tensor.transpose(psb[:, q * P:(q + 1) * P], brow[:, q, :], g.ident[:, :])
            last.then_inc(bps, 1)
            pe.wait_ge(csil_ready, 1)
            for j in range(NCH):
                pe.wait_ge(wloaded[j % RING], 16 * (j // RING + 1))
                if j >= 2:
                    pe.wait_ge(row_out, j - 1)
                for k in range(KD):
                    last = nc.tensor.matmul(psw[0:1, j % 2, :], csil[:, k:k + 1], wm[:, j % RING, k, :],
                                            start=(k == 0), stop=(k == KD - 1))
                last.then_inc(wused, 1)
                if j == 3:
                    pe.wait_ge(rot_ready, 1)
                    for t in range(NT):
                        if t >= 2:
                            pe.wait_ge(rot_copied, t - 1)
                        for v in range(2):
                            last = nc.tensor.transpose(psr[:, t % 2, v * P:(v + 1) * P], rot[:, t, v, :], g.ident[:, :])
                        last.then_inc(rot_ps, 1)
            pe.wait_ge(row_out, NCH)
            for col in range(6 * KD):
                last = nc.tensor.matmul(psm[:, col:col + 1], modrow[0:1, col * P:(col + 1) * P], ones1[0:1, 0:1],
                                        start=True, stop=True)
            last.then_inc(cols_ready, 1)
            pe.wait_ge(lam_one, 1)
            nc.tensor.matmul(psl[:, 0:1], ones1[0:1, :], lsum[0:1, 3:4], start=True, stop=True).then_inc(lam_ps, 1)
            pe.wait_ge(gains_ready, 1)
            for n in range(4):
                if n >= 2:
                    pe.wait_ge(gain_out, n - 1)
                bank = (psw, psr)[n % 2]
                for k in range(KD):
                    last = nc.tensor.matmul(bank[0:1, k // 4, (k % 4) * P:(k % 4 + 1) * P], gcol[:, n, k:k + 1],
                                            g.ident[:, :], start=True, stop=True)
                last.then_inc(gain_ps, 1)

        @block.scalar
        def _(act):
            act.wait_ge(vready, 1)
            nc.scalar.activation(csil[:, :], g.vcol[:, R_C:R_C + KD], ACT.Sigmoid).then_inc(sig, 1)
            act.wait_ge(lam_sum, 1)
            nc.scalar.activation(lsum[0:1, 0:2], lsum[0:1, 0:2], ACT.Exp).then_inc(lam_exp, 1)
            act.wait_ge(trig, 1)
            nc.scalar.activation(sinv[:, :, :], rsin[:, :, :], ACT.Sin).then_inc(sines, 1)
            nc.scalar.activation(cosv[:, :, :], rcos[:, :, :], ACT.Sin).then_inc(sines, 1)
            for j in range(NCH):
                act.wait_ge(wused, j + 1)
                nc.scalar.copy(modrow[0:1, j * BANK:(j + 1) * BANK], psw[0:1, j % 2, :]).then_inc(row_out, 1)
            for n in range(4):
                act.wait_ge(gain_ps, n + 1)
                nc.scalar.copy(outgain[0:1, n], (psw, psr)[n % 2][0:1, :, :].rearrange("p b c -> p (b c)")).then_inc(gain_out, 1)

        @block.vector
        def _(dve):
            link = Link(dve, dlink)
            dve.wait_ge(vcols, 1)
            nc.vector.tensor_copy(g.vcol[:, :], psv[:, 0:P]).then_inc(vready, 1)
            dve.wait_ge(vready, 1)
            dve.wait_ge(sig, 1)
            nc.vector.tensor_tensor(csil[:, :], csil[:, :], g.vcol[:, R_C:R_C + KD], ALU.mult).then_inc(csil_ready, 1)
            dve.wait_ge(bps, 1)
            link(nc.vector.tensor_copy(bcol[:, :], psb[:, :]))
            ups = bcol[:, :].rearrange("p (e h f) -> p e h f", h=2, f=KD)[:, :, 1, :]
            nc.vector.tensor_scalar(ups, ups, 1.0, None, ALU.add).then_inc(bias_done, 1)
            dve.wait_ge(loaded, 16 * 14)
            link(nc.vector.tensor_tensor(lprod[:, :, :], lamv[:, 0:2, :], lamv[:, 2:4, :], ALU.mult))
            nc.vector.tensor_reduce(lsum[0:1, 0:2], lprod[:, :, :], AX, ALU.add).then_inc(lam_sum, 1)
            dve.wait_ge(lam_exp, 1)
            link(nc.vector.tensor_tensor(lsum[0:1, 2:3], lsum[0:1, 1:2], lsum[0:1, 0:1], ALU.subtract))
            nc.vector.tensor_scalar(lsum[0:1, 3:4], lsum[0:1, 2:3], -LAMBDA_INIT, None, ALU.add).then_inc(lam_one, 1)
            link(nc.vector.tensor_copy(posf[:, :], posi[:, :]))
            inv = np.float32(THETA) ** (-np.arange(0, ROPE, 2, dtype=np.float32) / np.float32(ROPE))
            for i in range(HALF):
                link(nc.vector.tensor_scalar(ang[:, :, i], posf[:, :], float(inv[i]), None, ALU.mult))
            near, far = 1.5 * 2.0 ** 23, 1.5 * 2.0 ** 35
            link(nc.vector.tensor_scalar(tmp[:, :, :], ang[:, :, :], 1.0 / (2 * math.pi), None, ALU.mult))
            link(nc.vector.tensor_scalar(kk[:, 0], tmp[:, :, :], near, None, ALU.add))
            link(nc.vector.tensor_scalar(kk[:, 0], kk[:, 0], near, None, ALU.subtract))
            link(nc.vector.tensor_scalar(kk[:, 1], kk[:, 0], far, None, ALU.add))
            link(nc.vector.tensor_scalar(kk[:, 1], kk[:, 1], far, None, ALU.subtract))
            link(nc.vector.tensor_tensor(kk[:, 0], kk[:, 0], kk[:, 1], ALU.subtract))
            c1 = math.floor(2 * math.pi * 2 ** 8) / 2 ** 8
            c2 = math.floor((2 * math.pi - c1) * 2 ** 19) / 2 ** 19
            for part in (c1, c2, 2 * math.pi - c1 - c2):
                for q in (1, 0):
                    link(nc.vector.scalar_tensor_tensor(out=ang[:, :, :], in0=kk[:, q], scalar=-part, in1=ang[:, :, :],
                                                        op0=ALU.mult, op1=ALU.add))
            lim = 3.1415925
            link(nc.vector.tensor_scalar(rsin[:, :, :], ang[:, :, :], lim, -lim, ALU.min, ALU.max))
            link(nc.vector.tensor_scalar(tmp[:, :, :], rsin[:, :, :], -1.0, None, ALU.mult))
            link(nc.vector.tensor_tensor(tmp[:, :, :], tmp[:, :, :], rsin[:, :, :], ALU.min))
            nc.vector.tensor_scalar(rcos[:, :, :], tmp[:, :, :], math.pi / 2, None, ALU.add).then_inc(trig, 1)
            dve.wait_ge(sines, 2)
            dve.wait_ge(rot_set, 1)
            tab = rot[:, :, :, :].rearrange("p t v (h c) -> p t v h c", c=HD)
            for h in range(2):
                link(nc.vector.tensor_copy(tab[:, :, 0, h, 0:HALF], cosv[:, :, :]))
                link(nc.vector.tensor_copy(tab[:, :, 0, h, HALF:ROPE], cosv[:, :, :]))
                link(nc.vector.tensor_scalar(tab[:, :, 1, h, 0:HALF], sinv[:, :, :], -1.0, None, ALU.mult))
                link(nc.vector.tensor_copy(tab[:, :, 1, h, HALF:ROPE], sinv[:, :, :]))
            nc.vector.memset(tmp[:, :, :], 0.0).then_inc(rot_ready, 1)
            for t in range(NT):
                dve.wait_ge(rot_ps, t + 1)
                nc.vector.tensor_copy(g.rot[:, :, t * P:(t + 1) * P], psr[:, t % 2, 0:2 * P].rearrange("p (v c) -> p v c", v=2)).then_inc(rot_copied, 1)
            dve.wait_ge(lam_ps, 1)
            nc.vector.tensor_copy(g.neglam[:, :], psl[:, 0:1])
            dve.wait_ge(cols_ready, 1)
            link(nc.vector.tensor_tensor(mod[:, :], psm[:, 0:6 * KD], g.vcol[:, R_BMOD:R_BMOD + 6 * KD], ALU.add))
            for n, (r_pre, r_post) in enumerate(((R_GPRE, R_GPOST), (R_GFPRE, R_GFPOST))):
                m = 3 * KD * n
                link(nc.vector.tensor_copy(g.shift[:, n, :], mod[:, m:m + KD]))
                link(nc.vector.scalar_tensor_tensor(out=g.gain[:, n, :], in0=mod[:, m + KD:m + 2 * KD], scalar=1.0,
                                                    in1=g.vcol[:, r_pre:r_pre + KD], op0=ALU.add, op1=ALU.mult))
                link(nc.vector.tensor_tensor(gcol[:, n, :], mod[:, m + 2 * KD:m + 3 * KD],
                                             g.vcol[:, r_post:r_post + KD], ALU.mult))
            link(nc.vector.tensor_copy(gcol[:, 2, :], g.gain[:, 1, :]))
            nc.vector.tensor_copy(gcol[:, 3, :], g.shift[:, 1, :]).then_inc(gains_ready, 1)


def normalise(nc, a, g):
    with ExitStack() as ctx:
        sb, ps, sem = allocators(nc, ctx)
        G = 4
        x = sb("n_x", [P, 2, G, D])
        junk = sb("n_junk", [P, D])
        rms = sb("n_rms", [P, NT])
        inv = sb("n_inv", [P, NT])
        u = sb("n_u", [P, 2, KD, P])
        pst = ps("n_pst", [P, 2, KD, P])
        loaded = [sem(f"n_l{i}") for i in range(2)]
        squared, rooted, dlink = sem("n_sq"), sem("n_root"), sem("n_dlink")
        mean_ready, scaled, turned, u_ready, lo_done = sem("n_mean"), sem("n_sc"), sem("n_tu"), sem("n_u"), sem("n_lo")
        block = ctx.enter_context(nc.Block())
        xd = a.x[0].rearrange("(t p) d -> p t d", p=P)

        @block.sync
        def _(sp):
            for q in range(NT // G):
                if q >= 2:
                    sp.wait_ge(turned, G * (q - 1))
                sp.dma_start(x[:, q % 2], xd[:, G * q:G * q + G, :]).then_inc(loaded[q % 2], 16)

        @block.scalar
        def _(act):
            def squares(q):
                act.wait_ge(loaded[q % 2], 16 * (q // 2 + 1))
                for t in range(G * q, G * q + G):
                    if t:
                        act.wait_ge(squared, t)
                    nc.scalar.activation(junk[:, :], x[:, q % 2, t % G, :], ACT.Square,
                                         accum_out=rms[:, t:t + 1]).then_inc(squared, 1)
                act.wait_ge(mean_ready, q + 1)
                nc.scalar.activation(inv[:, G * q:G * q + G], inv[:, G * q:G * q + G], ACT.Sqrt).then_inc(rooted, 1)

            squares(0)
            for t in range(NT):
                if t % G == 0 and t + G < NT:
                    squares(t // G + 1)
                act.wait_ge(turned, t + 1)
                if t >= 2:
                    act.wait_ge(lo_done, t - 1)
                for k in range(KD):
                    ins = nc.scalar.activation(u[:, t % 2, k, :], pst[:, t % 2, k, :], ACT.Identity,
                                               scale=g.gain[:, 0, k:k + 1], bias=g.shift[:, 0, k:k + 1])
                ins.then_inc(u_ready, 1)

        @block.vector
        def _(dve):
            link = Link(dve, dlink)

            def means(q):
                dve.wait_ge(squared, G * q + G)
                nc.vector.tensor_scalar(inv[:, G * q:G * q + G], rms[:, G * q:G * q + G], 1.0 / D, EPS,
                                        ALU.mult, ALU.add).then_inc(mean_ready, 1)
                dve.wait_ge(rooted, q + 1)
                link(nc.vector.reciprocal(inv[:, G * q:G * q + G], inv[:, G * q:G * q + G]))

            def scale(t):
                xt = x[:, t // G % 2, t % G, :]
                nc.vector.tensor_scalar(xt, xt, inv[:, t:t + 1], None, ALU.mult).then_inc(scaled, 1)

            means(0)
            scale(0)
            scale(1)
            for t in range(NT):
                if t % G == 0 and t + G < NT:
                    means(t // G + 1)
                dve.wait_ge(u_ready, t + 1)
                cols = slice(t * P, (t + 1) * P)
                link(nc.vector.tensor_copy(g.uth[:, :, cols], u[:, t % 2]))
                nc.vector.tensor_tensor(g.utl[:, :, cols], u[:, t % 2], g.uth[:, :, cols].bitcast(F32),
                                        ALU.subtract).then_inc(lo_done, 1)
                if t + 2 < NT:
                    scale(t + 2)

        @block.tensor
        def _(pe):
            for t in range(NT):
                pe.wait_ge(scaled, t + 1)
                if t >= 2:
                    pe.wait_ge(u_ready, t - 1)
                for k in range(KD):
                    ins = nc.tensor.transpose(pst[:, t % 2, k, :], x[:, t // G % 2, t % G, k * P:(k + 1) * P],
                                              g.ident[:, :])
                ins.then_inc(turned, 1)


COLS = 2 * P
BLOCKS = IN_W // COLS
TB = T // BANK
SEGMENTS = (("q", 0, QKW // COLS), ("k", QKW // COLS, QKW // COLS), ("v", 2 * QKW // COLS, VW // COLS),
            ("p", (2 * QKW + VW) // COLS, PG * P // COLS),
            ("g", (2 * QKW + VW + PG * P) // COLS, 2 * D // COLS))


SWAP = [HALF + i for i in range(HALF)] + list(range(HALF)) + list(range(ROPE, 32))


def units_of(kind):
    return [(m, t) for m in range(2) for t in range(TB)] if kind != "v" else [(0, t) for t in range(NT)]


def project(nc, a, g):
    with ExitStack() as ctx:
        sb, ps, sem = allocators(nc, ctx)
        RING = 4
        raw = sb("j_raw", [P, KD, COLS])
        wh = [sb(f"j_wh{i}", [P, KD, COLS], F32R) for i in range(2)]
        wl = [sb(f"j_wl{i}", [P, KD, COLS], F32R) for i in range(2)]
        z = sb("j_z", [P, RING, BANK])
        swap = sb("j_swap", [P, 2, BANK])
        psz = ps("j_psz", [P, RING, BANK])
        wloaded, hi_done, lo_done = sem("j_w"), sem("j_hi"), sem("j_lo")
        made, copied, roped, dlink = sem("j_made"), sem("j_copied"), sem("j_roped"), sem("j_dlink")
        stored = [sem(f"j_st{i}") for i in range(RING)]
        block = ctx.enter_context(nc.Block())
        w = a.w_in[0].rearrange("(k p) n -> p k n", p=P)

        def blocks(eng, body, peel_last=False):
            unit = 0
            for kind, first, count in SEGMENTS:
                per = len(units_of(kind))
                turns = count // 2 - (peel_last and kind == "g")
                with eng.Fori(0, turns) as i:
                    for slot in range(2):
                        body(kind, i * 2 + (first + slot), slot, i * (2 * per) + (unit + slot * per), False)
                if turns < count // 2:
                    for slot in range(2):
                        body(kind, first + 2 * turns + slot, slot, unit + (2 * turns + slot) * per, slot == 1)
                unit += count * per

        @block.gpsimd
        def _(pool):
            nc.gpsimd.dma_start(raw[:, :, :], w[:, :, 0:COLS]).then_inc(wloaded, 16)
            with pool.Fori(1, BLOCKS) as b:
                pool.wait_ge(lo_done, b)
                nc.gpsimd.dma_start(raw[:, :, :], w[:, :, ds(b * COLS, COLS)]).then_inc(wloaded, 16)

        @block.scalar
        def _(act):
            for r in range(RING):
                act.sem_inc(stored[r], 16)
            act.sem_inc(copied, RING)
            act.wait_ge(wloaded, 16)
            nc.scalar.copy(wh[0][:, :, :], raw[:, :, :]).then_inc(hi_done, 1)

            def body(kind, b, slot, unit, last):
                for n in range(len(units_of(kind))):
                    r = n % RING
                    act.wait_ge(made, unit + (n + 1))
                    act.wait_ge(stored[r], unit * (16 // RING) + 16 * (n // RING + 1))
                    wide = psz[:, r, :] if kind != "v" else psz[:, r, 0:COLS]
                    out = z[:, r, :] if kind != "v" else z[:, r, 0:COLS]
                    if kind == "g":
                        ins = nc.scalar.activation(out, wide, ACT.Sigmoid)
                    elif kind == "q":
                        ins = nc.scalar.activation(out, wide, ACT.Copy, scale=HD ** -0.5)
                    else:
                        ins = nc.scalar.copy(out, wide)
                    ins.then_inc(copied, 1)
                    if n == 1 and not last:
                        act.wait_ge(wloaded, b * 16 + 32)
                        nc.scalar.copy(wh[1 - slot][:, :, :], raw[:, :, :]).then_inc(hi_done, 1)

            blocks(act, body, peel_last=True)

        @block.vector
        def _(dve):
            def split_lo(after, slot):
                dve.wait_ge(hi_done, after)
                nc.vector.tensor_tensor(wl[slot][:, :, :], raw[:, :, :], wh[slot][:, :, :].bitcast(F32),
                                        ALU.subtract).then_inc(lo_done, 1)

            split_lo(1, 0)

            def body(kind, b, slot, unit, last):
                for n, (m, t) in enumerate(units_of(kind)):
                    r = n % RING
                    if kind in "qk":
                        dve.wait_ge(copied, unit + (n + 1 + RING))
                        zz = z[:, r, :]
                        nc.vector.tensor_tensor(swap[:, 1, :], zz, g.rot[:, 0, t * BANK:(t + 1) * BANK],
                                                ALU.mult).then_inc(dlink, 1)
                        nc.vector.stream_shuffle(swap[:, 0, :], zz, SWAP).then_inc(dlink, 1)
                        dve.wait_ge(dlink, unit * 3 + (3 * n + 2))
                        nc.vector.tensor_tensor(swap[:, 0, :], swap[:, 0, :], g.rot[:, 1, t * BANK:(t + 1) * BANK],
                                                ALU.mult).then_inc(dlink, 1)
                        dve.wait_ge(dlink, unit * 3 + (3 * n + 3))
                        nc.vector.tensor_tensor(zz, swap[:, 0, :], swap[:, 1, :], ALU.add).then_inc(roped, 1)
                        dve.wait_ge(roped, unit + (n + 1))
                    if n == 1 and not last:
                        split_lo(b + 2, 1 - slot)

            blocks(dve, body, peel_last=True)

        @block.tensor
        def _(pe):
            def body(kind, b, slot, unit, last):
                pe.wait_ge(lo_done, b + 1)
                for n, (m, t) in enumerate(units_of(kind)):
                    r = n % RING
                    pe.wait_ge(copied, unit + (n + 1))
                    for k in range(KD):
                        if kind != "v":
                            tok = slice(t * BANK, (t + 1) * BANK)
                            col = slice(m * P, (m + 1) * P)
                            terms = ((wh[slot][:, k, col], g.uth[:, k, tok]), (wh[slot][:, k, col], g.utl[:, k, tok]),
                                     (wl[slot][:, k, col], g.uth[:, k, tok]))
                            out = psz[:, r, :]
                        else:
                            tok = slice(t * P, (t + 1) * P)
                            terms = ((g.uth[:, k, tok], wh[slot][:, k, :]), (g.uth[:, k, tok], wl[slot][:, k, :]),
                                     (g.utl[:, k, tok], wh[slot][:, k, :]))
                            out = psz[:, r, 0:COLS]
                        for j, (still, moving) in enumerate(terms):
                            ins = nc.tensor.matmul(out, still, moving, start=(k == 0 and j == 0),
                                                   stop=(k == KD - 1 and j == 2))
                    ins.then_inc(made, 1)

            blocks(pe, body)

        @block.sync
        def _(sp):
            def body(kind, b, slot, unit, last):
                for n, (m, t) in enumerate(units_of(kind)):
                    r = n % RING
                    if kind in "qk":
                        sp.wait_ge(roped, unit + (n + 1))
                    else:
                        sp.wait_ge(copied, unit + (n + 1 + RING))
                    if kind == "v":
                        out = g.v_d[t * P:(t + 1) * P, ds(b * COLS - 2 * QKW, COLS)]
                        src = z[:, r, 0:COLS]
                    else:
                        out = g.zt_d[ds(b * COLS + m * P, P), t * BANK:(t + 1) * BANK]
                        src = z[:, r, :]
                    nc.sync.dma_start(out, src).then_inc(stored[r], 16)

            blocks(sp, body)
            total = sum(count * len(units_of(kind)) for kind, _, count in SEGMENTS)
            for r in range(RING):
                sp.wait_ge(stored[r], 16 * (total // RING + 1))


def pool_mix(nc, a, g):
    with ExitStack() as ctx:
        sb, ps, sem = allocators(nc, ctx)
        PAD = max(WINDOWS)
        p = sb("w_p", [P, 2, PAD + T])
        lev = sb("w_lev", [P, 2, PAD + T])
        cnt = sb("w_cnt", [P, PG, PAD])
        head = sb("w_head", [P, PAD])
        mh = sb("w_mh", [P, T], F32R)
        ml = sb("w_ml", [P, T], F32R)
        wraw = sb("w_raw", [P, PG, P])
        wh = sb("w_wh", [P, PG, P], F32R)
        wl = sb("w_wl", [P, PG, P], F32R)
        y = sb("w_y", [P, 2, T])
        psy = ps("w_ps", [P, 4, BANK])
        ploaded, wloaded = [sem("w_pl0"), sem("w_pl1")], sem("w_wl")
        cleared, wsplit, dlink, mixed = sem("w_clr"), sem("w_ws"), sem("w_dl"), sem("w_mix")
        hi_done, lo_done, made, left = sem("w_hi"), sem("w_lo"), sem("w_made"), sem("w_left")
        wlow, stored, table = sem("w_wlow"), [sem("w_st0"), sem("w_st1")], sem("w_tab")
        block = ctx.enter_context(nc.Block())
        p_row = 2 * QKW + VW

        @block.sync
        def _(sp):
            sp.dma_start(wraw[:, :, :], a.w_pool_group[0].rearrange("g c d -> c g d")).then_inc(wloaded, 16)
            for q in range(PG):
                if q >= 2:
                    sp.wait_ge(lo_done, q - 1)
                sp.dma_start(p[:, q % 2, PAD:], g.zt_d[p_row + q * P:p_row + (q + 1) * P, :]).then_inc(ploaded[q % 2], 16)
                if q >= 1:
                    sp.wait_ge(left, 4 * q)
                    sp.dma_start(g.yt_d[(q - 1) * P:q * P, :], y[:, (q - 1) % 2, :]).then_inc(stored[(q - 1) % 2], 16)
            sp.wait_ge(left, 4 * PG)
            sp.dma_start(g.yt_d[(PG - 1) * P:PG * P, :], y[:, (PG - 1) % 2, :]).then_inc(stored[(PG - 1) % 2], 16)
            sp.wait_ge(stored[0], 32)
            sp.wait_ge(stored[1], 32)

        @block.gpsimd
        def _(pool):
            nc.gpsimd.memset(lev[:, :, 0:PAD], 0.0)
            nc.gpsimd.memset(p[:, :, 0:PAD], 0.0).then_inc(cleared, 1)
            for q, w in enumerate(WINDOWS):
                for t in range(PAD):
                    ins = nc.gpsimd.memset(cnt[:, q, t:t + 1], 1.0 / min(t + 1, w))
            ins.then_inc(table, 1)

        @block.scalar
        def _(act):
            act.wait_ge(wloaded, 16)
            nc.scalar.copy(wh[:, :, :], wraw[:, :, :]).then_inc(wsplit, 1)
            for q in range(PG):
                act.wait_ge(mixed, q + 1)
                if q:
                    act.wait_ge(made, 4 * q)
                nc.scalar.copy(mh[:, :], p[:, q % 2, PAD:]).then_inc(hi_done, 1)
                for t in range(TB):
                    act.wait_ge(made, 4 * q + t + 1)
                    if t == 0 and q >= 2:
                        act.wait_ge(stored[q % 2], 16)
                    nc.scalar.activation(y[:, q % 2, t * BANK:(t + 1) * BANK], psy[:, t, :], ACT.Copy,
                                         scale=g.vcol[:, R_PSC + q:R_PSC + q + 1]).then_inc(left, 1)

        @block.vector
        def _(dve):
            link = Link(dve, dlink)
            dve.wait_ge(wsplit, 1)
            nc.vector.tensor_tensor(wl[:, :, :], wraw[:, :, :], wh[:, :, :].bitcast(F32), ALU.subtract).then_inc(wlow, 1)
            dve.wait_ge(cleared, 1)
            dve.wait_ge(table, 1)
            for q, w in enumerate(WINDOWS):
                dve.wait_ge(ploaded[q % 2], 16 * (q // 2 + 1))
                src, step, n = p[:, q % 2], 1, 0
                while step < w:
                    dst = lev[:, n % 2]
                    link(nc.vector.tensor_tensor(dst[:, PAD:], src[:, PAD:], src[:, PAD - step:PAD + T - step], ALU.add))
                    src, step, n = dst, step * 2, n + 1
                pq = p[:, q % 2]
                link(nc.vector.tensor_tensor(head[:, :], src[:, PAD:2 * PAD], cnt[:, q], ALU.mult))
                link(nc.vector.tensor_tensor(head[:, :], head[:, :], pq[:, PAD:2 * PAD], ALU.subtract))
                link(nc.vector.scalar_tensor_tensor(out=pq[:, PAD:], in0=src[:, PAD:], scalar=1.0 / w, in1=pq[:, PAD:],
                                                    op0=ALU.mult, op1=ALU.subtract))
                nc.vector.tensor_copy(pq[:, PAD:2 * PAD], head[:, :]).then_inc(mixed, 1)
                dve.wait_ge(hi_done, q + 1)
                nc.vector.tensor_tensor(ml[:, :], pq[:, PAD:], mh[:, :].bitcast(F32), ALU.subtract).then_inc(lo_done, 1)

        @block.tensor
        def _(pe):
            pe.wait_ge(wlow, 1)
            for q in range(PG):
                pe.wait_ge(lo_done, q + 1)
                for t in range(TB):
                    if q:
                        pe.wait_ge(left, 4 * (q - 1) + t + 1)
                    c = slice(t * BANK, (t + 1) * BANK)
                    nc.tensor.matmul(psy[:, t, :], wh[:, q, :], mh[:, c], start=True, stop=False)
                    nc.tensor.matmul(psy[:, t, :], wh[:, q, :], ml[:, c], start=False, stop=False)
                    nc.tensor.matmul(psy[:, t, :], wl[:, q, :], mh[:, c], start=False, stop=True).then_inc(made, 1)


def attend(nc, a, g):
    with ExitStack() as ctx:
        sb, ps, sem = allocators(nc, ctx)
        SR, TR = 5, 2
        PC = T // 2
        kh = [sb(f"t_kh{i}", [P, 2, T], F32R) for i in range(2)]
        kl = [sb(f"t_kl{i}", [P, 2, T], F32R) for i in range(2)]
        rq = sb("t_rq", [P, 2, T])
        qs = [sb(f"t_qs{i}", [P, 2, T], F32R) for i in range(2)]
        v2 = [sb(f"t_v2{i}", [P, NT, 2, P], F32R) for i in range(2)]
        pr = sb("t_pr", [P, 2, 2, T])
        ath = sb("t_ath", [P, NT, P], F32R)
        atl = sb("t_atl", [P, NT, P], F32R)
        ost = sb("t_ost", [P, NT, P])
        o1 = sb("t_o1", [P, P])
        mx = sb("t_mx", [P, 2, 4])
        mm = sb("t_mm", [P, 2])
        negm = sb("t_negm", [P, 2, 2])
        part = sb("t_part", [P, 2, 2, 4])
        tot = sb("t_tot", [P, 2, 2])
        rec = sb("t_rec", [P, 2, 2])
        mix = sb("t_mix", [P, 2])
        mrow = sb("t_mrow", [1, P], BF16)
        mcol = sb("t_mcol", [1, CHUNK], BF16)
        pss = ps("t_pss", [P, SR, BANK])
        pst = ps("t_pst", [P, TR, BANK])
        pso = ps("t_pso", [P, BANK])
        raw_in, raw_ready, hi_done, split = sem("t_raw"), sem("t_rawr"), sem("t_hi"), sem("t_split")
        s_ready, exp_done, negm_ready, a_ready = sem("t_s"), sem("t_exp"), sem("t_negm"), sem("t_a")
        t_ready, th_done, tl_done, av_done = sem("t_t"), sem("t_th"), sem("t_tl"), sem("t_av")
        o1_done, o_done, ostored, masks, dl = sem("t_o1"), sem("t_o"), [sem("t_ost0"), sem("t_ost1")], sem("t_masks"), sem("t_dl")
        block = ctx.enter_context(nc.Block())

        nb = [-(-(i + 1) * P // BANK) for i in range(NT)]
        width = lambda i, b: min(BANK, (i + 1) * P - b * BANK)
        seq, n = {}, 0
        for i in range(NT):
            for s in range(2):
                for b in range(nb[i]):
                    seq[i, s, b] = n
                    n += 1
        SB = n
        gbase = [sum(nb[:i]) for i in range(NT + 1)]
        GB = gbase[NT]
        assert SB % SR == 0 and GB % TR == 0
        PIECES = 10

        def steps(eng, start, behind, both, finish, begin=lambda hh: None):
            def run(head, first, limit):
                for n in range(first, 2 * NT + 2):
                    if first == 0 and n == 2:
                        break
                    this, last, older = [(head + m // NT, m // NT % 2, m % NT) if 0 <= m < limit else None
                                         for m in (n, n - 1, n - 2)]
                    if this:
                        start(*this)
                    behind(last, older)
                    both(last, this)
                    finish(older, this)

            begin(None)
            run(0, 0, 2)
            with eng.Fori(0, HEADS // 2 - 1) as hh:
                begin(hh)
                run(hh * 2, 2, 2 * NT + 2)
            begin(HEADS // 2 - 1)
            run(HEADS - 2, 2, 2 * NT)

        def hi_piece(par, n):
            if n < 4:
                c = slice(n % 2 * PC, (n % 2 + 1) * PC)
                return kh[par][:, n // 2, c], kl[par][:, n // 2, c].bitcast(F32)
            if n < 8:
                c = slice(n % 2 * PC, (n % 2 + 1) * PC)
                return qs[par][:, n // 2 - 2, c], rq[:, n // 2 - 2, c]
            t = slice((n - 8) * NT // 2, (n - 7) * NT // 2)
            return v2[par][:, t, 0, :], v2[par][:, t, 1, :].bitcast(F32)

        def lo_piece(par, n):
            hi, raw = hi_piece(par, n)
            if 4 <= n < 8:
                return hi[HD:P], raw[HD:P], hi[HD:P].bitcast(F32)
            if n < 4:
                return kl[par][:, n // 2, n % 2 * PC:(n % 2 + 1) * PC], raw, hi.bitcast(F32)
            return v2[par][:, (n - 8) * NT // 2:(n - 7) * NT // 2, 1, :], raw, hi.bitcast(F32)

        @block.gpsimd
        def _(pool):
            nc.gpsimd.memset(mrow[:, :], 0.0).then_inc(masks, 1)
            pool.wait_ge(masks, 1)
            nc.gpsimd.memset(mrow[:, 0:CHUNK], 1.0).then_inc(masks, 1)
            nc.gpsimd.memset(mcol[:, :], NEG).then_inc(masks, 1)
            q_v = g.zt_d[0:QKW, :]
            k_v = g.zt_d[QKW:2 * QKW, :]
            v_v = g.v_d.rearrange("(t p) d -> p t d", p=P)

            def load(h, par):
                row = h * P
                for half in range(2):
                    rows = slice(half * HD, (half + 1) * HD)
                    nc.gpsimd.dma_start(kl[par][rows].bitcast(F32),
                                        k_v[ds(row, P), :].rearrange("(s d) t -> d s t", s=2)).then_inc(raw_in, 16)
                    nc.gpsimd.dma_start(rq[rows], q_v[ds(row, P), :].rearrange("(s d) t -> d s t", s=2)).then_inc(raw_in, 16)
                nc.gpsimd.dma_start(v2[par][:, :, 1, :].bitcast(F32), v_v[:, :, ds(row, P)]).then_inc(raw_in, 16)
                pool.wait_ge(raw_in, h * 80 + 80)

            load(0, 0)
            pool.sem_inc(raw_ready, 1)
            pool.wait_ge(split, PIECES)

            def following(h, par):
                pool.wait_ge(av_done, h * NT + 1)
                load(h + 1, 1 - par)
                pool.sem_inc(raw_ready, 1)
                for n in range(PIECES):
                    pool.wait_ge(hi_done, h * PIECES + (PIECES + n + 1))
                    out, raw, hi = lo_piece(1 - par, n)
                    nc.gpsimd.tensor_tensor(out, raw, hi, ALU.subtract).then_inc(split, 1)
                    pool.wait_ge(split, h * PIECES + (PIECES + n + 1))

            with pool.Fori(0, HEADS // 2 - 1) as hh:
                for par in range(2):
                    following(hh * 2 + par, par)
            following(HEADS - 2, 0)

        @block.sync
        def _(sp):
            for half in range(2):
                sp.sem_inc(ostored[half], 16)
            with sp.Fori(0, HEADS) as h:
                for half in range(2):
                    t = slice(half * NT // 2, (half + 1) * NT // 2)
                    sp.wait_ge(o_done, h * NT + ((half + 1) * NT // 2 + 1))
                    sp.dma_start(g.o_d.rearrange("(t p) d -> p t d", p=P)[:, t, ds(h * P, P)],
                                 ost[:, t, :]).then_inc(ostored[half], 16)
            for half in range(2):
                sp.wait_ge(ostored[half], 16 * (HEADS + 1))

        @block.scalar
        def _(act):
            act.sem_inc(s_ready, 1)
            act.sem_inc(av_done, 1)
            act.sem_inc(o_done, 1)
            act.sem_inc(exp_done, SR)
            act.sem_inc(tl_done, TR)
            act.wait_ge(raw_ready, 1)
            for n in range(PIECES):
                out, raw = hi_piece(0, n)
                nc.scalar.copy(out, raw).then_inc(hi_done, 1)

            def exps(h, i, s):
                act.wait_ge(negm_ready, h * (2 * NT) + (2 * i + s + 1))
                for b in range(nb[i]):
                    w = width(i, b)
                    nc.scalar.activation(pr[:, i % 2, s, b * BANK:b * BANK + w], pss[:, seq[i, s, b] % SR, 0:w],
                                         ACT.Exp, bias=negm[:, i % 2, s:s + 1],
                                         accum_out=part[:, i % 2, s, b:b + 1]).then_inc(exp_done, 1)

            def start(h, par, i):
                exps(h, i, 0)

            def behind(last, older):
                h, par, i = last or (0, 0, -1)
                if 0 <= i - 5 < PIECES and not (isinstance(h, int) and h == HEADS - 1):
                    if i == 5:
                        act.wait_ge(raw_ready, h + 2)
                    out, raw = hi_piece(1 - par, i - 5)
                    nc.scalar.copy(out, raw).then_inc(hi_done, 1)

            def both(last, this):
                if last:
                    h, par, i = last
                    for q in range(nb[i]):
                        act.wait_ge(t_ready, h * GB + (gbase[i] + q + 1))
                        c = min(4, i + 1 - 4 * q) * P
                        nc.scalar.copy(ath[:, 4 * q:4 * q + c // P, :].rearrange("p t c -> p (t c)"),
                                       pst[:, (gbase[i] + q) % TR, 0:c]).then_inc(th_done, 1)

            def finish(older, this):
                if older:
                    h, par, i = older
                    act.wait_ge(av_done, h * NT + (i + 2))
                    act.wait_ge(o_done, h * NT + (i + 1))
                    nc.scalar.activation(o1[:, :], pso[:, 0:P], ACT.Copy, scale=rec[:, i % 2, 0:1]).then_inc(o1_done, 1)
                if this:
                    exps(this[0], this[2], 1)

            steps(act, start, behind, both, finish)

        @block.vector
        def _(dve):
            for n in range(PIECES):
                dve.wait_ge(hi_done, n + 1)
                out, raw, hi = lo_piece(0, n)
                nc.vector.tensor_tensor(out, raw, hi, ALU.subtract).then_inc(split, 1)

            LINKS = sum((2 * (n + (n > 1))) + (n > 1) + 2 for n in nb)
            counts = {"ahead": 0, "base": 0, "here": 0}

            def begin(hh):
                if hh is not None:
                    if not isinstance(hh, int):
                        counts["ahead"] = counts["here"]
                    counts["base"] = hh * (2 * LINKS) + counts["ahead"]
                    counts["here"] = 0

            def link(ins):
                counts["here"] += 1
                ins.then_inc(dl, 1)
                dve.wait_ge(dl, counts["base"] + counts["here"])

            def maximum(h, i, s, b):
                dve.wait_ge(s_ready, h * SB + (seq[i, s, b] + 2))
                ins = nc.vector.tensor_reduce(mx[:, s, b:b + 1], pss[:, seq[i, s, b] % SR, 0:width(i, b)], AX, ALU.max)
                if b + 1 < nb[i]:
                    counts["here"] += 1
                    ins.then_inc(dl, 1)
                    return
                link(ins)
                top = mx[:, s, 0:1]
                if nb[i] > 1:
                    link(nc.vector.tensor_reduce(mm[:, s:s + 1], mx[:, s, 0:nb[i]], AX, ALU.max))
                    top = mm[:, s:s + 1]
                nc.vector.tensor_scalar(negm[:, i % 2, s:s + 1], top, -1.0, None, ALU.mult).then_inc(negm_ready, 1)

            def start(h, par, i):
                for b in range(nb[i]):
                    maximum(h, i, 0, b)

            def behind(last, older):
                if not last:
                    return
                h, par, i = last
                dve.wait_ge(exp_done, h * SB + (seq[i, 1, nb[i] - 1] + 1 + SR))
                sums = part[:, i % 2, :, 0]
                if nb[i] > 1:
                    link(nc.vector.tensor_reduce(tot[:, i % 2], part[:, i % 2, :, 0:nb[i]], AX, ALU.add))
                    sums = tot[:, i % 2]
                link(nc.vector.reciprocal(rec[:, i % 2], sums))
                link(nc.vector.scalar_tensor_tensor(out=mix[:, i % 2:i % 2 + 1], in0=sums[:, 0:1],
                                                    scalar=g.neglam[:, 0:1], in1=rec[:, i % 2, 1:2],
                                                    op0=ALU.mult, op1=ALU.mult))
                w = (i + 1) * P
                nc.vector.scalar_tensor_tensor(out=pr[:, i % 2, 0, 0:w], in0=pr[:, i % 2, 1, 0:w],
                                               scalar=mix[:, i % 2:i % 2 + 1], in1=pr[:, i % 2, 0, 0:w],
                                               op0=ALU.mult, op1=ALU.add).then_inc(a_ready, 1)

            def both(last, this):
                for q in range(4):
                    if this and q < nb[this[2]]:
                        maximum(this[0], this[2], 1, q)
                    if last and q < nb[last[2]]:
                        h, par, i = last
                        dve.wait_ge(th_done, h * GB + (gbase[i] + q + 1))
                        c = min(4, i + 1 - 4 * q) * P
                        flat = slice(4 * q, 4 * q + c // P)
                        nc.vector.tensor_tensor(atl[:, flat, :].rearrange("p t c -> p (t c)"),
                                                pst[:, (gbase[i] + q) % TR, 0:c],
                                                ath[:, flat, :].rearrange("p t c -> p (t c)").bitcast(F32),
                                                ALU.subtract).then_inc(tl_done, 1)

            def finish(older, this):
                if not older:
                    return
                h, par, i = older
                if i % (NT // 2) == 0:
                    dve.wait_ge(ostored[i // (NT // 2)], h * 16 + 16)
                dve.wait_ge(o1_done, h * NT + (i + 1))
                nc.vector.scalar_tensor_tensor(out=ost[:, i, :], in0=pso[:, P:2 * P], scalar=rec[:, i % 2, 0:1],
                                               in1=o1[:, :], op0=ALU.mult, op1=ALU.add).then_inc(o_done, 1)

            steps(dve, start, behind, both, finish, begin)

        @block.tensor
        def _(pe):
            pe.wait_ge(masks, 3)

            def scores(h, par, i, s, b):
                still = qs[par][:, s, i * P:(i + 1) * P]
                n, w = seq[i, s, b], width(i, b)
                last = b == nb[i] - 1
                pe.wait_ge(exp_done, h * SB + (n + 1))
                c = slice(b * BANK, b * BANK + w)
                nc.tensor.matmul(pss[:, n % SR, 0:w], still, kh[par][:, s, c], start=True, stop=False)
                ins = nc.tensor.matmul(pss[:, n % SR, 0:w], still, kl[par][:, s, c], start=False, stop=not last)
                if last:
                    ins = nc.tensor.matmul(pss[:, n % SR, w - CHUNK:w], mrow[:, :], mcol[:, :], start=False, stop=True)
                ins.then_inc(s_ready, 1)

            def start(h, par, i):
                if i == 0:
                    pe.wait_ge(split, h * PIECES + PIECES)
                for b in range(nb[i]):
                    scores(h, par, i, 0, b)

            def behind(last, older):
                if not older:
                    return
                h, par, i = older
                pe.wait_ge(o_done, h * NT + (i + 1))
                pe.wait_ge(tl_done, h * GB + (gbase[i + 1] + TR))
                for t in range(i + 1):
                    both_v = v2[par][:, t].rearrange("p s c -> p (s c)")
                    nc.tensor.matmul(pso[:, 0:2 * P], ath[:, t, :], both_v, start=(t == 0), stop=False)
                    ins = nc.tensor.matmul(pso[:, 0:2 * P], atl[:, t, :], both_v, start=False, stop=(t == i))
                ins.then_inc(av_done, 1)

            def both(last, this):
                for q in range(4):
                    if this and q < nb[this[2]]:
                        scores(*this, 1, q)
                    if last and q < nb[last[2]]:
                        h, par, i = last
                        if q == 0:
                            pe.wait_ge(a_ready, h * NT + (i + 1))
                        pe.wait_ge(tl_done, h * GB + (gbase[i] + q + 1))
                        for t in range(4 * q, min(4 * q + 4, i + 1)):
                            ins = nc.tensor.transpose(pst[:, (gbase[i] + q) % TR, (t % 4) * P:(t % 4 + 1) * P],
                                                      pr[:, i % 2, 0, t * P:(t + 1) * P], g.ident[:, :])
                        ins.then_inc(t_ready, 1)

            steps(pe, start, behind, both, lambda older, this: None)


def pipeline(eng, stages, count):
    deepest = max(lag for _, lag in stages)
    first = deepest + 2 + deepest % 2

    def step(at, base):
        for fn, lag in stages:
            if base is None:
                if 0 <= at - lag < count:
                    fn(at - lag, (at - lag) % 2)
            else:
                fn(base + (at - lag), (at - lag) % 2)

    for n in range(first):
        step(n, None)
    with eng.Fori(0, (count - first) // 2) as i:
        step(first, i * 2)
        step(first + 1, i * 2)
    for n in range(count, count + deepest):
        step(n, None)


def early(t, n):
    return isinstance(t, int) and t < n


def branches(nc, a, g):
    with ExitStack() as ctx:
        sb, ps, sem = allocators(nc, ctx)
        KP = PG
        KW = KD + KP
        RING = 4
        raw = sb("b_raw", [P, RING, D])
        wh = sb("b_wh", [P, KW, D], F32R)
        wl = sb("b_wl", [P, KW, D], F32R)
        o = sb("b_o", [P, TB, HEADS, P])
        sq = sb("b_sq", [P, HEADS, P])
        rs = sb("b_rs", [P, TB, HEADS])
        gs = sb("b_gs", [P, 1])
        xh = sb("b_xh", [P, KW, BANK], F32R)
        xl = sb("b_xl", [P, KW, BANK], F32R)
        gate = sb("b_gate", [P, 2, 2, BANK])
        ma = sb("b_ma", [P, BANK])
        mg = sb("b_mg", [P, 2, BANK])
        yraw = gate[:, :, :, :].rearrange("p a b c -> p (a b) c")
        psa = ps("b_psa", [P, 2, 2, BANK])
        pst = ps("b_pst", [P, 2, BANK])
        wloaded, whi, wlo = [sem(f"b_w{i}") for i in range(RING)], sem("b_whi"), sem("b_wlo")
        oin, yin, gin = sem("b_oin"), sem("b_yin"), [sem("b_g0"), sem("b_g1")]
        dl, mean, rooted, normed = sem("b_dl"), sem("b_mean"), sem("b_root"), sem("b_norm")
        turned, xhi, xlo, yhi, ylo = sem("b_turn"), sem("b_xhi"), sem("b_xlo"), sem("b_yhi"), sem("b_ylo")
        made, merged, stored = sem("b_made"), sem("b_merged"), [sem("b_s0"), sem("b_s1")]
        block = ctx.enter_context(nc.Block())
        watt = a.w_att_branch[0].rearrange("(k p) n -> k p n", p=P)
        wpool = a.w_pool_branch[0].rearrange("(k p) n -> k p n", p=P)
        ov = g.o_d.rearrange("(b t p) (h c) -> b p t h c", t=TB, p=P, h=HEADS)
        GA = 2 * QKW + VW + PG * P

        @block.gpsimd
        def _(pool):
            def outputs(b):
                nc.gpsimd.dma_start(o[:, :, :, :].rearrange("p t h c -> p t (h c)"),
                                    ov[b].rearrange("p t h c -> p t (h c)")).then_inc(oin, 16)

            for k in range(KW):
                if k >= RING:
                    pool.wait_ge(wlo, k - RING + 1)
                src = watt[k] if k < KD else wpool[k - KD]
                nc.gpsimd.dma_start(raw[:, k % RING], src).then_inc(wloaded[k % RING], 16)
                if k == 1:
                    outputs(0)
            for b in range(1, TB):
                pool.wait_ge(turned, KD * b)
                outputs(b)

        @block.sync
        def _(sp):
            for b in range(TB):
                cols = slice(b * BANK, (b + 1) * BANK)
                if b:
                    sp.wait_ge(merged, KD * b)
                sp.dma_start(yraw, g.yt_d.rearrange("(k p) t -> p k t", p=P)[:, :, cols]).then_inc(yin, 16)
                sp.wait_ge(ylo, b + 1)
                for m in range(KD):
                    if m >= 2:
                        sp.wait_ge(merged, KD * b + m - 1)
                    for v in range(2):
                        row = GA + v * D + m * P
                        sp.dma_start(gate[:, m % 2, v], g.zt_d[row:row + P, cols]).then_inc(gin[m % 2], 16)
                    if m >= 1:
                        sp.wait_ge(merged, KD * b + m)
                        sp.dma_start(g.mt_d[(m - 1) * P:m * P, cols], mg[:, (m - 1) % 2]).then_inc(stored[(m - 1) % 2], 16)
                sp.wait_ge(merged, KD * b + KD)
                sp.dma_start(g.mt_d[(KD - 1) * P:KD * P, cols], mg[:, (KD - 1) % 2]).then_inc(stored[(KD - 1) % 2], 16)
            for r in range(2):
                sp.wait_ge(stored[r], 16 * TB * KD // 2)

        @block.scalar
        def _(act):
            def weights(first, last):
                for k in range(first, last):
                    act.wait_ge(wloaded[k % RING], 16 * (k // RING + 1))
                    nc.scalar.copy(wh[:, k, :], raw[:, k % RING]).then_inc(whi, 1)

            weights(0, RING)
            for b in range(TB):
                act.wait_ge(mean, b + 1)
                nc.scalar.activation(rs[:, :, :], rs[:, :, :], ACT.Sqrt).then_inc(rooted, 1)
                if b == 0:
                    weights(RING, KD)
                if b:
                    act.wait_ge(made, KD * b)
                for h in range(HEADS):
                    act.wait_ge(turned, KD * b + h + 1)
                    nc.scalar.activation(xh[:, h, :], pst[:, h % 2, :], ACT.Copy, scale=gs[:, 0:1]).then_inc(xhi, 1)
                if b == 0:
                    weights(KD, KW)
                act.wait_ge(yin, 16 * (b + 1))
                nc.scalar.copy(xh[:, KD:, :], yraw).then_inc(yhi, 1)

        @block.vector
        def _(dve):
            link = Link(dve, dl)
            link(nc.vector.tensor_scalar(gs[:, :], g.vcol[:, R_GSUB:R_GSUB + 1], 1.0 - LAMBDA_INIT, None, ALU.mult))
            def weights(first, last):
                for k in range(first, last):
                    dve.wait_ge(whi, k + 1)
                    nc.vector.tensor_tensor(wl[:, k, :], raw[:, k % RING], wh[:, k, :].bitcast(F32),
                                            ALU.subtract).then_inc(wlo, 1)

            def norm(b, part):
                if part < TB:
                    if part == 0:
                        dve.wait_ge(oin, 16 * (b + 1))
                    link(nc.vector.tensor_tensor(sq[:, :, :], o[:, part], o[:, part], ALU.mult))
                    link(nc.vector.tensor_reduce(rs[:, part, :], sq[:, :, :], AX, ALU.add))
                    if part == TB - 1:
                        nc.vector.tensor_scalar(rs[:, :, :], rs[:, :, :], 1.0 / P, EPS, ALU.mult, ALU.add).then_inc(mean, 1)
                else:
                    dve.wait_ge(rooted, b + 1)
                    link(nc.vector.reciprocal(rs[:, :, :], rs[:, :, :]))
                    for t in range(TB):
                        ins = nc.vector.tensor_tensor(o[:, t], o[:, t], rs[:, t, :].to_broadcast([P, HEADS, P]), ALU.mult)
                    ins.then_inc(normed, 1)
                    dve.wait_ge(normed, b + 1)

            weights(0, RING)
            for part in range(TB + 1):
                norm(0, part)
            weights(RING, KD)
            for b in range(TB):
                for h in range(HEADS):
                    dve.wait_ge(xhi, KD * b + h + 1)
                    nc.vector.scalar_tensor_tensor(out=xl[:, h, :], in0=pst[:, h % 2, :], scalar=gs[:, 0:1],
                                                   in1=xh[:, h, :].bitcast(F32), op0=ALU.mult,
                                                   op1=ALU.subtract).then_inc(xlo, 1)
                if b == 0:
                    weights(KD, KW)
                dve.wait_ge(yhi, b + 1)
                nc.vector.tensor_tensor(xl[:, KD:, :], yraw, xh[:, KD:, :].bitcast(F32), ALU.subtract).then_inc(ylo, 1)
                for m in range(KD):
                    n = KD * b + m
                    dve.wait_ge(made, n + 1)
                    dve.wait_ge(gin[m % 2], 32 * (n // 2 + 1))
                    if n:
                        dve.wait_ge(merged, n)
                    link(nc.vector.tensor_tensor(ma[:, :], psa[:, m % 2, 0, :], gate[:, m % 2, 0], ALU.mult))
                    if n >= 2:
                        dve.wait_ge(stored[m % 2], 16 * (n // 2))
                    link(nc.vector.tensor_tensor(mg[:, m % 2], psa[:, m % 2, 1, :], gate[:, m % 2, 1], ALU.mult))
                    nc.vector.tensor_tensor(mg[:, m % 2], mg[:, m % 2], ma[:, :], ALU.add).then_inc(merged, 1)
                    if b + 1 < TB and 1 <= m <= TB + 1:
                        norm(b + 1, m - 1)

        @block.tensor
        def _(pe):
            for b in range(TB):
                pe.wait_ge(normed, b + 1)
                for h in range(HEADS):
                    if KD * b + h >= 2:
                        pe.wait_ge(xlo, KD * b + h - 1)
                    for t in range(TB):
                        ins = nc.tensor.transpose(pst[:, h % 2, t * P:(t + 1) * P], o[:, t, h, :], g.ident[:, :])
                    ins.then_inc(turned, 1)
                pe.wait_ge(xlo, KD * b + KD)
                pe.wait_ge(wlo, KD)
                for m in range(KD):
                    n = KD * b + m
                    if n >= 2:
                        pe.wait_ge(merged, n - 1)
                    c = slice(m * P, (m + 1) * P)
                    for v, ks in enumerate((range(KD), range(KD, KW))):
                        if m == 0 and v == 1:
                            pe.wait_ge(ylo, b + 1)
                            pe.wait_ge(wlo, KW)
                        for k in ks:
                            out = psa[:, m % 2, v, :]
                            nc.tensor.matmul(out, wh[:, k, c], xh[:, k, :], start=(k == ks[0]), stop=False)
                            nc.tensor.matmul(out, wh[:, k, c], xl[:, k, :], start=False, stop=False)
                            ins = nc.tensor.matmul(out, wl[:, k, c], xh[:, k, :], start=False, stop=(k == ks[-1]))
                    ins.then_inc(made, 1)


def merge(nc, a, g):
    with ExitStack() as ctx:
        sb, ps, sem = allocators(nc, ctx)
        raw = sb("e_raw", [P, KD, D])
        wh = sb("e_wh", [P, KD, D], F32R)
        wl = sb("e_wl", [P, KD, D], F32R)
        wr = sb("e_wr", [P, KD, E])
        br = sb("e_br", [P, E])
        rows = sb("e_rows", [P, 4, D])
        mraw = sb("e_mraw", [P, 2, KD, P])
        mh = sb("e_mh", [P, 2, KD, P], F32R)
        ml = sb("e_ml", [P, 2, KD, P], F32R)
        x = sb("e_x", [P, 2, D])
        u2 = sb("e_u2", [P, 2, D])
        u2t = sb("e_u2t", [P, 2, KD, P])
        junk = sb("e_junk", [P, D])
        rt = sb("e_rt", [P, 2, 2])
        psm = ps("e_psm", [P, 2, 2, BANK])
        pst = ps("e_pst", [P, 2, BANK])
        psr = ps("e_psr", [P, 2, BANK])
        rows_in = sem("e_rows")
        wloaded, whi, wlo, small = [sem(f"e_w{i}") for i in range(KD)], sem("e_whi"), sem("e_wlo"), sem("e_small")
        min_, xin, mhi, mlo = [sem("e_m0"), sem("e_m1")], [sem("e_x0"), sem("e_x1")], sem("e_mhi"), sem("e_mlo")
        made, sq1, mean1, root1, x1_ready = sem("e_made"), sem("e_sq1"), sem("e_mean1"), sem("e_root1"), sem("e_x1r")
        sq2, mean2, root2, u2_ready = sem("e_sq2"), sem("e_mean2"), sem("e_root2"), sem("e_u2r")
        x1st, u2st, turned, u2t_ready = [sem("e_a0"), sem("e_a1")], [sem("e_b0"), sem("e_b1")], sem("e_turn"), sem("e_u2t")
        routed, logit, dl = sem("e_routed"), sem("e_logit"), sem("e_dl")
        block = ctx.enter_context(nc.Block())
        w_out = a.w_out[0].rearrange("(k p) n -> k p n", p=P)
        mt = g.mt_d.rearrange("(k p) t -> p k t", p=P)

        @block.gpsimd
        def _(pool):
            nc.gpsimd.dma_start(wr[:, :, :], a.w_router[0].rearrange("(k p) e -> p k e", p=P)).then_inc(small, 16)
            nc.gpsimd.dma_start(br[:, :], a.b_router.to_broadcast([P, E])).then_inc(small, 16)

            def load(t, r):
                if not early(t, 2):
                    pool.wait_ge(mlo, t - 1)
                    pool.wait_ge(u2_ready, t - 1)
                    pool.wait_ge(x1st[r], (t - r) * 8)
                nc.gpsimd.dma_start(mraw[:, r], mt[:, :, ds(t * P, P)]).then_inc(min_[r], 16)
                nc.gpsimd.dma_start(x[:, r], a.x[0][ds(t * P, P), :]).then_inc(xin[r], 16)

            pipeline(pool, [(load, 0)], NT)

        @block.sync
        def _(sp):
            for k in range(KD):
                sp.dma_start(raw[:, k], w_out[k]).then_inc(wloaded[k], 16)
            sp.dma_start(rows[:, :, :].rearrange("p n d -> p (n d)"), g.outgain_d.to_broadcast([P, 4 * D])).then_inc(rows_in, 16)

            def store(t, r):
                sp.wait_ge(x1_ready, t + 1)
                sp.dma_start(g.x1_d[ds(t * P, P), :], x[:, r]).then_inc(x1st[r], 16)
                sp.wait_ge(u2_ready, t + 1)
                sp.dma_start(g.u2_d[ds(t * P, P), :], u2[:, r]).then_inc(u2st[r], 16)

            pipeline(sp, [(store, 0)], NT)
            for r in range(2):
                sp.wait_ge(x1st[r], 8 * NT)
                sp.wait_ge(u2st[r], 8 * NT)

        @block.scalar
        def _(act):
            for k in range(KD):
                act.wait_ge(wloaded[k], 16)
                nc.scalar.copy(wh[:, k, :], raw[:, k]).then_inc(whi, 1)

            def high(t, r):
                act.wait_ge(min_[r], (t - r) * 8 + 16)
                if not early(t, 2):
                    act.wait_ge(made, t - 1)
                nc.scalar.copy(mh[:, r], mraw[:, r]).then_inc(mhi, 1)

            def norms(t, r):
                act.wait_ge(made, t + 1)
                if not early(t, 1):
                    act.wait_ge(sq2, t)
                nc.scalar.activation(junk[:, :], psm[:, r].rearrange("p b c -> p (b c)"), ACT.Square,
                                     accum_out=rt[:, r, 0:1]).then_inc(sq1, 1)
                act.wait_ge(mean1, t + 1)
                nc.scalar.activation(rt[:, r, 0:1], rt[:, r, 0:1], ACT.Sqrt).then_inc(root1, 1)
                act.wait_ge(x1_ready, t + 1)
                nc.scalar.activation(junk[:, :], x[:, r], ACT.Square, accum_out=rt[:, r, 1:2]).then_inc(sq2, 1)
                act.wait_ge(mean2, t + 1)
                nc.scalar.activation(rt[:, r, 1:2], rt[:, r, 1:2], ACT.Sqrt).then_inc(root2, 1)

            def columns(t, r):
                for half in range(2):
                    act.wait_ge(turned, t * 2 + (half + 1))
                    if not early(t, 2) and half == 0:
                        act.wait_ge(routed, t - 1)
                    nc.scalar.copy(u2t[:, r, 4 * half:4 * half + 4].rearrange("p k c -> p (k c)"),
                                   pst[:, half, :]).then_inc(u2t_ready, 1)

            pipeline(act, [(high, 0), (columns, 2), (norms, 1)], NT)

        @block.vector
        def _(dve):
            for k in range(KD):
                dve.wait_ge(whi, k + 1)
                nc.vector.tensor_tensor(wl[:, k, :], raw[:, k], wh[:, k, :].bitcast(F32), ALU.subtract).then_inc(wlo, 1)

            def low(t, r):
                dve.wait_ge(mhi, t + 1)
                nc.vector.tensor_tensor(ml[:, r], mraw[:, r], mh[:, r].bitcast(F32), ALU.subtract).then_inc(mlo, 1)

            def norms(t, r):
                n = [0]

                def link(ins):
                    n[0] += 1
                    ins.then_inc(dl, 1)
                    dve.wait_ge(dl, t * 4 + n[0])

                if early(t, 1):
                    dve.wait_ge(rows_in, 16)
                    dve.wait_ge(small, 32)
                dve.wait_ge(sq1, t + 1)
                nc.vector.tensor_scalar(rt[:, r, 0:1], rt[:, r, 0:1], 1.0 / D, EPS, ALU.mult, ALU.add).then_inc(mean1, 1)
                dve.wait_ge(root1, t + 1)
                link(nc.vector.reciprocal(rt[:, r, 0:1], rt[:, r, 0:1]))
                if not early(t, 2):
                    dve.wait_ge(u2st[r], (t - r) * 8)
                    dve.wait_ge(turned, t * 2 - 2)
                link(nc.vector.scalar_tensor_tensor(out=u2[:, r], in0=psm[:, r].rearrange("p b c -> p (b c)"),
                                                    scalar=rt[:, r, 0:1], in1=rows[:, 0], op0=ALU.mult, op1=ALU.mult))
                dve.wait_ge(xin[r], (t - r) * 8 + 16)
                nc.vector.tensor_tensor(x[:, r], x[:, r], u2[:, r], ALU.add).then_inc(x1_ready, 1)
                dve.wait_ge(sq2, t + 1)
                nc.vector.tensor_scalar(rt[:, r, 1:2], rt[:, r, 1:2], 1.0 / D, EPS, ALU.mult, ALU.add).then_inc(mean2, 1)
                dve.wait_ge(root2, t + 1)
                link(nc.vector.reciprocal(rt[:, r, 1:2], rt[:, r, 1:2]))
                link(nc.vector.scalar_tensor_tensor(out=u2[:, r], in0=x[:, r], scalar=rt[:, r, 1:2], in1=rows[:, 2],
                                                    op0=ALU.mult, op1=ALU.mult))
                nc.vector.tensor_tensor(u2[:, r], u2[:, r], rows[:, 3], ALU.add).then_inc(u2_ready, 1)

            def logits(t, r):
                dve.wait_ge(routed, t + 1)
                nc.vector.tensor_tensor(g.logits[:, ds(t * E, E)], psr[:, r, 0:E], br[:, :], ALU.add).then_inc(logit, 1)

            pipeline(dve, [(logits, 3), (low, 0), (norms, 1)], NT)

        @block.tensor
        def _(pe):
            def product(t, r):
                pe.wait_ge(mlo, t + 1)
                if not early(t, 2):
                    pe.wait_ge(x1_ready, t - 1)
                for half in range(2):
                    c = slice(half * BANK, (half + 1) * BANK)
                    out = psm[:, r, half, :]
                    for k in range(KD):
                        if early(t, 1) and half == 0:
                            pe.wait_ge(wlo, k + 1)
                        nc.tensor.matmul(out, mh[:, r, k, :], wh[:, k, c], start=(k == 0), stop=False)
                        nc.tensor.matmul(out, mh[:, r, k, :], wl[:, k, c], start=False, stop=False)
                        ins = nc.tensor.matmul(out, ml[:, r, k, :], wh[:, k, c], start=False, stop=(k == KD - 1))
                ins.then_inc(made, 1)

            def turn(t, r):
                pe.wait_ge(u2_ready, t + 1)
                if not early(t, 1):
                    pe.wait_ge(u2t_ready, t * 2)
                for half in range(2):
                    for k in range(4 * half, 4 * half + 4):
                        ins = nc.tensor.transpose(pst[:, half, (k % 4) * P:(k % 4 + 1) * P],
                                                  u2[:, r, k * P:(k + 1) * P], g.ident[:, :])
                    ins.then_inc(turned, 1)

            def route(t, r):
                pe.wait_ge(u2t_ready, t * 2 + 2)
                if not early(t, 2):
                    pe.wait_ge(logit, t - 1)
                if early(t, 1):
                    pe.wait_ge(small, 32)
                for k in range(KD):
                    ins = nc.tensor.matmul(psr[:, r, 0:E], u2t[:, r, k, :], wr[:, k, :], start=(k == 0), stop=(k == KD - 1))
                ins.then_inc(routed, 1)

            pipeline(pe, [(route, 2), (product, 0), (turn, 1)], NT)


def dispatch(nc, a, g):
    with ExitStack() as ctx:
        sb, ps, sem = allocators(nc, ctx)
        S1 = SLOTS + 1
        C = NT * TOPK
        iota_e = sb("d_iota_e", [P, C, E])
        iota_s = sb("d_iota_s", [P, E, S1])
        before = sb("d_before", [P, P])
        ones = sb("d_ones", [P, P])
        tokid = sb("d_tokid", [P, NT], I32)
        zeros = sb("d_zeros", [P, (SLOTS + 1) * SLOT // P], I32)
        top = sb("d_top", [P, NT, 8])
        index = sb("d_index", [P, NT, 8], U32)
        idx = sb("d_idx", [P, C])
        hot = sb("d_hot", [P, C, E])
        mask = sb("d_mask", [P, NT, E])
        tot = sb("d_tot", [P, NT, E])
        count = sb("d_count", [P, E])
        nblk = sb("d_nblk", [P, E])
        cum = sb("d_cum", [P, 2, E + 16])
        start = sb("d_start", [P, E])
        run = sb("d_run", [P, NT, E])
        prod = sb("d_prod", [P, NT, E])
        posf = sb("d_posf", [P, NT, TOPK])
        ended = sb("d_ended", [P, E, S1])
        begun = sb("d_begun", [P, E, S1])
        slotf = sb("d_slotf", [P, 2, S1])
        cnt = sb("d_cnt", [P, S1])
        tmp4 = sb("d_tmp4", [P, NT, TOPK])
        psum1 = sb("d_psum1", [P, NT])
        psr = ps("d_psr", [P, BANK])
        psn = ps("d_psn", [P, BANK])
        consts, cleared, zeroed, dl, pl = sem("d_consts"), sem("d_clr"), sem("d_zero"), sem("d_dl"), sem("d_pl")
        masked, ranked, powers, diffs = sem("d_masked"), sem("d_ranked"), sem("d_pow"), sem("d_diff")
        placed, scattered = sem("d_placed"), sem("d_scat")
        block = ctx.enter_context(nc.Block())

        @block.sync
        def _(sp):
            sp.wait_ge(cleared, 1)
            sp.dma_start(g.tok_d.rearrange("(p c) o -> p (c o)", p=P), zeros[:, :]).then_inc(zeroed, 16)
            sp.wait_ge(zeroed, 16)

        @block.gpsimd
        def _(pool):
            link = Link(pool, pl)
            nc.gpsimd.memset(zeros[:, :], 0).then_inc(cleared, 1)
            link(nc.gpsimd.iota(iota_e[:, :, :], [[0, C], [1, E]], base=0, channel_multiplier=0,
                                allow_small_or_imprecise_dtypes=True))
            link(nc.gpsimd.iota(iota_s[:, :, :], [[0, E], [1, S1]], base=0, channel_multiplier=0,
                                allow_small_or_imprecise_dtypes=True))
            link(nc.gpsimd.iota(tokid[:, :], [[P, NT]], base=0, channel_multiplier=1))
            link(nc.gpsimd.memset(ones[:, :], 1.0))
            link(nc.gpsimd.affine_select(out=before[:, :], in_=ones[:, :], compare_op=ALU.is_gt, fill=0.0, base=0,
                                         pattern=[[1, P]], channel_multiplier=-1))
            nc.gpsimd.memset(cum[:, :, :], 0.0).then_inc(consts, 1)
            pool.wait_ge(placed, 1)
            pool.wait_ge(zeroed, 16)
            for t in range(NT):
                for k in range(TOPK):
                    c = t * TOPK + k
                    nc.gpsimd.indirect_dma_start(g.tok_d, bass.IndirectOffsetOnAxis(ap=g.pos[:, c:c + 1], axis=0),
                                                 tokid[:, t:t + 1], None).then_inc(scattered, 16)
            pool.wait_ge(scattered, 16 * C)

        @block.tensor
        def _(pe):
            pe.wait_ge(consts, 1)
            pe.wait_ge(masked, 1)
            flat = mask[:, :, :].rearrange("p t e -> p (t e)")
            nc.tensor.matmul(psr[:, :], before[:, :], flat, start=True, stop=True).then_inc(ranked, 1)
            nc.tensor.matmul(psn[:, :], ones[:, :], flat, start=True, stop=True).then_inc(ranked, 1)

        @block.scalar
        def _(act):
            act.wait_ge(diffs, 1)
            nc.scalar.activation(g.prob[:, :, :], g.prob[:, :, :], ACT.Exp).then_inc(powers, 1)

        @block.vector
        def _(dve):
            link = Link(dve, dl)
            logits = g.logits[:, :].rearrange("p (t e) -> p t e", e=E)
            for t in range(NT):
                link(nc.vector.max(top[:, t, :], logits[:, t, :]))
                link(nc.vector.max_index(index[:, t, :], top[:, t, :], logits[:, t, :]))
            nc.vector.tensor_tensor(g.prob[:, :, :], top[:, :, 0:TOPK], top[:, :, 0].to_broadcast([P, NT, TOPK]),
                                    ALU.subtract).then_inc(diffs, 1)
            link(nc.vector.tensor_copy(idx[:, :].rearrange("p (t k) -> p t k", k=TOPK), index[:, :, 0:TOPK]))
            dve.wait_ge(consts, 1)
            link(nc.vector.tensor_tensor(hot[:, :, :], iota_e[:, :, :], idx[:, :].to_broadcast([P, C, E]), ALU.is_equal))
            h4 = hot[:, :, :].rearrange("p (t k) e -> p t k e", k=TOPK)
            link(nc.vector.tensor_tensor(mask[:, :, :], h4[:, :, 0, :], h4[:, :, 1, :], ALU.add))
            link(nc.vector.tensor_tensor(mask[:, :, :], mask[:, :, :], h4[:, :, 2, :], ALU.add))
            nc.vector.tensor_tensor(mask[:, :, :], mask[:, :, :], h4[:, :, 3, :], ALU.add).then_inc(masked, 1)
            dve.wait_ge(powers, 1)
            link(nc.vector.tensor_reduce(psum1[:, :], g.prob[:, :, :], AX, ALU.add))
            link(nc.vector.reciprocal(psum1[:, :], psum1[:, :]))
            link(nc.vector.tensor_tensor(g.prob[:, :, :], g.prob[:, :, :], psum1[:, :].to_broadcast([P, NT, TOPK]), ALU.mult))
            dve.wait_ge(ranked, 2)
            link(nc.vector.tensor_copy(tot[:, :, :].rearrange("p t e -> p (t e)"), psn[:, :]))
            link(nc.vector.tensor_reduce(count[:, :], tot[:, :, :].rearrange("p t e -> p e t"), AX, ALU.add))
            link(nc.vector.tensor_scalar(nblk[:, :], count[:, :], 0.0, None, ALU.is_gt))
            for j in range(1, MAXB):
                link(nc.vector.scalar_tensor_tensor(out=nblk[:, :], in0=count[:, :], scalar=float(j * SLOT), in1=nblk[:, :],
                                                    op0=ALU.is_gt, op1=ALU.add))
            link(nc.vector.tensor_copy(cum[:, 0, 16:], nblk[:, :]))
            n = 0
            for step in (1, 2, 4, 8, 16):
                link(nc.vector.tensor_tensor(cum[:, 1 - n, 16:], cum[:, n, 16:], cum[:, n, 16 - step:16 - step + E], ALU.add))
                n = 1 - n
            cm = cum[:, n, 16:]
            link(nc.vector.tensor_tensor(start[:, :], cm, nblk[:, :], ALU.subtract))
            link(nc.vector.tensor_scalar(run[:, 0, :], start[:, :], float(SLOT), None, ALU.mult))
            for t in range(NT - 1):
                link(nc.vector.tensor_tensor(run[:, t + 1, :], run[:, t, :], tot[:, t, :], ALU.add))
            link(nc.vector.tensor_tensor(run[:, :, :].rearrange("p t e -> p (t e)"), psr[:, :],
                                         run[:, :, :].rearrange("p t e -> p (t e)"), ALU.add))
            for k in range(TOPK):
                link(nc.vector.tensor_tensor(prod[:, :, :], h4[:, :, k, :], run[:, :, :], ALU.mult))
                link(nc.vector.tensor_reduce(posf[:, :, k], prod[:, :, :], AX, ALU.add))
            nc.vector.tensor_copy(g.pos[:, :], posf[:, :, :].rearrange("p t k -> p (t k)")).then_inc(placed, 1)
            link(nc.vector.tensor_tensor(ended[:, :, :], iota_s[:, :, :], cm.to_broadcast([P, E, S1]), ALU.is_ge))
            link(nc.vector.tensor_tensor(begun[:, :, :], iota_s[:, :, :], start[:, :].to_broadcast([P, E, S1]), ALU.is_ge))
            link(nc.vector.tensor_tensor(begun[:, :, :], begun[:, :, :], ended[:, :, :], ALU.subtract))
            link(nc.vector.tensor_reduce(slotf[:, 0, :], ended[:, :, :].rearrange("p e s -> p s e"), AX, ALU.add))
            link(nc.vector.tensor_scalar(slotf[:, 0, :], slotf[:, 0, :], float(E - 1), None, ALU.min))
            link(nc.vector.scalar_tensor_tensor(out=count[:, :], in0=start[:, :], scalar=float(SLOT), in1=count[:, :],
                                                op0=ALU.mult, op1=ALU.add))
            link(nc.vector.tensor_tensor(begun[:, :, :], begun[:, :, :], count[:, :].to_broadcast([P, E, S1]), ALU.mult))
            link(nc.vector.tensor_reduce(cnt[:, :], begun[:, :, :].rearrange("p e s -> p s e"), AX, ALU.add))
            link(nc.vector.scalar_tensor_tensor(out=cnt[:, :], in0=iota_s[:, 0, :], scalar=-float(SLOT), in1=cnt[:, :],
                                                op0=ALU.mult, op1=ALU.add))
            link(nc.vector.tensor_scalar(slotf[:, 1, :], cnt[:, :], 0.0, None, ALU.is_gt))
            for j in range(1, JT):
                link(nc.vector.scalar_tensor_tensor(out=slotf[:, 1, :], in0=cnt[:, :], scalar=float(j * P),
                                                    in1=slotf[:, 1, :], op0=ALU.is_gt, op1=ALU.add))
            link(nc.vector.tensor_copy(g.table[:, :], slotf[:, :, :].rearrange("p n s -> p (n s)")))


def experts(nc, a, g):
    with ExitStack() as ctx:
        sb, ps, sem = allocators(nc, ctx)
        PIECES = KD + D // COLS
        RAW = 4
        raw = sb("x_raw", [P, RAW, KD, COLS])
        wh = [sb(f"x_wh{i}", [P, KD, BANK], F32R) for i in range(2)]
        wl = [sb(f"x_wl{i}", [P, KD, BANK], F32R) for i in range(2)]
        xg = sb("x_xg", [P, JT, D])
        xh = sb("x_xh", [P, KD, SLOT], F32R)
        xl = sb("x_xl", [P, KD, SLOT], F32R)
        ah = sb("x_ah", [P, KD, SLOT], F32R)
        al = sb("x_al", [P, KD, SLOT], F32R)
        gt = sb("x_gt", [P, SLOT])
        ut = sb("x_ut", [P, SLOT])
        sg = sb("x_sg", [P, SLOT])
        y = sb("x_y", [P, JT, D])
        bd = sb("x_bd", [P, D])
        ball = sb("x_ball", [P, BANK])
        bias = sb("x_bias", [P, 2 * KD])
        tok = sb("x_tok", [P, JT], I32)
        psg = ps("x_psg", [P, 4, BANK])
        pst = ps("x_pst", [P, 4, BANK])
        wloaded = [sem(f"x_w{i}") for i in range(RAW)]
        whi, wlo, bin_, bdin, tokin = sem("x_whi"), sem("x_wlo"), sem("x_bin"), sem("x_bdin"), sem("x_tokin")
        tokseen, filled = sem("x_tokseen"), sem("x_filled")
        xin, turned, xhi, xlo = sem("x_in"), sem("x_turn"), sem("x_xhi"), sem("x_xlo")
        made, gated, sig, acted, ahi, alo = sem("x_made"), sem("x_gated"), sem("x_sig"), sem("x_acted"), sem("x_ahi"), sem("x_alo")
        rows_made, rows_out = sem("x_rmade"), sem("x_rout")
        down, yout, stored, yfree, dl = sem("x_down"), sem("x_yout"), sem("x_stored"), sem("x_yfree"), sem("x_dl")
        block = ctx.enter_context(nc.Block())
        wgu = a.w_gate_up[0].rearrange("e (k p) n -> e p k n", p=P)
        wdn = a.w_down[0].rearrange("e (k p) n -> e p k n", p=P)
        tokv = g.tok_d.rearrange("(s j p) o -> s p (j o)", j=JT, p=P)
        yv = g.y_d.rearrange("(s j p) d -> s p j d", j=JT, p=P)
        H = D // 2
        LEAST = T * TOPK // SLOT

        def tiles(eng, s):
            return eng.value_load(g.table[0:1, ds(s + (SLOTS + 1), 1)], min_val=0, max_val=JT)

        def slots(eng, body, first=0):
            with eng.Fori(first, SLOTS) as s:
                n = tiles(eng, s)
                with eng.If(n > 0):
                    body(s, n, None if eng == nc.sync else tiles(eng, s + 1))

        def split_piece(part, i):
            return part[i // 2 % 2][:, :, i % 2 * COLS:(i % 2 + 1) * COLS]

        def by_tiles(eng, n, body):
            for v in range(1, JT + 1):
                with eng.If(n == v):
                    body(v)

        turning = [part[:, P:P + COLS] for part in (gt, ut)]

        def bank(v, half, j):
            return 3 if half and j == v - 1 else j

        @block.sync
        def _(sp):
            sp.dma_start(ball[:, :], g.bcol_d).then_inc(bin_, 16)

            def body(s, n, after):
                e = sp.value_load(g.table[0:1, ds(s, 1)], min_val=0, max_val=E - 1)
                for i in range(PIECES):
                    sp.wait_ge(wlo, s * PIECES + (i + 1))
                    r = i % RAW
                    for v in range(2):
                        if i < KD:
                            lo = v * FF + i * P
                            src = wgu[ds(e, 1), :, :, lo:lo + P].rearrange("e p k n -> p (e k) n")
                            sp.dma_start(raw[:, r, :, v * P:(v + 1) * P], src).then_inc(wloaded[r], 16)
                        else:
                            k = slice(v * KD // 2, (v + 1) * KD // 2)
                            src = wdn[ds(e, 1), :, k, (i - KD) * COLS:(i - KD + 1) * COLS].rearrange("e p k n -> p (e k) n")
                            sp.dma_start(raw[:, r, k, :], src).then_inc(wloaded[r], 16)
                    if i == 7:
                        sp.wait_ge(yout, s * 8 + 5)
                        sp.dma_start(bd[:, :], a.b_down[0][ds(e, 1), :].to_broadcast([P, D])).then_inc(bdin, 16)

            def fill(s):
                for q in range(2):
                    far = s * 2 + (LEAST + q)
                    with sp.If(tiles(sp, far) > 0):
                        sp.sem_inc(filled, 16)
                    with sp.Else():
                        sp.dma_start(g.y_d[ds(far * SLOT, SLOT), :], g.u2_d[0:SLOT, :]).then_inc(filled, 16)

            with sp.Fori(0, LEAST) as s:
                body(s, None, None)
                fill(s)
            slots(sp, body, LEAST)
            sp.wait_ge(filled, 16 * 2 * LEAST)

        @block.gpsimd
        def _(pool):
            def gather(s, v):
                with nc.allow_non_contiguous_dma(reason="a slot's token numbers, one to a partition"):
                    nc.gpsimd.dma_start(tok[:, :], tokv[ds(s, 1)].rearrange("s p j -> p (s j)")).then_inc(tokin, 16)
                pool.wait_ge(tokin, s * 16 + 16)
                pool.sem_inc(tokseen, 1)
                for j in range(JT):
                    rows = slice(0, P if j < v else 2)
                    nc.gpsimd.indirect_dma_start(xg[rows, j, :], None, g.u2_d,
                                                 bass.IndirectOffsetOnAxis(ap=tok[rows, j:j + 1], axis=0)).then_inc(xin, 16)
                pool.wait_ge(xin, s * 64 + 64)

            gather(0, JT)

            def body(s, n, after):
                def following(v):
                    pool.wait_ge(turned, s * KD + KD)
                    gather(s + 1, v)

                by_tiles(pool, after, following)
                for half in range(2):
                    pool.wait_ge(yout, s * 8 + (4 * half + 9))
                    nc.gpsimd.dma_start(yv[ds(s, 1), :, :, half * H:(half + 1) * H].rearrange("s p j d -> p (s j) d"),
                                        y[:, :, half * H:(half + 1) * H]).then_inc(stored, 16)
                    pool.wait_ge(stored, s * 32 + (16 * half + 16))
                    pool.sem_inc(yfree, 1)

            slots(pool, body)

        @block.scalar
        def _(act):
            def split(s, i):
                act.wait_ge(wloaded[i % RAW], s * (32 * PIECES // RAW) + (32 * (i // RAW) + 32))
                nc.scalar.copy(split_piece(wh, i), raw[:, i % RAW]).then_inc(whi, 1)

            def rows(s, part, v):
                for k in range(4 * part, 4 * part + 4):
                    act.wait_ge(turned, s * KD + (k + 1))
                    nc.scalar.copy(xh[:, k, 0:v * P], pst[:, k % 4, 0:v * P]).then_inc(xhi, 1)

            act.sem_inc(xlo, 4)
            act.sem_inc(yout, 5)
            act.sem_inc(yfree, 2)
            for i in range(4):
                split(0, i)
            rows(0, 0, JT)
            rows(0, 1, JT)

            def body(s, n, after):
                def version(v):
                    w = v * P
                    def take_rows(f):
                        act.wait_ge(rows_made, s * KD + (f + 1))
                        nc.scalar.copy(turning[f % 2], psg[:, f % 2, 0:COLS]).then_inc(rows_out, 1)

                    if v == 1:
                        take_rows(0)
                    else:
                        act.sem_inc(rows_out, KD)
                    for f in range(KD):
                        if v == 1 and f + 1 < KD:
                            take_rows(f + 1)
                        act.wait_ge(gated, s * 16 + (2 * f + 1))
                        nc.scalar.activation(sg[:, 0:w], gt[:, 0:w], ACT.Sigmoid, scale=ALPHA).then_inc(sig, 1)
                        if f < KD - 1:
                            split(s, f + 4)
                        act.wait_ge(acted, s * KD + (f + 1))
                        nc.scalar.copy(ah[:, f, 0:w], ut[:, 0:w]).then_inc(ahi, 1)
                    split(s, PIECES - 1)

                by_tiles(act, n, version)

                def following(v):
                    rows(s + 1, 0, v)
                    rows(s + 1, 1, v)
                    for half in range(2):
                        act.wait_ge(down, s * 8 + (4 * half + 4))
                        split(s + 1, 2 * half)
                        split(s + 1, 2 * half + 1)

                by_tiles(act, after, following)

            slots(act, body)

        @block.vector
        def _(dve):
            def split(s, i):
                dve.wait_ge(whi, s * PIECES + (i + 1))
                nc.vector.tensor_tensor(split_piece(wl, i), raw[:, i % RAW], split_piece(wh, i).bitcast(F32),
                                        ALU.subtract).then_inc(wlo, 1)

            def rows(s, part, v):
                w = v * P
                for k in range(4 * part, 4 * part + 4):
                    dve.wait_ge(xhi, s * KD + (k + 1))
                    nc.vector.tensor_tensor(xl[:, k, 0:w], pst[:, k % 4, 0:w], xh[:, k, 0:w].bitcast(F32),
                                            ALU.subtract).then_inc(xlo, 1)

            nc.vector.memset(y[:, :, :], 0.0).then_inc(dl, 1)
            dve.sem_inc(wlo, 4)
            dve.wait_ge(bin_, 16)
            for i in range(3):
                split(0, i)
            rows(0, 0, JT)
            rows(0, 1, JT)

            def body(s, n, after):
                e = dve.value_load(g.table[0:1, ds(s, 1)], min_val=0, max_val=E - 1)
                DL = KD + 1
                dve.wait_ge(alo, s * KD + 1)
                nc.vector.tensor_copy(bias[:, :], ball[:, ds(e * (2 * KD), 2 * KD)]).then_inc(dl, 1)

                def version(v):
                    w = v * P
                    dve.wait_ge(dl, s * DL + 2)
                    for f in range(KD):
                        dve.wait_ge(made, s * KD + (f + 1))
                        dve.wait_ge(alo, s * KD + (f + 1))
                        pair = 2 * (f % 2)
                        gate_sums, up_sums = psg[:, pair, 0:w], psg[:, pair + 1, 0:w]
                        if v == 1:
                            gate_sums, up_sums = psg[:, 2 + f % 2, 0:P], psg[:, 2 + f % 2, P:2 * P]
                        nc.vector.tensor_scalar(gt[:, 0:w], gate_sums, bias[:, f:f + 1], LIMIT,
                                                ALU.add, ALU.min).then_inc(gated, 1)
                        nc.vector.tensor_scalar(ut[:, 0:w], up_sums, bias[:, KD + f:KD + f + 1], LIMIT + 1,
                                                ALU.add, ALU.min).then_inc(gated, 1)
                        if f < KD - 1:
                            split(s, f + 3)
                        dve.wait_ge(sig, s * KD + (f + 1))
                        dve.wait_ge(gated, s * 16 + (2 * f + 2))
                        nc.vector.tensor_tensor(gt[:, 0:w], gt[:, 0:w], sg[:, 0:w], ALU.mult).then_inc(dl, 1)
                        dve.wait_ge(dl, s * DL + (f + 3))
                        nc.vector.scalar_tensor_tensor(out=ut[:, 0:w], in0=ut[:, 0:w], scalar=1.0 - LIMIT, in1=gt[:, 0:w],
                                                       op0=ALU.max, op1=ALU.mult).then_inc(acted, 1)
                        dve.wait_ge(ahi, s * KD + (f + 1))
                        nc.vector.tensor_tensor(al[:, f, 0:w], ut[:, 0:w], ah[:, f, 0:w].bitcast(F32),
                                                ALU.subtract).then_inc(alo, 1)

                by_tiles(dve, n, version)
                split(s, PIECES - 2)
                by_tiles(dve, after, lambda v: rows(s + 1, 0, v))
                split(s, PIECES - 1)
                for half in range(2):
                    def outputs(v):
                        dve.wait_ge(bdin, s * 16 + 16)
                        dve.wait_ge(yfree, s * 2 + (half + 1))
                        for j in range(v):
                            dve.wait_ge(down, s * 8 + (4 * half + j + 1))
                            nc.vector.tensor_tensor(y[:, j, half * H:(half + 1) * H], psg[:, bank(v, half, j), :], bd[:, half * H:(half + 1) * H],
                                                    ALU.add).then_inc(yout, 1 if j < v - 1 else JT + 1 - v)

                    by_tiles(dve, n, outputs)
                    if half == 0:
                        by_tiles(dve, after, lambda v: rows(s + 1, 1, v))
                    with dve.If(after > 0):
                        split(s + 1, half)
                        if half:
                            split(s + 1, 2)

            dve.sem_inc(alo, 1)
            slots(dve, body)

        @block.tensor
        def _(pe):
            def turn(s, part, v):
                pe.wait_ge(xin, s * 64 + 64)
                for k in range(4 * part, 4 * part + 4):
                    pe.wait_ge(xlo, s * KD + (k + 1))
                    for j in range(v):
                        ins = nc.tensor.transpose(pst[:, k % 4, j * P:(j + 1) * P], xg[:, j, k * P:(k + 1) * P], g.ident[:, :])
                    ins.then_inc(turned, 1)

            turn(0, 0, JT)
            turn(0, 1, JT)

            def body(s, n, after):
                pe.wait_ge(xlo, s * KD + (KD + 4))
                pe.wait_ge(yout, s * 8 + 5)

                def one_tile():
                    for f in range(KD + 1):
                        if f < KD:
                            pe.wait_ge(wlo, s * PIECES + (f + 5))
                            if f >= 2:
                                pe.wait_ge(rows_out, s * KD + (f - 1))
                            out, cols = psg[:, f % 2, 0:COLS], slice(f % 2 * COLS, (f % 2 + 1) * COLS)
                            high, low = wh[f // 2 % 2], wl[f // 2 % 2]
                            for k in range(KD):
                                nc.tensor.matmul(out, xh[:, k, 0:P], high[:, k, cols], start=(k == 0), stop=False)
                                nc.tensor.matmul(out, xh[:, k, 0:P], low[:, k, cols], start=False, stop=False)
                                ins = nc.tensor.matmul(out, xl[:, k, 0:P], high[:, k, cols], start=False,
                                                       stop=(k == KD - 1))
                            ins.then_inc(rows_made, 1)
                        if f >= 1:
                            pe.wait_ge(rows_out, s * KD + f)
                            if f >= 3:
                                pe.wait_ge(gated, s * 16 + (2 * f - 4))
                            for u in range(2):
                                ins = nc.tensor.transpose(psg[:, 2 + (f - 1) % 2, u * P:(u + 1) * P],
                                                          turning[(f - 1) % 2][:, u * P:(u + 1) * P], g.ident[:, :])
                            ins.then_inc(made, 1)

                def version(v):
                    if v == 1:
                        one_tile()
                        return
                    pe.sem_inc(rows_made, KD)
                    w = v * P
                    for f in range(KD):
                        c = f // 2
                        pe.wait_ge(wlo, s * PIECES + (f + 5))
                        if f >= 2:
                            pe.wait_ge(gated, s * 16 + (2 * f - 2))
                        for u in range(2):
                            col = slice((f % 2) * COLS + u * P, (f % 2) * COLS + (u + 1) * P)
                            out = psg[:, 2 * (f % 2) + u, 0:w]
                            for k in range(KD):
                                nc.tensor.matmul(out, wh[c % 2][:, k, col], xh[:, k, 0:w], start=(k == 0), stop=False)
                                nc.tensor.matmul(out, wh[c % 2][:, k, col], xl[:, k, 0:w], start=False, stop=False)
                                ins = nc.tensor.matmul(out, wl[c % 2][:, k, col], xh[:, k, 0:w], start=False,
                                                       stop=(k == KD - 1))
                        ins.then_inc(made, 1)

                by_tiles(pe, n, version)
                for half in range(2):
                    by_tiles(pe, after, lambda v: turn(s + 1, half, v))

                    def outputs(v):
                        pe.wait_ge(wlo, s * PIECES + (KD + 2 * half + 6))
                        for j in range(v):
                            if half:
                                pe.wait_ge(yout, s * 8 + (min(bank(v, half, j), v - 1) + 6))
                            out = psg[:, bank(v, half, j), :]
                            t = slice(j * P, (j + 1) * P)
                            for k in range(KD):
                                if half == 0 and j == 0:
                                    pe.wait_ge(alo, s * KD + (k + 2))
                                nc.tensor.matmul(out, ah[:, k, t], wh[half][:, k, :], start=(k == 0), stop=False)
                                nc.tensor.matmul(out, ah[:, k, t], wl[half][:, k, :], start=False, stop=False)
                                ins = nc.tensor.matmul(out, al[:, k, t], wh[half][:, k, :], start=False,
                                                       stop=(k == KD - 1))
                            ins.then_inc(down, 1 if j < v - 1 else JT + 1 - v)

                    by_tiles(pe, n, outputs)

            slots(pe, body)


def combine(nc, a, g, out):
    with ExitStack() as ctx:
        sb, ps, sem = allocators(nc, ctx)
        yg = sb("c_y", [P, 2, TOPK, D])
        x1 = sb("c_x1", [P, 2, D])
        row = sb("c_row", [P, D])
        f = sb("c_f", [P, 2, D])
        junk = sb("c_junk", [P, D])
        res = sb("c_res", [P, 2, D])
        rt = sb("c_rt", [P, 2, 1])
        small, yin, xin, dl = sem("c_small"), [sem("c_y0"), sem("c_y1")], [sem("c_x0"), sem("c_x1")], sem("c_dl")
        chain = sem("c_chain")
        summed, sq, mean, root, done = sem("c_sum"), sem("c_sq"), sem("c_mean"), sem("c_root"), sem("c_done")
        stored = [sem("c_s0"), sem("c_s1")]
        block = ctx.enter_context(nc.Block())
        od = out[0]

        @block.gpsimd
        def _(pool):
            for t in range(NT):
                r = t % 2
                if t >= 2:
                    pool.wait_ge(summed, t - 1)
                for k in range(TOPK):
                    nc.gpsimd.indirect_dma_start(yg[:, r, k, :], None, g.y_d,
                                                 bass.IndirectOffsetOnAxis(ap=g.pos[:, t * TOPK + k:t * TOPK + k + 1], axis=0)
                                                 ).then_inc(yin[r], 16)

        @block.sync
        def _(sp):
            sp.dma_start(row[:, :], g.outgain_d[:, D:2 * D].to_broadcast([P, D])).then_inc(small, 16)

            def load(t, r):
                if not early(t, 2):
                    sp.wait_ge(done, t - 1)
                sp.dma_start(x1[:, r], g.x1_d[ds(t * P, P), :]).then_inc(xin[r], 16)

            def store(t, r):
                sp.wait_ge(done, t + 1)
                sp.dma_start(od[ds(t * P, P), :], res[:, r]).then_inc(stored[r], 16)

            pipeline(sp, [(load, 0), (store, 1)], NT)
            for r in range(2):
                sp.wait_ge(stored[r], 8 * NT)

        @block.scalar
        def _(act):
            def body(t, r):
                act.wait_ge(summed, t + 1)
                if not early(t, 1):
                    act.wait_ge(sq, t)
                nc.scalar.activation(junk[:, :], f[:, r], ACT.Square, accum_out=rt[:, r, :]).then_inc(sq, 1)
                act.wait_ge(mean, t + 1)
                nc.scalar.activation(rt[:, r, :], rt[:, r, :], ACT.Sqrt).then_inc(root, 1)

            pipeline(act, [(body, 0)], NT)

        @block.vector
        def _(dve):
            dve.wait_ge(small, 16)

            def total(t, r):
                dve.wait_ge(yin[r], (t - r) * 32 + 64)
                if not early(t, 2):
                    dve.wait_ge(done, t - 1)
                for k in range(TOPK):
                    weight = g.prob[:, ds(t, 1), k:k + 1].rearrange("p a b -> p (a b)")
                    if k == 0:
                        ins = nc.vector.tensor_scalar(f[:, r], yg[:, r, 0, :], weight, None, ALU.mult)
                    else:
                        ins = nc.vector.scalar_tensor_tensor(out=f[:, r], in0=yg[:, r, k, :], scalar=weight, in1=f[:, r],
                                                             op0=ALU.mult, op1=ALU.add)
                    if k < TOPK - 1:
                        ins.then_inc(chain, 1)
                        dve.wait_ge(chain, t * (TOPK - 1) + (k + 1))
                ins.then_inc(summed, 1)

            def finish(t, r):
                dve.wait_ge(sq, t + 1)
                nc.vector.tensor_scalar(rt[:, r, :], rt[:, r, :], 1.0 / D, EPS, ALU.mult, ALU.add).then_inc(mean, 1)
                dve.wait_ge(root, t + 1)
                nc.vector.reciprocal(rt[:, r, :], rt[:, r, :]).then_inc(dl, 1)
                dve.wait_ge(dl, t * 2 + 1)
                nc.vector.scalar_tensor_tensor(out=f[:, r], in0=f[:, r], scalar=rt[:, r, :], in1=row[:, :],
                                               op0=ALU.mult, op1=ALU.mult).then_inc(dl, 1)
                dve.wait_ge(dl, t * 2 + 2)
                dve.wait_ge(xin[r], (t - r) * 8 + 16)
                if not early(t, 2):
                    dve.wait_ge(stored[r], (t - r) * 8)
                nc.vector.tensor_tensor(res[:, r], x1[:, r], f[:, r], ALU.add).then_inc(done, 1)

            pipeline(dve, [(total, 0), (finish, 1)], NT)


def build(nc, a, out):
    with ExitStack() as ctx:
        g = Shared()
        sb, ps, sem = allocators(nc, ctx)

        def dram(name, shape, dt=F32):
            return nc.dram_tensor(name, shape, dt).ap()

        g.outgain_d = dram("outgain_d", [1, 4 * D])
        g.bcol_d = dram("bcol_d", [P, BANK])
        g.zt_d = dram("zt_d", [IN_W, T])
        g.yt_d = dram("yt_d", [PG * P, T])
        g.o_d = dram("o_d", [T, VW])
        g.mt_d = dram("mt_d", [D, T])
        g.x1_d = dram("x1_d", [T, D])
        g.u2_d = dram("u2_d", [T, D])
        g.tok_d = dram("tok_d", [(SLOTS + 1) * SLOT, 1], I32)
        g.y_d = dram("y_d", [(SLOTS + 1) * SLOT, D])
        g.v_d = dram("v_d", [T, VW])
        g.ident = sb("ident", [P, P])
        g.vcol = sb("vcol", [P, P])
        g.neglam = sb("neglam", [P, 1])
        g.shift = sb("shift", [P, 2, KD])
        g.gain = sb("gain", [P, 2, KD])
        with ExitStack() as mixing:
            esb = allocators(nc, mixing)[0]
            g.rot = esb("rot_t", [P, 2, T])
            modulate(nc, a, g)
            g.uth = esb("uth", [P, KD, T], F32R)
            g.utl = esb("utl", [P, KD, T], F32R)
            normalise(nc, a, g)
            project(nc, a, g)
        pool_mix(nc, a, g)
        attend(nc, a, g)
        branches(nc, a, g)
        g.prob = sb("prob", [P, NT, TOPK])
        g.pos = sb("pos", [P, NT * TOPK], I32)
        g.table = sb("table", [P, 2 * (SLOTS + 1)], I32)
        with ExitStack() as routing:
            g.logits = allocators(nc, routing)[0]("logits", [P, NT * E])
            merge(nc, a, g)
            dispatch(nc, a, g)
        experts(nc, a, g)
        combine(nc, a, g, out)


_INS = ["x", "c", "positions", "w_mod", "b_mod", "g_pre_mix", "w_in", "lambda_q1", "lambda_k1", "lambda_q2",
        "lambda_k2", "g_sub", "w_pool_group", "pool_scale", "w_att_branch", "w_pool_branch", "w_out", "g_post_mix",
        "g_pre_ffn", "w_router", "b_router", "w_gate_up", "b_gate_up", "w_down", "b_down", "g_post_ffn"]


def kernel(**inputs):
    import numpy as _np
    import concourse.bacc as _bacc
    from concourse import mybir as _mybir
    from concourse.bass_utils import run_bass_kernel_spmd as _run

    nc = _bacc.Bacc("TRN2", target_bir_lowering=False, num_devices=1)
    arrays, aps = {}, {}
    for name in _INS:
        arr = _np.ascontiguousarray(inputs[name])
        arrays[f"in_{name}"] = arr
        aps[name] = nc.dram_tensor(f"in_{name}", arr.shape, _mybir.dt.from_np(arr.dtype), kind="ExternalInput").ap()
    out = nc.dram_tensor("out_dram", (1, T, D), _mybir.dt.float32, kind="ExternalOutput").ap()
    build(nc, Inputs(aps), out)
    r = _run(nc, [arrays], core_ids=[0])
    return r.results[0]["out_dram"]
```
